# Optimizing a Trainium2 kernel written in Bass

```python
import jax
import jax.numpy as jnp
from jax import lax
import numpy as np

D_MODEL = 1024
BATCH = 1
SEQ = 128
DEPTH = 2
DEC_BATCH = 1
DEC_SEQ = 512
PAST_LEN = 128

GRID_W = 64
N_EVEN = (DEPTH + 1) // 2
N_ODD = DEPTH // 2
EPS = 1e-6
NEG_INF = -1e30
ROPE_BASE = 10000.0
ATTN_Q_BLOCK = 128

A_HEADS = 4
A_DK = 64
A_DV = 128
A_GATE_RANK = 16
A_GATE_TAU = 16.0
A_CHUNK = 64

B_HEADS = 8
B_Q_RANK = 256
B_KV_RANK = 256
B_NOPE = 64
B_ROPE = 64
B_V = 64

C_GROUPS = 4
C_GROUP_W = 128
C_WINDOWS = (2, 4, 8, 16)

D_HEADS = 8
D_KV_HEADS = 2
D_HEAD = 64
D_WINDOW = 128
D_BLOCK = 128

P_HEADS = 8
P_NKEYS = 128
P_EXPERTS = P_NKEYS * P_NKEYS
P_QDIM = 256
P_TOPK = 16
P_TOKEN_BLOCK = 128

EVEN_SPLIT = (A_HEADS * A_DK, A_HEADS * A_DK, A_HEADS * A_DV, A_HEADS * A_DV, A_GATE_RANK, A_GATE_RANK, B_Q_RANK, B_KV_RANK, B_ROPE)
EVEN_IN = sum(EVEN_SPLIT)
EVEN_MIX = A_HEADS * A_DV + B_HEADS * B_V
ODD_SPLIT = (C_GROUPS * C_GROUP_W, D_HEADS * D_HEAD, D_KV_HEADS * D_HEAD, D_KV_HEADS * D_HEAD)
ODD_IN = sum(ODD_SPLIT)
ODD_MIX = C_GROUPS * C_GROUP_W + D_HEADS * D_HEAD

kernel_name = 'hybrid_diffusion_prefix_trunk_step'

def split_cols(x, sizes):
    return jnp.split(x, np.cumsum(sizes)[:-1].tolist(), axis=-1)

def rms_norm(x, g):
    xf = x.astype(jnp.float32)
    y = xf * lax.rsqrt(jnp.mean(xf * xf, axis=-1, keepdims=True) + EPS)
    return (y * g.astype(jnp.float32)).astype(x.dtype)

def ada_mod(cond, w, b):
    m = jax.nn.silu(cond) @ w + b
    return jnp.split(m[..., None, :], 6, axis=-1)

def modulate(x, g, shift, scale):
    return rms_norm(x, g) * (1.0 + scale) + shift

def axial_rope(rows, rot_dim):
    quarter = rot_dim // 4
    inv = ROPE_BASE ** (-jnp.arange(quarter, dtype=jnp.float32) / quarter)
    row = jnp.repeat(jnp.arange(rows, dtype=jnp.float32), GRID_W)
    col = jnp.tile(jnp.arange(GRID_W, dtype=jnp.float32), rows)
    ar = row[:, None] * inv
    ac = col[:, None] * inv
    ang = jnp.concatenate([ar, ar, ac, ac], axis=-1)
    return jnp.cos(ang), jnp.sin(ang)

def rope_last(x, cos, sin):
    r = cos.shape[-1]
    xa, xr = x[..., :-r], x[..., -r:]
    q4 = r // 4
    x4 = xr.reshape(xr.shape[:-1] + (2, 2, q4))
    rot = jnp.stack([-x4[..., 1, :], x4[..., 0, :]], axis=-2).reshape(xr.shape)
    c = cos[None, :, None, :].astype(x.dtype)
    s = sin[None, :, None, :].astype(x.dtype)
    return jnp.concatenate([xa, xr * c + rot * s], axis=-1)

def gla_log_decay(low, w_up, b_up):
    bsz, t, _ = low.shape
    z = (low @ w_up + b_up).astype(jnp.float32)
    return (jax.nn.log_sigmoid(z) / A_GATE_TAU).reshape(bsz, t, A_HEADS, A_DK)

def gla_chunked(q, k, v, log_a, s0):
    bsz, t, h, dk = q.shape
    dv = v.shape[-1]
    n, l = t // A_CHUNK, A_CHUNK
    f32 = jnp.float32
    qc = q.reshape(bsz, n, l, h, dk).astype(f32)
    kc = k.reshape(bsz, n, l, h, dk).astype(f32)
    vc = v.reshape(bsz, n, l, h, dv).astype(f32)
    b = jnp.cumsum(log_a.reshape(bsz, n, l, h, dk).astype(f32), axis=2)
    b_last = b[:, :, -1]
    q_dec = qc * jnp.exp(b)
    k_intra = kc * jnp.exp(-b)
    k_state = kc * jnp.exp(b_last[:, :, None] - b)
    lower = jnp.tril(jnp.ones((l, l), dtype=bool))
    att = jnp.where(lower, jnp.einsum('bnihd,bnjhd->bnhij', q_dec, k_intra), 0.0)
    o_intra = jnp.einsum('bnhij,bnjhv->bnihv', att, vc)
    upd = jnp.einsum('bnjhd,bnjhv->bnhdv', k_state, vc)
    decay = jnp.exp(b_last)

    def step(s, inp):
        d, u = inp
        return d[..., None] * s + u, s

    s_fin, s_start = lax.scan(step, s0.astype(f32), (jnp.moveaxis(decay, 1, 0), jnp.moveaxis(upd, 1, 0)))
    o_inter = jnp.einsum('bnihd,bnhdv->bnihv', q_dec, jnp.moveaxis(s_start, 0, 1))
    o = (o_intra + o_inter).reshape(bsz, t, h, dv)
    return o.astype(v.dtype), s_fin.astype(s0.dtype)

def gla_bidir(q, k, v, la_f, la_b, s0_f, s0_b):
    o_f, s_f = gla_chunked(q, k, v, la_f, s0_f)
    flip = lambda a: jnp.flip(a, axis=1)
    o_b, s_b = gla_chunked(flip(q), flip(k), flip(v), flip(la_b), s0_b)
    return o_f + flip(o_b), s_f, s_b

def attn_blocked(q, k, v, sink):
    bsz, t, hk, g, dq = q.shape
    nb = t // ATTN_Q_BLOCK
    scale = dq ** -0.5
    s_len = k.shape[1]
    qb = jnp.moveaxis(q.reshape(bsz, nb, ATTN_Q_BLOCK, hk, g, dq), 1, 0)

    def one(qi):
        s = jnp.einsum('bqkgd,bskd->bkgqs', qi, k).astype(jnp.float32) * scale
        if sink is not None:
            sk = jnp.broadcast_to(sink.astype(jnp.float32)[None, :, :, None, None], s.shape[:-1] + (1,))
            s = jnp.concatenate([s, sk], axis=-1)
        p = jax.nn.softmax(s, axis=-1)[..., :s_len]
        return jnp.einsum('bkgqs,bskd->bqkgd', p.astype(v.dtype), v)

    o = lax.map(one, qb)
    return jnp.moveaxis(o, 0, 1).reshape(bsz, t, hk * g * v.shape[-1])

def window_attn(q, k, v, k_ctx, v_ctx, sink):
    bsz, t, hk, g, d = q.shape
    nb = t // D_BLOCK
    span = D_BLOCK + 2 * D_WINDOW
    p_len = k_ctx.shape[1]
    padw = ((0, 0), (D_WINDOW, D_WINDOW), (0, 0), (0, 0))
    kp = jnp.pad(k, padw)
    vp = jnp.pad(v, padw)
    scale = d ** -0.5
    sk = sink.astype(jnp.float32)[None, :, :, None, None]

    def one(bi):
        start = bi * D_BLOCK
        qi = lax.dynamic_slice_in_dim(q, start, D_BLOCK, axis=1)
        ki = lax.dynamic_slice_in_dim(kp, start, span, axis=1)
        vi = lax.dynamic_slice_in_dim(vp, start, span, axis=1)
        qpos = start + jnp.arange(D_BLOCK)
        kpos = start - D_WINDOW + jnp.arange(span)
        valid = (jnp.abs(qpos[:, None] - kpos[None, :]) <= D_WINDOW) & (kpos >= 0)[None, :] & (kpos < t)[None, :]
        s_loc = jnp.einsum('bqkgd,bskd->bkgqs', qi, ki).astype(jnp.float32) * scale
        s_loc = jnp.where(valid, s_loc, NEG_INF)
        s_ctx = jnp.einsum('bqkgd,bpkd->bkgqp', qi, k_ctx).astype(jnp.float32) * scale
        s = jnp.concatenate([s_loc, s_ctx, jnp.broadcast_to(sk, s_loc.shape[:-1] + (1,))], axis=-1)
        p = jax.nn.softmax(s, axis=-1)
        o = jnp.einsum('bkgqs,bskd->bqkgd', p[..., :span].astype(v.dtype), vi)
        return o + jnp.einsum('bkgqp,bpkd->bqkgd', p[..., span:span + p_len].astype(v.dtype), v_ctx)

    o = lax.map(one, jnp.arange(nb))
    return jnp.moveaxis(o, 0, 1).reshape(bsz, t, hk * g * d)

def mla_keys(c_kv, k_rope, w_uk, w_uv, g_kn):
    bsz, s, _ = c_kv.shape
    k_nope = (c_kv @ w_uk).reshape(bsz, s, B_HEADS, B_NOPE)
    k_r = jnp.broadcast_to(k_rope[:, :, None, :], (bsz, s, B_HEADS, B_ROPE)).astype(k_nope.dtype)
    k = rms_norm(jnp.concatenate([k_nope, k_r], axis=-1), g_kn)
    v = (c_kv @ w_uv).reshape(bsz, s, B_HEADS, B_V)
    return k, v

def pool_mixer(xc, w_pool, scale):
    bsz, t, _ = xc.shape
    xg = xc.reshape(bsz, t, C_GROUPS, C_GROUP_W).astype(jnp.float32)
    cs = jnp.concatenate([jnp.zeros_like(xg[:, :1]), jnp.cumsum(xg, axis=1)], axis=1)
    pos = jnp.arange(t)
    pooled = []
    for gi, w in enumerate(C_WINDOWS):
        lo = jnp.clip(pos - w // 2, 0, t)
        hi = jnp.clip(pos - w // 2 + w, 0, t)
        csg = cs[:, :, gi]
        pooled.append((csg[:, hi] - csg[:, lo]) / (hi - lo).astype(jnp.float32)[None, :, None])
    y = jnp.stack(pooled, axis=2) - xg
    y = jnp.einsum('btgc,gcd->btgd', y, w_pool.astype(jnp.float32))
    return (y.reshape(bsz, t, C_GROUPS * C_GROUP_W) * scale).astype(xc.dtype)

def peer_ffn(h, wq, subkeys, u_tab, v_tab):
    bsz, t, d = h.shape
    x = h.reshape(-1, P_TOKEN_BLOCK, d)

    def one(xb):
        nt = xb.shape[0]
        q = (xb @ wq).reshape(nt, P_HEADS, 2, P_QDIM // 2)
        s = jnp.einsum('thcd,hckd->thck', q, subkeys).astype(jnp.float32)
        s1, i1 = lax.top_k(s[:, :, 0], P_TOPK)
        s2, i2 = lax.top_k(s[:, :, 1], P_TOPK)
        cand_s = (s1[..., :, None] + s2[..., None, :]).reshape(nt, P_HEADS, P_TOPK * P_TOPK)
        cand_i = (i1[..., :, None] * P_NKEYS + i2[..., None, :]).reshape(nt, P_HEADS, P_TOPK * P_TOPK)
        top_s, pos = lax.top_k(cand_s, P_TOPK)
        idx = jnp.take_along_axis(cand_i, pos, axis=-1)
        gate = jax.nn.softmax(top_s, axis=-1).astype(xb.dtype)
        u = jnp.take(u_tab, idx, axis=0)
        act = jax.nn.gelu(jnp.einsum('thkd,td->thk', u, xb), approximate=False) * gate
        vv = jnp.take(v_tab, idx, axis=0)
        return jnp.einsum('thk,thkd->td', act, vv)

    return lax.map(one, x).reshape(bsz, t, d)

def even_mixer(h, p, ctx, rope):
    (w_in, w_gu, b_gu, g_go, g_cq, g_ckv, w_uq, w_uk, w_uv, g_qn, g_kn, w_out) = p
    bsz, t, _ = h.shape
    qa, ka, va, ra, glf, glb, cq, ckv_raw, kr = split_cols(h @ w_in, EVEN_SPLIT)
    qa = qa.reshape(bsz, t, A_HEADS, A_DK) * (A_DK ** -0.5)
    ka = ka.reshape(bsz, t, A_HEADS, A_DK)
    va = va.reshape(bsz, t, A_HEADS, A_DV)
    la_f = gla_log_decay(glf, w_gu[0], b_gu[0])
    la_b = gla_log_decay(glb, w_gu[1], b_gu[1])
    if ctx is None:
        s0_f = jnp.zeros((bsz, A_HEADS, A_DK, A_DV), h.dtype)
        s0_b = s0_f
    else:
        s0_f, s0_b, ckv_ctx, kr_ctx = ctx
    oa, s_f, s_b = gla_bidir(qa, ka, va, la_f, la_b, s0_f, s0_b)
    oa = rms_norm(oa, g_go) * jax.nn.silu(ra).reshape(bsz, t, A_HEADS, A_DV)
    c_kv = rms_norm(ckv_raw, g_ckv)
    qb = (rms_norm(cq, g_cq) @ w_uq).reshape(bsz, t, B_HEADS, B_NOPE + B_ROPE)
    qb = rms_norm(qb, g_qn)
    kb, vb = mla_keys(c_kv, kr, w_uk, w_uv, g_kn)
    if ctx is None:
        new_ctx = (s_f, s_b, c_kv, kr)
    else:
        cos, sin = rope
        qb = rope_last(qb, cos, sin)
        kb = rope_last(kb, cos, sin)
        kc, vc = mla_keys(ckv_ctx, kr_ctx, w_uk, w_uv, g_kn)
        kb = jnp.concatenate([kb, kc], axis=1)
        vb = jnp.concatenate([vb, vc], axis=1)
        new_ctx = None
    ob = attn_blocked(qb[:, :, :, None, :], kb, vb, None)
    out = jnp.concatenate([oa.reshape(bsz, t, A_HEADS * A_DV), ob], axis=-1) @ w_out
    return out, new_ctx

def odd_mixer(h, p, ctx, rope):
    (w_in, w_pool, p_scale, g_qn, g_kn, sink, w_out) = p
    bsz, t, _ = h.shape
    g = D_HEADS // D_KV_HEADS
    xc, qd, kd, vd = split_cols(h @ w_in, ODD_SPLIT)
    oc = pool_mixer(xc, w_pool, p_scale)
    q = rms_norm(qd.reshape(bsz, t, D_HEADS, D_HEAD), g_qn)
    k = rms_norm(kd.reshape(bsz, t, D_KV_HEADS, D_HEAD), g_kn)
    v = vd.reshape(bsz, t, D_KV_HEADS, D_HEAD)
    sink_g = sink.reshape(D_KV_HEADS, g)
    if ctx is None:
        od = attn_blocked(q.reshape(bsz, t, D_KV_HEADS, g, D_HEAD), k, v, sink_g)
        new_ctx = (k, v)
    else:
        k_ctx, v_ctx = ctx
        cos, sin = rope
        q = rope_last(q, cos, sin)
        k = rope_last(k, cos, sin)
        od = window_attn(q.reshape(bsz, t, D_KV_HEADS, g, D_HEAD), k, v, k_ctx, v_ctx, sink_g)
        new_ctx = None
    out = jnp.concatenate([oc, od], axis=-1) @ w_out
    return out, new_ctx

def setup_inputs(seed: int = 0) -> dict:
    key = jax.random.key(seed)
    ks = iter(jax.random.split(key, 40))
    nrm = lambda shape, s: jax.random.normal(next(ks), shape, jnp.float32) * s
    gain = lambda shape: 1.0 + 0.05 * jax.random.normal(next(ks), shape, jnp.float32)
    d = D_MODEL
    sd = d ** -0.5
    return {
        'x_prompt': nrm((BATCH, SEQ, d), 1.0),
        'x_sample': nrm((DEC_BATCH, DEC_SEQ, d), 1.0),
        'state_gla': nrm((DEC_BATCH, N_EVEN, 2, A_HEADS, A_DK, A_DV), 1.0),
        'cache_mla_ckv': nrm((DEC_BATCH, N_EVEN, PAST_LEN, B_KV_RANK), 1.0),
        'cache_mla_krope': nrm((DEC_BATCH, N_EVEN, PAST_LEN, B_ROPE), 1.0),
        'cache_win_kv': nrm((DEC_BATCH, N_ODD, 2, PAST_LEN, D_KV_HEADS, D_HEAD), 1.0),
        'c': nrm((DEC_BATCH, d), 1.0),
        'c_ctx': nrm((d,), 1.0),
        'g_norm': gain((DEPTH, 2, d)),
        'w_ada': nrm((DEPTH, d, 6 * d), 0.5 * sd),
        'b_ada': nrm((DEPTH, 6 * d), 0.02),
        'w_in_even': nrm((N_EVEN, d, EVEN_IN), sd),
        'w_gate_up': nrm((N_EVEN, 2, A_GATE_RANK, A_HEADS * A_DK), A_GATE_RANK ** -0.5),
        'b_gate_up': nrm((N_EVEN, 2, A_HEADS * A_DK), 0.1),
        'g_gla_out': gain((N_EVEN, A_DV)),
        'g_mla_cq': gain((N_EVEN, B_Q_RANK)),
        'g_mla_ckv': gain((N_EVEN, B_KV_RANK)),
        'w_mla_uq': nrm((N_EVEN, B_Q_RANK, B_HEADS * (B_NOPE + B_ROPE)), B_Q_RANK ** -0.5),
        'w_mla_uk': nrm((N_EVEN, B_KV_RANK, B_HEADS * B_NOPE), B_KV_RANK ** -0.5),
        'w_mla_uv': nrm((N_EVEN, B_KV_RANK, B_HEADS * B_V), B_KV_RANK ** -0.5),
        'g_mla_qn': gain((N_EVEN, B_NOPE + B_ROPE)),
        'g_mla_kn': gain((N_EVEN, B_NOPE + B_ROPE)),
        'w_out_even': nrm((N_EVEN, EVEN_MIX, d), EVEN_MIX ** -0.5),
        'w_in_odd': nrm((N_ODD, d, ODD_IN), sd),
        'w_pool': nrm((N_ODD, C_GROUPS, C_GROUP_W, C_GROUP_W), C_GROUP_W ** -0.5),
        'pool_scale': gain((N_ODD, C_GROUPS * C_GROUP_W)),
        'g_win_qn': gain((N_ODD, D_HEAD)),
        'g_win_kn': gain((N_ODD, D_HEAD)),
        'win_sink': nrm((N_ODD, D_HEADS), 0.5),
        'w_out_odd': nrm((N_ODD, ODD_MIX, d), ODD_MIX ** -0.5),
        'peer_wq': nrm((DEPTH, d, P_HEADS * P_QDIM), sd),
        'peer_subkeys': nrm((DEPTH, P_HEADS, 2, P_NKEYS, P_QDIM // 2), (P_QDIM // 2) ** -0.5),
        'peer_u': nrm((DEPTH, P_EXPERTS, d), sd),
        'peer_v': nrm((DEPTH, P_EXPERTS, d), (P_HEADS * P_TOPK) ** -0.5),
    }

def reference(x_prompt, x_sample, state_gla, cache_mla_ckv, cache_mla_krope, cache_win_kv, c, c_ctx,
              g_norm, w_ada, b_ada, w_in_even, w_gate_up, b_gate_up, g_gla_out, g_mla_cq, g_mla_ckv,
              w_mla_uq, w_mla_uk, w_mla_uv, g_mla_qn, g_mla_kn, w_out_even, w_in_odd, w_pool, pool_scale,
              g_win_qn, g_win_kn, win_sink, w_out_odd, peer_wq, peer_subkeys, peer_u, peer_v):
    rows = x_sample.shape[1] // GRID_W
    rope_b = axial_rope(rows, B_ROPE)
    rope_d = axial_rope(rows, D_HEAD)
    xp, xs = x_prompt, x_sample
    gla_states, mla_ckv, mla_kr, win_kv = [], [], [], []
    for l in range(DEPTH):
        sh1p, sc1p, gt1p, sh2p, sc2p, gt2p = ada_mod(c_ctx, w_ada[l], b_ada[l])
        sh1s, sc1s, gt1s, sh2s, sc2s, gt2s = ada_mod(c, w_ada[l], b_ada[l])
        hp = modulate(xp, g_norm[l, 0], sh1p, sc1p)
        hs = modulate(xs, g_norm[l, 0], sh1s, sc1s)
        if l % 2 == 0:
            e = l // 2
            pe = (w_in_even[e], w_gate_up[e], b_gate_up[e], g_gla_out[e], g_mla_cq[e], g_mla_ckv[e],
                  w_mla_uq[e], w_mla_uk[e], w_mla_uv[e], g_mla_qn[e], g_mla_kn[e], w_out_even[e])
            mp, (s_f, s_b, ckv_p, kr_p) = even_mixer(hp, pe, None, None)
            ctx_s = (state_gla[:, e, 0], state_gla[:, e, 1], cache_mla_ckv[:, e], cache_mla_krope[:, e])
            ms, _ = even_mixer(hs, pe, ctx_s, rope_b)
            gla_states.append(jnp.stack([s_f, s_b], axis=1))
            mla_ckv.append(ckv_p)
            mla_kr.append(kr_p)
        else:
            o = l // 2
            po = (w_in_odd[o], w_pool[o], pool_scale[o], g_win_qn[o], g_win_kn[o], win_sink[o], w_out_odd[o])
            mp, (k_p, v_p) = odd_mixer(hp, po, None, None)
            ms, _ = odd_mixer(hs, po, (cache_win_kv[:, o, 0], cache_win_kv[:, o, 1]), rope_d)
            win_kv.append(jnp.stack([k_p, v_p], axis=1))
        xp = xp + gt1p * mp
        xs = xs + gt1s * ms
        hp = modulate(xp, g_norm[l, 1], sh2p, sc2p)
        hs = modulate(xs, g_norm[l, 1], sh2s, sc2s)
        xp = xp + gt2p * peer_ffn(hp, peer_wq[l], peer_subkeys[l], peer_u[l], peer_v[l])
        xs = xs + gt2s * peer_ffn(hs, peer_wq[l], peer_subkeys[l], peer_u[l], peer_v[l])
    state_gla_new = jnp.stack(gla_states, axis=1)
    cache_mla_ckv_new = jnp.stack(mla_ckv, axis=1)
    cache_mla_krope_new = jnp.stack(mla_kr, axis=1)
    cache_win_kv_new = jnp.stack(win_kv, axis=1)
    return (xp, xs, state_gla_new, cache_mla_ckv_new, cache_mla_krope_new, cache_win_kv_new)


_drawn_inputs = setup_inputs


def setup_inputs(seed=0):
    import zlib

    import numpy as np

    out = dict(_drawn_inputs(seed))
    spreads = {}
    factors = {'state_gla': 8.0,
     'cache_mla_ckv': 8.0,
     'cache_mla_krope': 8.0,
     'cache_win_kv': 4.719,
     'g_gla_out': 8.0,
     'g_mla_cq': 8.0,
     'w_mla_uk': 3.209,
     'g_mla_qn': 8.0,
     'g_mla_kn': 8.0,
     'pool_scale': 5.768,
     'g_win_qn': 8.0,
     'win_sink': 64.0,
     'peer_wq': 2.996,
     'peer_subkeys': 3.001,
     'peer_u': 3.331,
     'peer_v': 2.982}
    for name, (base, spread) in spreads.items():
        noise = np.random.default_rng([zlib.crc32(name.encode()), seed]).standard_normal(out[name].shape)
        drawn = base * np.exp(spread * noise) if base else spread * noise
        out[name] = jnp.asarray(drawn.astype(out[name].dtype))
    for name, factor in factors.items():
        out[name] = (out[name] * factor).astype(out[name].dtype)
    return out
```

```python
from contextlib import ExitStack

import numpy as np

import concourse.bass as bass
from concourse import mybir

F32 = mybir.dt.float32
U32 = mybir.dt.uint32
ACT = mybir.ActivationFunctionType
ALU = mybir.AluOpType
AX = mybir.AxisListType

P = 128
D = 1024
KD = D // P
NT = 5
T = NT * P
EPS = 1e-6
LAYERS = 2
NH = 8
TOPK = 16
NEXP = 128
GROUP = 4
NG = NEXP // GROUP
TB = 32
NB = T // TB
GRID_W = 64
WINDOWS = (2, 4, 8, 16)
LOWEST = -3.0e38
MLA_SCALE = 128.0 ** -0.5
WIN_SCALE = 64.0 ** -0.5

Q0, K0, V0, R0, CQ0, CKV0, GL0, KR0, EVEN_W = 0, 256, 512, 1024, 1536, 1792, 2048, 2080, 2144
EVEN_CHUNKS = [(0, 512), (512, 512), (1024, 512), (1536, 512), (2048, 96)]
XC0, QD0, KD0, VD0, ODD_W = 0, 512, 1024, 1152, 1280
ODD_CHUNKS = [(0, 512), (512, 512), (1024, 256)]

C_ID, C_IOTA, C_CUM, C_REST, C_IND, C_SEL, C_ROPE, C_MASK = 0, 128, 256, 512, 768, 770, 1026, 1538
C_ONE = 2050
C_N = 2052
(S_C, S_GN, S_CKV, S_CQ, S_QN, S_KN, S_GO, S_WQN, S_WKN, S_SINK, S_PS) = (
    0, 16, 48, 304, 560, 688, 816, 817, 881, 945, 953)
S_N = 957


def build_program(nc, a):
    ctx = ExitStack()
    with ctx:
        def sb(name, shape, dt=F32):
            return ctx.enter_context(nc.sbuf_tensor(name, shape, dt))

        const = sb("const", [P, C_N])
        vecs = sb("vecs", [P, S_N])
        x = sb("x", [P, NT, D])
        hT = sb("hT", [P, KD, T])
        gate = sb("gate", [P, 2, 2, D])
        ring = sb("ring", [P, 4, 4096])
        arena = sb("arena", [P, 16384])
        silu_c = sb("silu_c", [P, KD, 2])
        ada_col = sb("ada_col", [P, 2, 2, KD, 2])
        mod = sb("mod", [P, 2, KD, 2])
        stat = sb("stat", [P, 64])
        sums = sb("sums", [P, NH])
        sinks = sb("sinks", [P, NH])
        sums40 = sb("sums40", [P, NT * NH])[:, :]
        tmp_i = sb("tmp_i", [P, TOPK], U32)
        bank = [ctx.enter_context(nc.psum_tensor(f"bank{i}", [P, 512], F32)) for i in range(4)]
        pair = ctx.enter_context(nc.psum_tensor("pair", [P, 4, 512], F32))

        ident = const[:, C_ID:C_ID + P]
        iota = const[:, C_IOTA:C_IOTA + P]
        cum = [const[:, C_CUM + P * i:C_CUM + P * (i + 1)] for i in range(2)]
        rest = [const[:, C_REST + P * i:C_REST + P * (i + 1)] for i in range(2)]
        ind = const[:, C_IND:C_IND + 2]
        rope = const[:, C_ROPE:C_ROPE + 512].rearrange("p (t s d) -> p t s d", t=4, s=2)
        wmask = const[:, C_MASK:C_MASK + 512]

        def views(base, *sizes):
            out, at = [], base
            for n in sizes:
                out.append(arena[:, at:at + n])
                at += n
            assert at <= 16384
            return out

        bias_rows, ada_rows = views(12288, 1024, 1024)
        xn0, xn1, junk = views(8192, 1024, 1024, 1024)
        pe_ = arena[:, 0:NT * EVEN_W].rearrange("p (t n) -> p t n", t=NT)
        (la, eb, en, es, kiT, attT, glT, sq5, wgu) = views(
            NT * EVEN_W, 512, 512, 512, 512, 512, 1024, 128, 512, 512)
        attT = attT.rearrange("p (r d q n) -> p r d q n", r=2, d=2, q=2)
        scan_cur = views(NT * EVEN_W + 2560, 512, 512)
        s_out = es.rearrange("p (d n) -> p d n", d=2)
        spare = ring[:, 2:4, :].rearrange("p a b -> p (a b)")
        upd = spare[:, 0:5120].rearrange("p (c d n) -> p c d n", c=10, d=2)
        qdT = spare[:, 5120:7680].rearrange("p (t q n) -> p t q n", t=NT, q=4)
        s_in = spare[:, 7680:8192].rearrange("p (d n) -> p d n", d=2)
        decay = sb("decay", [P, NT, 2, 2, 2])
        kT = spare[:, 0:6144].rearrange("p (h n) -> p h n", h=NH)
        probs = spare[:, 6144:7424].rearrange("p (b n) -> p b n", b=2)
        ckvT = spare[:, 7424:7680]
        ctx_ckv = spare[:, 7680:7936]
        ctx_kr = spare[:, 7936:8000]
        krr = spare[:, 8000:8064]
        krt = spare[:, 8064:8128]
        vals, qk, qT, att_o = views(NT * EVEN_W, 6 * 512, 1024, 1024, 512)
        vals = vals.rearrange("p (t n) -> p t n", t=6)
        sq10 = arena[:, 0:1024]
        pT = arena[:, EVEN_W:EVEN_W + 1280].rearrange("p (b n) -> p b n", b=2)
        po_ = arena[:, 0:NT * ODD_W].rearrange("p (t n) -> p t n", t=NT)
        (yT, kT2, k2, qn, qT2, soft_s, probs2, pT2, kctx, vctx, sqo, att_o2) = views(
            NT * ODD_W, 1280, 1536, 256, 512, 512, 1024, 1024, 1024, 128, 128, 512, 512)
        yT = yT.rearrange("p (b n) -> p b n", b=2)
        kT2 = kT2.rearrange("p (v n) -> p v n", v=2)
        soft_s = soft_s.rearrange("p (b n) -> p b n", b=2)
        probs2 = probs2.rearrange("p (b n) -> p b n", b=2)
        pT2 = pT2.rearrange("p (b n) -> p b n", b=2)
        (pickT, top_v, top_i, subk, qsT, sc_cut, cand, cand_cut, fin_v, fin_p, hot, pick, posab) = views(
            0, 3 * T, 1280, 1280, 2048, 1280, P, 256, 256, 640, 640, 2048, 1920, 1280)
        pickT = pickT.rearrange("p (k t) -> p k t", k=3)
        top_v5 = top_v.rearrange("p (t h c k) -> p t h c k", t=NT, h=NH, c=2)
        top_i5 = top_i.rearrange("p (t h c k) -> p t h c k", t=NT, h=NH, c=2)
        subk = subk.rearrange("p (g n) -> p g n", g=16)
        qsT = qsT.rearrange("p (b t) -> p b t", b=2)
        fin_v4 = fin_v.rearrange("p (t h k) -> p t h k", t=NT, h=NH)
        pick3 = pick.rearrange("p (w t n) -> p w t n", w=3, t=NT)
        (stage, hot_i, hot_j, cols) = views(1920, 8192, 1024, 1024, 192)
        stage = stage.rearrange("p (b j t) -> p b j t", b=2, j=P)
        hot_i = hot_i.rearrange("p (b q n) -> p b q n", b=2, q=4)
        hot_j = hot_j.rearrange("p (b q n) -> p b q n", b=2, q=4)
        cols = cols.rearrange("p (b k t) -> p b k t", b=2, k=3)
        acc, act_, gmat = views(0, 5120, 5120, 5120)
        acc = acc.rearrange("p (t d) -> p t d", t=NT)
        act_ = act_.rearrange("p (b j t) -> p b j t", b=2, j=GROUP)
        gmat = gmat.rearrange("p (b k j t) -> p b k j t", b=2, k=NB, j=GROUP)
        utab = [ring[:, 2 * b, :].rearrange("p (j c e) -> p j c e", j=GROUP, c=KD) for b in range(2)]
        vtab = [ring[:, 2 * b + 1, :].rearrange("p (j d) -> p j d", j=GROUP) for b in range(2)]

        names = """
        const_in x_in bias_in0 bias_in1 slot_in0 slot_in1 wgu_in s_in_in ctx_in kvctx_in subk_in
        silu_done mods_done ss_ready var_ready std_ready xn_ready
        z_part z_exp la_ready exps_mul ctx_state s_ready oa_ready
        ckv_ready k_ready q_ready m_ready p_ready es_ready x_done
        d_full d_free a_full a_free s_full s_free
        gate_in gate_exp pick_ready hot_ready g_full g_free stage_out0 stage_out1
        u_in0 u_in1 v_in0 v_in1 g_in0 g_in1 h_full gelu_done act_ready o_full o_free
        out_state out_cache out_y chain_v chain_a
        """.split()
        sem = {n: ctx.enter_context(nc.semaphore(n)) for n in names}
        total = {}

        class Turn:

            def __init__(self, eng, chain=None):
                self.eng, self.n, self.chain = eng, {}, chain

            def next(self, name):
                self.n[name] = self.n.get(name, 0) + 1
                return self.n[name]

            def due(self, name, step=1):
                return sem[name], self.next(name) * step

            def after(self, name, k):
                if k > 0:
                    self.eng.wait_ge(sem[name], k)

            def give(self, ins, name):
                ins.then_inc(sem[name], 1)
                total[name] = total.get(name, 0) + 1
                self.eng.wait_ge(sem[name], total[name])

            def link(self, ins):
                self.give(ins, self.chain)

        def bc(ap, n, at):
            ap = ap.unsqueeze(at)
            shape = [int(s) for s in ap.shape]
            shape[at] = n
            return ap.broadcast_to(shape)

        freed = {}
        marks = {}
        items = []
        per_layer = []

        for l in range(LAYERS):
            items += [a["w_ada"][l, n] for n in range(12)]
            items += [a[f"w_in{l}_{n}"] for n in range(5 if l == 0 else 3)]
            items += [a["w_mla"] if l == 0 else a["w_band"]]
            items += [a[f"w_out{l}"][n] for n in range(2)]
            items += [a["peer_wq"][l, n] for n in range(4)]
            per_layer.append(len(items))
        routing = nc.dram_tensor("routing", (NG, P, NB, GROUP, TB), F32, kind="Internal").ap()

        def window_tiles(qt):
            return [0] if qt == 0 else [t for t in (qt - 1, qt, qt + 1) if 1 <= t < NT] + [5]

        block = ctx.enter_context(nc.Block())

        @block.tensor
        def _(pe):
            me = Turn(pe)
            mm = nc.tensor.matmul
            tr = nc.tensor.transpose
            item = [0]

            def slot():
                n = item[0]
                item[0] += 1
                pe.wait_ge(sem[f"slot_in{n % 2}"], 16 * (n // 2 + 1))
                return ring[:, n % 2, :]

            def slot_done():
                freed[item[0] - 1] = (last_stream[0], me.n[last_stream[0]])

            def mark(name):
                marks[name] = dict(me.n)

            def copied():
                pe.wait_ge(sem["d_free"], me.n["d_full"])
                pe.wait_ge(sem["a_free"], me.n["a_full"])

            last_stream = ["d_full"]

            def open_d():
                n = me.next("d_full") - 1
                me.after("d_free", n - 1)
                last_stream[0] = "d_full"
                return bank[n % 2]

            def open_a():
                n = me.next("a_full") - 1
                me.after("a_free", n - 1)
                last_stream[0] = "a_full"
                return bank[2 + n % 2]

            def open_s():
                n = me.next("s_full") - 1
                me.after("s_free", n - 1)
                return pair[:, 2 * (n % 2):2 * (n % 2) + 2, :]

            def ada(l):
                if l == 0:
                    pe.wait_ge(*me.due("silu_done"))
                    pe.wait_ge(sem["const_in"], 32)
                else:
                    pe.wait_ge(sem["o_free"], 4 + 10 * NG * l)
                for n in range(12):
                    w = slot().rearrange("p (k n) -> p k n", k=KD)
                    out = open_d()
                    for k in range(KD):
                        mm(out[0:2, :], silu_c[:, k, :], w[:, k, :], start=(k == 0), stop=False)
                    i = l * 12 + n
                    pe.wait_ge(sem[f"bias_in{i % 2}"], 16 * (i // 2 + 1))
                    mm(out[0:2, :], const[0:1, C_ONE:C_ONE + 2], bias_rows[0:1, 512 * (i % 2):512 * (i % 2) + 512],
                       start=False, stop=True).then_inc(sem["d_full"], 1)
                    slot_done()
                    pe.wait_ge(sem["d_free"], me.n["d_full"])
                    row = ada_rows[0:2, 512 * (i % 2):512 * (i % 2) + 512]
                    if n // 2 in (2, 5):
                        for c in range(2):
                            mm(open_a()[:, :], const[0:2, C_SEL + P * c:C_SEL + P * (c + 1)], row,
                               start=True, stop=True).then_inc(sem["a_full"], 1)
                    else:
                        out = open_d()
                        for k in range(4):
                            last = tr(out[:, 2 * k:2 * k + 2], row[:, P * k:P * (k + 1)], ident[0:2, 0:2])
                        last.then_inc(sem["d_full"], 1)

            def norm(l, s):
                for t in range(NT):
                    pe.wait_ge(*me.due("xn_ready"))
                    xn = (xn0, xn1)[t % 2]
                    out = open_a()
                    for k in range(4, 8):
                        last = tr(out[:, P * (k - 4):P * (k - 3)], xn[:, P * k:P * (k + 1)], ident)
                    last.then_inc(sem["a_full"], 1)
                    out = open_d()
                    for k in range(4):
                        last = tr(out[:, P * k:P * (k + 1)], xn[:, P * k:P * (k + 1)], ident)
                    last.then_inc(sem["d_full"], 1)

            def project(chunks):
                copied()
                for n, (_, w) in enumerate(chunks):
                    weights = slot()[:, 0:KD * w].rearrange("p (k n) -> p k n", k=KD)
                    for t in range(NT):
                        to_d = (n * NT + t) % 2 == 0 and n != 2
                        out = open_d() if to_d else open_a()
                        for k in range(KD):
                            last = mm(out[:, 0:w], hT[:, k, P * t:P * (t + 1)], weights[:, k, :],
                                      start=(k == 0), stop=(k == KD - 1))
                        last.then_inc(sem["d_full" if to_d else "a_full"], 1)
                    slot_done()
                mark(("proj", layer[0]))

            def gla():
                copied()
                pe.wait_ge(sem["wgu_in"], 16)
                for t in range(NT):
                    pt = pe_[:, t, :]
                    tr(open_d()[0:32, 0:P], pt[:, GL0:GL0 + 32], ident).then_inc(sem["d_full"], 1)
                    pe.wait_ge(sem["d_free"], me.n["d_full"])
                    mm(open_d()[:, :], glT[0:33, :], wgu[0:33, :], start=True, stop=True).then_inc(sem["d_full"], 1)
                    pe.wait_ge(*me.due("la_ready"))
                    for mats in (cum, rest):
                        out = open_a()
                        for d in range(2):
                            last = mm(out[:, 256 * d:256 * d + 256], mats[d], la[:, 256 * d:256 * d + 256],
                                      start=True, stop=True)
                        last.then_inc(sem["a_full"], 1)
                    out = open_a()
                    for d in range(2):
                        for q in range(2):
                            last = mm(out[:, 4 * d + 2 * q:4 * d + 2 * q + 2],
                                      la[:, 256 * d + P * q:256 * d + P * (q + 1)], ind, start=True, stop=True)
                    last.then_inc(sem["a_full"], 1)
                    mark(("exps", t))
                    pe.wait_ge(*me.due("exps_mul"))
                    for src, opened, full in ((eb, open_d, "d_full"), (en, open_a, "a_full")):
                        out = opened()
                        for q in range(4):
                            last = tr(out[:, P * q:P * (q + 1)], src[:, P * q:P * (q + 1)], ident)
                        last.then_inc(sem[full], 1)
                    copied()
                    out = open_s()
                    for r in range(2):
                        for d in range(2):
                            for q in range(2):
                                h = slice(64 * r, 64 * r + 64)
                                last = mm(out[:, r, 256 * d + P * q:256 * d + P * (q + 1)],
                                          kiT[h, P * (2 * d + q):P * (2 * d + q + 1)],
                                          qdT[h, t, 2 * d + q, :], start=True, stop=True)
                    last.then_inc(sem["s_full"], 1)
                    out = open_s()
                    for c in range(2):
                        for d in range(2):
                            for h in range(4):
                                r, q = h % 2, h // 2
                                last = mm(out[64 * r:64 * r + 64, c, 256 * d + P * q:256 * d + P * (q + 1)],
                                          es[64 * c:64 * c + 64, 256 * d + 64 * h:256 * d + 64 * h + 64],
                                          pt[64 * c:64 * c + 64, V0 + P * h:V0 + P * (h + 1)],
                                          start=True, stop=True)
                    last.then_inc(sem["s_full"], 1)
                    pe.wait_ge(sem["s_free"], me.n["s_full"] - 1)
                    out = open_d()
                    for h in range(4):
                        for d in range(2):
                            last = mm(out[:, P * h:P * (h + 1)], attT[:, h % 2, d, h // 2, :],
                                      pt[:, V0 + P * h:V0 + P * (h + 1)], start=(d == 0), stop=(d == 1))
                    last.then_inc(sem["d_full"], 1)
                mark("gla_tiles")
                pe.wait_ge(*me.due("s_ready"))
                for t in range(NT):
                    out = open_s()
                    for c in range(2):
                        for r in range(2):
                            for q in range(2):
                                for d in range(2):
                                    h = slice(64 * r, 64 * r + 64)
                                    last = mm(out[64 * c:64 * c + 64, r, P * q:P * (q + 1)],
                                              qdT[h, t, 2 * d + q, 64 * c:64 * c + 64],
                                              upd[h, 2 * t + c, d, P * q:P * (q + 1)],
                                              start=(d == 0 and q == 0), stop=(d == 1), skip_group_check=True)
                    last.then_inc(sem["s_full"], 1)
                for t in range(NT):
                    pe.wait_ge(*me.due("oa_ready"))
                    out = open_a()
                    for h in range(4):
                        last = tr(out[:, P * h:P * (h + 1)], pe_[:, t, P * h:P * (h + 1)], ident)
                    last.then_inc(sem["a_full"], 1)
                mark("oa")

            def attend(q_lhs, keys):
                out = open_s().rearrange("p a b -> p (a b)")
                for k_ap, at, n in keys:
                    last = mm(out[:, at:at + n], q_lhs, k_ap, start=(at % 512 == 0), stop=True, skip_group_check=True)
                last.then_inc(sem["s_full"], 1)

            def weigh(probs_b, pT_b, tiles, v_of):
                pe.wait_ge(*me.due("p_ready"))
                n = len(tiles)
                out = open_d()
                for i in range(min(n, 4)):
                    last = tr(out[:, P * i:P * (i + 1)], probs_b[:, P * i:P * (i + 1)], ident)
                last.then_inc(sem["d_full"], 1)
                if n > 4:
                    tr(open_a()[:, 0:P], probs_b[:, 4 * P:5 * P], ident).then_inc(sem["a_full"], 1)
                copied()
                out = open_d()
                for i, kt in enumerate(tiles):
                    last = mm(out[:, 0:64], pT_b[:, P * i:P * (i + 1)], v_of(kt), start=(i == 0), stop=(i == n - 1))
                last.then_inc(sem["d_full"], 1)

            def mla():
                w = slot()
                w_uq = w[:, 0:2048].rearrange("p (k n) -> p k n", k=2)
                w_uk = w[:, 2048:3072].rearrange("p (k n) -> p k n", k=2)
                w_uv = w[:, 3072:4096].rearrange("p (k n) -> p k n", k=2)
                for kt in range(6):
                    pe.wait_ge(*me.due("ckv_ready"))
                    ckv = pe_[:, kt, CKV0:CKV0 + 256] if kt < NT else ctx_ckv
                    out = open_d()
                    for k in range(2):
                        last = tr(out[:, P * k:P * (k + 1)], ckv[:, P * k:P * (k + 1)], ident)
                    last.then_inc(sem["d_full"], 1)
                    pe.wait_ge(sem["d_free"], me.n["d_full"])
                    for wk, opened, full in ((w_uk, open_d, "d_full"), (w_uv, open_a, "a_full")):
                        out = opened()
                        for k in range(2):
                            last = mm(out[:, :], ckvT[:, P * k:P * (k + 1)], wk[:, k, :], start=(k == 0), stop=(k == 1))
                        last.then_inc(sem[full], 1)
                    pe.wait_ge(*me.due("k_ready"))
                    for g in range(2):
                        out = open_a()
                        for i in range(4):
                            h = 4 * g + i
                            last = tr(out[:, P * i:P * (i + 1)], qk[:, P * h:P * (h + 1)], ident)
                        last.then_inc(sem["a_full"], 1)
                copied()
                for qt in range(NT):
                    pe.wait_ge(*me.due("ckv_ready"))
                    out = open_d()
                    for k in range(2):
                        last = tr(out[:, P * k:P * (k + 1)], pe_[:, qt, CQ0 + P * k:CQ0 + P * (k + 1)], ident)
                    last.then_inc(sem["d_full"], 1)
                    pe.wait_ge(sem["d_free"], me.n["d_full"])
                    for g in range(2):
                        out = open_d()
                        for k in range(2):
                            last = mm(out[:, :], ckvT[:, P * k:P * (k + 1)], w_uq[:, k, 512 * g:512 * g + 512],
                                      start=(k == 0), stop=(k == 1))
                        last.then_inc(sem["d_full"], 1)
                    if qt == NT - 1:
                        slot_done()
                    pe.wait_ge(*me.due("q_ready"))
                    for g in range(2):
                        out = open_a()
                        for i in range(4):
                            h = 4 * g + i
                            last = tr(out[:, P * i:P * (i + 1)], qk[:, P * h:P * (h + 1)], ident)
                        last.then_inc(sem["a_full"], 1)
                    copied()
                    tiles = [0] if qt == 0 else [1, 2, 3, 4, 5]
                    mark(("scores", qt))

                    def scores(h):
                        q_lhs = qT[:, P * h:P * (h + 1)]
                        if qt == 0:
                            attend(q_lhs, [(kT[:, h, 0:P], 0, P)])
                        else:
                            attend(q_lhs, [(kT[:, h, P:P + 512], 0, 512), (kT[:, h, P + 512:P + 640], 512, P)])

                    scores(0)
                    for h in range(NH):
                        if h + 1 < NH:
                            scores(h + 1)
                        weigh(probs[:, h % 2, :], pT[:, h % 2, :], tiles,
                              lambda kt, h=h: vals[:, kt, 64 * h:64 * h + 64])
                    turn_out()

            def turn_out():
                copied()
                out = open_a()
                src = att_o if layer[0] == 0 else att_o2
                for i in range(4):
                    last = tr(out[:, P * i:P * (i + 1)], src[:, P * i:P * (i + 1)], ident)
                last.then_inc(sem["a_full"], 1)

            def odd():
                copied()
                w = slot()
                band = w[:, 0:3072].rearrange("p (g b n) -> p g b n", g=4, b=6)
                w_pool = w[:, 3072:3584].rearrange("p (g n) -> p g n", g=4)
                for g in range(4):
                    xc = [po_[:, t, XC0 + P * g:XC0 + P * (g + 1)] for t in range(NT)]
                    near = {0: [(0, 0)], 1: [(1, 1), (2, 5)], 2: [(1, 4), (2, 2), (3, 5)],
                            3: [(2, 4), (3, 2), (4, 5)], 4: [(3, 4), (4, 3)]}
                    out = open_d()
                    mm(out[:, 0:P], xc[0], band[:, g, 0, :], start=True, stop=True).then_inc(sem["d_full"], 1)
                    out = open_d()
                    for t in range(1, NT):
                        for i, (u, b) in enumerate(near[t]):
                            last = mm(out[:, P * (t - 1):P * t], xc[u], band[:, g, b, :],
                                      start=(i == 0), stop=(i == len(near[t]) - 1))
                    last.then_inc(sem["d_full"], 1)
                    pe.wait_ge(sem["d_free"], me.n["d_full"])
                    for at, n in ((0, 512), (512, P)):
                        mm(open_a()[:, 0:n], w_pool[:, g, :], yT[:, g % 2, at:at + n],
                           start=True, stop=True).then_inc(sem["a_full"], 1)
                slot_done()
                for kt in range(6):
                    pe.wait_ge(*me.due("k_ready"))
                    out = open_a()
                    for v in range(2):
                        last = tr(out[:, P * v:P * (v + 1)], k2[:, P * v:P * (v + 1)], ident)
                    last.then_inc(sem["a_full"], 1)
                    mark(("odd_k", kt))
                pe.wait_ge(sem["kvctx_in"], 32)
                for qt in range(NT):
                    pe.wait_ge(*me.due("q_ready"))
                    out = open_a()
                    for i in range(4):
                        last = tr(out[:, P * i:P * (i + 1)], qn[:, P * i:P * (i + 1)], ident)
                    last.then_inc(sem["a_full"], 1)
                    copied()
                    tiles = window_tiles(qt)

                    def scores(h):
                        part = slice(64 * (h % 2), 64 * (h % 2) + 64)
                        q_lhs = qT2[part, P * (h // 2):P * (h // 2 + 1)]
                        local = [t for t in tiles if t < NT]
                        keys = [(kT2[part, h // 4, P * local[0]:P * (local[-1] + 1)], 0, P * len(local))]
                        if qt:
                            keys.append((kT2[part, h // 4, P * 5:P * 6], P * len(local), P))
                        attend(q_lhs, keys)

                    scores(0)
                    for h in range(NH):
                        if h + 1 < NH:
                            scores(h + 1)
                        weigh(probs2[:, h % 2, :], pT2[:, h % 2, :], tiles,
                              lambda kt, h=h: (po_[:, kt, VD0 + 64 * (h // 4):VD0 + 64 * (h // 4) + 64] if kt < NT
                                               else vctx[:, 64 * (h // 4):64 * (h // 4) + 64]))
                    turn_out()

            def out_project():
                copied()
                for n in range(2):
                    w = slot().rearrange("p (k n) -> p k n", k=KD)
                    for t in range(NT):
                        out = open_d()
                        for k in range(KD):
                            last = mm(out[:, :], hT[:, k, P * t:P * (t + 1)], w[:, k, :], start=(k == 0), stop=(k == KD - 1))
                        last.then_inc(sem["d_full"], 1)
                    slot_done()

            def route(l):
                copied()
                pe.wait_ge(sem["subk_in"], 16 * (l + 1))
                for g in range(16):
                    if g % 4 == 0:
                        w = slot().rearrange("p (k n) -> p k n", k=KD)
                    for at, n in ((0, 512), (512, P)):
                        out = open_a()
                        for k in range(KD):
                            last = mm(out[:, 0:n], w[:, k, P * (g % 4):P * (g % 4 + 1)], hT[:, k, at:at + n],
                                      start=(k == 0), stop=(k == KD - 1))
                        last.then_inc(sem["a_full"], 1)
                    if g % 4 == 3:
                        slot_done()
                    pe.wait_ge(sem["a_free"], me.n["a_full"])
                    out = open_s()
                    for t in range(NT):
                        last = mm(out[:, t // 4, P * (t % 4):P * (t % 4 + 1)], qsT[:, g % 2, P * t:P * (t + 1)],
                                  subk[:, g, :], start=True, stop=True)
                    last.then_inc(sem["s_full"], 1)
                for t in range(NT):
                    pe.wait_ge(*me.due("pick_ready"))
                    out = open_d()
                    for w3 in range(3):
                        last = tr(out[:, P * w3:P * (w3 + 1)], pick3[:, w3, t, :], ident)
                    last.then_inc(sem["d_full"], 1)

            def routing_matrix(l):
                jobs = TB // 4
                with pe.Fori(0, NB // 2) as i:
                    for n in range(2 * jobs):
                        at = l * (NB * jobs) + n
                        pe.wait_ge(sem["hot_ready"], i * (2 * jobs) + (at + 1))
                        pe.wait_ge(sem["g_free"], i * (2 * jobs) + (at + 1))
                        for q in range(4):
                            last = mm(pair[:, n % 4, P * q:P * (q + 1)], hot_i[:, n % 2, q, :], hot_j[:, n % 2, q, :],
                                      start=True, stop=True)
                        last.then_inc(sem["g_full"], 1)

            def dense(l):
                def experts(b, base, g):
                    pe.wait_ge(sem[f"u_in{b}"], 16 * (l * (NG // 2) + 1) + g * 16)
                    for j in range(GROUP):
                        for half, (at, n) in enumerate(((0, 384), (384, 256))):
                            m = 2 * j + half
                            pe.wait_ge(sem["gelu_done"], base + (m + 1))
                            for k in range(KD):
                                last = mm(pair[:, m % 4, 0:n], utab[b][:, j, k, :], hT[:, k, at:at + n],
                                          start=(k == 0), stop=(k == KD - 1))
                            last.then_inc(sem["h_full"], 1)

                def values(b, base, base_act, g):
                    pe.wait_ge(sem[f"v_in{b}"], 16 * (l * (NG // 2) + 1) + g * 16)
                    pe.wait_ge(sem["act_ready"], base_act)
                    for m in range(2 * NT):
                        t, half = m // 2, m % 2
                        pe.wait_ge(sem["o_free"], base + (m + 1))
                        for j in range(GROUP):
                            last = mm(bank[(2 * (b % 2) + m) % 4][:, :], act_[:, b, j, P * t:P * (t + 1)],
                                      vtab[b][:, j, 512 * half:512 * half + 512], start=(j == 0), stop=(j == GROUP - 1))
                        last.then_inc(sem["o_full"], 1)

                H0, O0 = l * 8 * NG, l * 10 * NG
                pe.wait_ge(sem["g_free"], 4 + (l + 1) * T // 4)
                experts(0, H0, 0)
                with pe.Fori(0, NG // 2 - 1) as i:
                    experts(1, i * 16 + (H0 + 8), i)
                    values(0, i * 20 + O0, i * 16 + (H0 + 8), i)
                    experts(0, i * 16 + (H0 + 16), i + 1)
                    values(1, i * 20 + (O0 + 10), i * 16 + (H0 + 16), i)
                i = NG // 2 - 1
                experts(1, i * 16 + (H0 + 8), i)
                values(0, i * 20 + O0, i * 16 + (H0 + 8), i)
                values(1, i * 20 + (O0 + 10), i * 16 + (H0 + 16), i)

            pe.sem_inc(sem["g_full"], 2)
            pe.sem_inc(sem["o_full"], 1)
            layer = [0]
            for l in range(LAYERS):
                layer[0] = l
                ada(l)
                norm(l, 0)
                if l == 0:
                    project(EVEN_CHUNKS)
                    gla()
                    mla()
                else:
                    project(ODD_CHUNKS)
                    odd()
                out_project()
                norm(l, 1)
                route(l)
                routing_matrix(l)
                dense(l)

        @block.scalar
        def _(act):
            me = Turn(act, "chain_a")
            do = nc.scalar.activation
            link, give = me.link, me.give

            def take_a():
                n = me.next("a_full")
                act.wait_ge(sem["a_full"], n)
                return bank[2 + (n - 1) % 2]

            def copy_a(dst, w=512, func=ACT.Copy, **how):
                out = take_a()
                src = out[0:int(dst.shape[0]), 0:w]
                if len(dst.shape) == 3:
                    src = src.rearrange("p (k n) -> p k n", k=int(dst.shape[1]))
                give(do(dst, src, func, **how), "a_free")

            def root(n, at):
                act.wait_ge(*me.due("var_ready"))
                give(do(stat[:, at:at + n], stat[:, at:at + n], ACT.Sqrt), "std_ready")

            def ada(l):
                for kind in (2, 5):
                    for n in range(2):
                        for c in range(2):
                            copy_a(gate[:, kind // 3, c, 512 * n:512 * n + 512])

            def norm(l, s):
                if l == 0 and s == 0:
                    act.wait_ge(sem["x_in"], 16)
                else:
                    act.wait_ge(*me.due("x_done"))
                for t in range(NT):
                    ins = do(junk, x[:, t, :], ACT.Square, accum_out=stat[:, t:t + 1])
                    if t < NT - 1:
                        link(ins)
                give(ins, "ss_ready")
                root(NT, 0)
                act.wait_ge(*me.due("mods_done"))
                for t in range(NT):
                    c = int(t > 0)
                    out = take_a()
                    for k in range(4, 8):
                        ins = do(hT[:, k, P * t:P * (t + 1)], out[:, P * (k - 4):P * (k - 3)], ACT.Identity,
                                 bias=ada_col[:, s, 0, k, c:c + 1], scale=mod[:, s, k, c:c + 1])
                    give(ins, "a_free")

            def project(chunks, dst):
                for n, (at, w) in enumerate(chunks):
                    for t in range(NT):
                        if not ((n * NT + t) % 2 == 0 and n != 2):
                            copy_a(dst[:, t, at:at + w], w, ACT.Silu if at == R0 and dst is pe_ else ACT.Copy)

            def gla():
                for t in range(NT):
                    act.wait_ge(*me.due("z_part"))
                    link(do(en, eb, ACT.Exp, scale=-1.0))
                    give(do(en, en, ACT.Ln, bias=1.0), "z_exp")
                    out = take_a()
                    do(eb, out[:, :], ACT.Exp)
                    give(do(en, out[:, :], ACT.Exp, scale=-1.0), "a_free")
                    out = take_a()
                    give(do(es, out[:, :], ACT.Exp), "a_free")
                    out = take_a()
                    give(do(decay[:, t].rearrange("p d q c -> p (d q c)"), out[:, 0:8], ACT.Exp), "a_free")
                    copy_a(kiT)
                for t in range(NT):
                    root(4, 8)
                for t in range(NT):
                    copy_a(hT[:, 0:4, P * t:P * (t + 1)], scale=vecs[:, S_GO:S_GO + 1])

            def mla():
                me.after("out_state", 64)
                for kt in range(6):
                    if kt < NT:
                        root(1, 16)
                    copy_a(vals[:, kt, :])
                    root(8, 24)
                    for g in range(2):
                        copy_a(kT[:, 4 * g:4 * g + 4, P * kt:P * (kt + 1)])
                for qt in range(NT):
                    root(1, 16)
                    root(8, 24)
                    for g in range(2):
                        copy_a(qT[:, 512 * g:512 * g + 512])
                    n = P if qt == 0 else 5 * P

                    def soften(h):
                        act.wait_ge(*me.due("m_ready"))
                        at = 2 * ((marks[("scores", qt)]["s_full"] + h) % 2)
                        out = pair[:, at:at + 2, :].rearrange("p a b -> p (a b)")
                        give(do(probs[:, h % 2, 0:n], out[:, 0:n], ACT.Exp, bias=stat[:, 32 + h:33 + h],
                                scale=MLA_SCALE, accum_out=sums[:, h:h + 1]), "p_ready")

                    soften(0)
                    for h in range(NH):
                        if h + 1 < NH:
                            soften(h + 1)
                        if n > 512:
                            copy_a(pT[:, h % 2, 512:640], P)
                    copy_a(hT[:, 4:8, P * qt:P * (qt + 1)])

            def odd():
                for g in range(4):
                    scale = vecs[:, S_PS + g:S_PS + g + 1]
                    for at, n in ((0, 512), (512, P)):
                        copy_a(hT[:, g, at:at + n], n, scale=scale)
                for kt in range(6):
                    if kt < NT:
                        root(2, 24)
                    copy_a(kT2[:, :, P * kt:P * (kt + 1)], 256)
                for qt in range(NT):
                    root(8, 24)
                    copy_a(qT2)
                    n = P * len(window_tiles(qt))

                    def soften(h):
                        act.wait_ge(*me.due("m_ready"))
                        bias = stat[:, 32 + h:33 + h]
                        give(do(probs2[:, h % 2, 0:n], soft_s[:, h % 2, 0:n], ACT.Exp, bias=bias,
                                accum_out=sums[:, h:h + 1]), "p_ready")
                        give(do(sinks[:, h:h + 1], vecs[:, S_SINK + h:S_SINK + h + 1], ACT.Exp, bias=bias), "es_ready")

                    for h in range(NH):
                        soften(h)
                    copy_a(hT[:, 4:8, P * qt:P * (qt + 1)])

            def route():
                for g in range(16):
                    copy_a(qsT[:, g % 2, 0:512])
                    copy_a(qsT[:, g % 2, 512:640], P)
                act.wait_ge(*me.due("gate_in"))
                give(do(fin_v, fin_v, ACT.Exp), "gate_exp")

            def routing_matrix(l):
                jobs = TB // 4
                at = l * NB * jobs
                with act.Fori(0, NB // 2) as i:
                    for b in range(2):
                        act.wait_ge(sem[f"stage_out{b}"], i * 16 + 16 * (l * (NB // 2) + 1))
                        for n in range(jobs):
                            m = b * jobs + n
                            act.wait_ge(sem["g_full"], i * (2 * jobs) + (at + m + 3))
                            do(stage[:, b, :, 4 * n:4 * n + 4], pair[:, m % 4, :].rearrange("p (q j) -> p j q", q=4),
                               ACT.Copy).then_inc(sem["g_free"], 1)

            def dense(l):
                H0, O0 = l * 8 * NG, l * 10 * NG

                def gelu(b, base, free):
                    act.wait_ge(sem["o_full"], free)
                    for m in range(2 * GROUP):
                        at, n = ((0, 384), (384, 256))[m % 2]
                        act.wait_ge(sem["h_full"], base + (m + 1))
                        do(act_[:, b, m // 2, at:at + n], pair[:, m % 4, 0:n], ACT.Gelu).then_inc(sem["gelu_done"], 1)

                for b in range(2):
                    act.wait_ge(sem[f"stage_out{b}"], 16 + 16 * (l + 1) * NB // 2)
                gelu(0, H0, O0 + 1)
                with act.Fori(0, NG // 2 - 1) as i:
                    gelu(1, i * 16 + (H0 + 8), i * 20 + (O0 + 1))
                    gelu(0, i * 16 + (H0 + 16), i * 20 + (O0 + 11))
                i = NG // 2 - 1
                gelu(1, i * 16 + (H0 + 8), i * 20 + (O0 + 1))

            act.sem_inc(sem["g_free"], 4)
            act.sem_inc(sem["gelu_done"], 4)
            act.wait_ge(sem["const_in"], 32)
            give(do(silu_c.rearrange("p k c -> p (k c)"), vecs[:, S_C:S_C + 16], ACT.Silu), "silu_done")
            for l in range(LAYERS):
                ada(l)
                norm(l, 0)
                if l == 0:
                    project(EVEN_CHUNKS, pe_)
                    gla()
                    mla()
                else:
                    project(ODD_CHUNKS, po_)
                    odd()
                norm(l, 1)
                route()
                routing_matrix(l)
                dense(l)

        @block.sync
        def _(sp):
            sp.sem_inc(sem["stage_out0"], 16)
            sp.sem_inc(sem["stage_out1"], 16)

            def after(name, k):
                if k > 0:
                    sp.wait_ge(sem[name], k)

            def load(n):
                l = 0 if n < per_layer[0] else 1
                if n - 2 >= (0 if l == 0 else per_layer[0]):
                    after(*freed[n - 2])
                src = items[n]
                w = int(src.shape[1])
                sp.dma_start(ring[:, n % 2, 0:w], src).then_inc(sem[f"slot_in{n % 2}"], 16)

            for l in range(LAYERS):
                first = 0 if l == 0 else per_layer[0]
                H0, O0 = l * 8 * NG, l * 10 * NG
                if l:
                    sp.wait_ge(sem["x_done"], 2)
                for n in range(first, per_layer[l]):
                    if n < first + 12:
                        i = l * 12 + n - first
                        if n - first >= 2:
                            after(*freed[n - 2])
                        sp.dma_start(bias_rows[0:1, 512 * (i % 2):512 * (i % 2) + 512],
                                     a["b_ada"][l, n - first]).then_inc(sem[f"bias_in{i % 2}"], 16)
                    load(n)
                at = l * (NG // 2)
                after(*freed[per_layer[l] - 2])
                sp.dma_start(ring[:, 0, :], a["peer_u"][l, 0]).then_inc(sem["u_in0"], 16)
                sp.dma_start(ring[:, 2, :], a["peer_u"][l, 1]).then_inc(sem["u_in1"], 16)
                sp.dma_start(ring[:, 3, :], a["peer_v"][l, 1]).then_inc(sem["v_in1"], 16)
                after(*freed[per_layer[l] - 1])
                sp.dma_start(ring[:, 1, :], a["peer_v"][l, 0]).then_inc(sem["v_in0"], 16)
                jobs = TB // 4
                with sp.Fori(0, NB // 2) as i:
                    for b in range(2):
                        sp.wait_ge(sem["g_free"], i * (2 * jobs) + (4 + l * NB * jobs + jobs * (b + 1)))
                        sp.dma_start(routing[:, :, bass.ds(i * 2 + b, 1), :, :].rearrange("g p k j t -> p g (k j t)"),
                                     stage[:, b, :, :].rearrange("p (g j) t -> p g (j t)", g=NG)
                                     ).then_inc(sem[f"stage_out{b}"], 16)
                for b in range(2):
                    sp.wait_ge(sem[f"stage_out{b}"], 16 + 16 * (l + 1) * NB // 2)
                for b in range(2):
                    sp.dma_start(gmat[:, b].rearrange("p k j t -> p (k j t)"),
                                 routing[b].rearrange("p k j t -> p (k j t)")).then_inc(sem[f"g_in{b}"], 16)
                with sp.Fori(1, NG // 2) as i:
                    for b in range(2):
                        g = i * 2 + b
                        sp.wait_ge(sem["h_full"], i * 16 + (H0 + 8 * b - 8))
                        sp.dma_start(ring[:, 2 * b, :], a["peer_u"][l, bass.ds(g, 1)].rearrange("g p n -> p (g n)")
                                     ).then_inc(sem[f"u_in{b}"], 16)
                        sp.wait_ge(sem["act_ready"], i * 16 + (H0 + 8 * b - 8))
                        sp.dma_start(gmat[:, b].rearrange("p k j t -> p (k j t)"),
                                     routing[bass.ds(g, 1)].rearrange("g p k j t -> p (g k j t)")
                                     ).then_inc(sem[f"g_in{b}"], 16)
                    for b in range(2):
                        g = i * 2 + b
                        sp.wait_ge(sem["o_full"], i * 20 + (O0 + 10 * b - 9))
                        sp.dma_start(ring[:, 2 * b + 1, :], a["peer_v"][l, bass.ds(g, 1)].rearrange("g p n -> p (g n)")
                                     ).then_inc(sem[f"v_in{b}"], 16)
            sp.wait_ge(sem["x_done"], 4)
            sp.dma_start(a["y_prompt"], x[:, 0, :]).then_inc(sem["out_y"], 16)
            sp.dma_start(a["y_sample"].rearrange("(t p) d -> p t d", p=P), x[:, 1:NT, :]).then_inc(sem["out_y"], 16)
            sp.wait_ge(sem["out_y"], 32)

        @block.gpsimd
        def _(pool):
            pool.dma_start(const[:, :], a["const"]).then_inc(sem["const_in"], 16)
            pool.dma_start(vecs[:, :], a["vecs"]).then_inc(sem["const_in"], 16)
            pool.dma_start(x[:, :, :], a["x"].rearrange("(t p) d -> p t d", p=P)).then_inc(sem["x_in"], 16)
            pool.dma_start(wgu[0:33, :], a["w_gu"]).then_inc(sem["wgu_in"], 16)
            for r in range(2):
                pool.dma_start(s_in[64 * r:64 * r + 64, :, :].rearrange("k d (q v) -> k d q v", q=2),
                               a["state_in"][:, :, r]).then_inc(sem["s_in_in"], 16)
            pool.wait_ge(sem["ctx_state"], 1)
            for d in range(2):
                for r in range(2):
                    pool.dma_start(a["state"][d].rearrange("(q r) k v -> r k q v", r=2)[r],
                                   s_out[64 * r:64 * r + 64, d, :].rearrange("k (q v) -> k q v", q=2)
                                   ).then_inc(sem["out_state"], 16)
            pool.wait_ge(sem["s_ready"], 1)
            pool.dma_start(ctx_ckv, a["ctx_ckv"]).then_inc(sem["ctx_in"], 16)
            pool.dma_start(ctx_kr, a["ctx_kr"]).then_inc(sem["ctx_in"], 16)
            pool.wait_ge(sem["ckv_ready"], 1)
            pool.dma_start(a["ckv"], pe_[:, 0, CKV0:CKV0 + 256]).then_inc(sem["out_cache"], 16)
            pool.dma_start(a["kr"], pe_[:, 0, KR0:KR0 + 64]).then_inc(sem["out_cache"], 16)
            for l in range(LAYERS):
                if l == 1:
                    pool.wait_ge(sem["k_ready"], 7)
                    pool.dma_start(kctx, a["k_ctx"]).then_inc(sem["kvctx_in"], 16)
                    pool.dma_start(vctx, a["v_ctx"]).then_inc(sem["kvctx_in"], 16)
                    pool.dma_start(a["win"][0], po_[:, 0, KD0:KD0 + P]).then_inc(sem["out_cache"], 16)
                    pool.dma_start(a["win"][1], po_[:, 0, VD0:VD0 + P]).then_inc(sem["out_cache"], 16)
                pool.wait_ge(sem["x_done"], 2 * l + 1)
                pool.dma_start(subk.rearrange("p g n -> p (g n)"), a["subkeys"][l]).then_inc(sem["subk_in"], 16)
            pool.wait_ge(sem["out_state"], 64)
            pool.wait_ge(sem["out_cache"], 64)

        @block.vector
        def _(dve):
            me = Turn(dve, "chain_v")
            V = nc.vector
            tt, ts, stt = V.tensor_tensor, V.tensor_scalar, V.scalar_tensor_tensor
            link, give = me.link, me.give

            def take_d():
                n = me.next("d_full")
                dve.wait_ge(sem["d_full"], n)
                return bank[(n - 1) % 2]

            def take_s():
                n = me.next("s_full")
                dve.wait_ge(sem["s_full"], n)
                return pair[:, 2 * ((n - 1) % 2):2 * ((n - 1) % 2) + 2, :]

            def signal(name):
                dve.sem_inc(sem[name], 1)
                total[name] = total.get(name, 0) + 1

            def rstd(ss, n):
                give(ts(ss, ss, 1.0 / n, EPS, ALU.mult, ALU.add), "var_ready")
                dve.wait_ge(*me.due("std_ready"))
                link(V.reciprocal(ss, ss))

            def ada(l):
                for n in range(12):
                    i = l * 12 + n
                    out = take_d()
                    row = ada_rows[0:2, 512 * (i % 2):512 * (i % 2) + 512]
                    give(V.tensor_copy(row, out[0:2, :]), "d_free")
                    kind = n // 2
                    if kind not in (2, 5):
                        out = take_d()
                        s, w = (0, kind) if kind < 2 else (1, kind - 3)
                        give(V.tensor_copy(ada_col[:, s, w, 4 * (n % 2):4 * (n % 2) + 4, :],
                                           out[:, 0:8].rearrange("p (k c) -> p k c", k=4)), "d_free")
                for s in range(2):
                    g = vecs[:, S_GN + 16 * l + 8 * s:S_GN + 16 * l + 8 * s + 8]
                    give(stt(mod[:, s, :, :], ada_col[:, s, 1, :, :], 1.0, bc(g, 2, 2), ALU.add, ALU.mult),
                         "mods_done")

            def norm(l, s):
                dve.wait_ge(*me.due("ss_ready"))
                rstd(stat[:, 0:NT], D)
                for t in range(NT):
                    give(ts((xn0, xn1)[t % 2], x[:, t, :], stat[:, t:t + 1], None, ALU.mult), "xn_ready")
                    if t:
                        evac_norm(s, t - 1)
                evac_norm(s, NT - 1)

            def evac_norm(s, t):
                out = take_d()
                c = int(t > 0)
                for k in range(4):
                    ins = ts(hT[:, k, P * t:P * (t + 1)], out[:, P * k:P * (k + 1)], mod[:, s, k, c:c + 1],
                             ada_col[:, s, 0, k, c:c + 1], ALU.mult, ALU.add)
                give(ins, "d_free")

            def project(chunks, dst):
                for n, (at, w) in enumerate(chunks):
                    for t in range(NT):
                        if (n * NT + t) % 2 == 0 and n != 2:
                            out = take_d()
                            give(V.tensor_copy(dst[:, t, at:at + w], out[:, 0:w]), "d_free")
                me.after("a_free", marks[("proj", layer[0])]["a_full"])

            def gla():
                link(V.memset(attT.rearrange("p r d q n -> p (r d q n)"), 0.0))
                link(V.memset(glT[32:33, :], 1.0))
                for t in range(NT):
                    pt = pe_[:, t, :]
                    out = take_d()
                    give(V.tensor_copy(glT[0:32, :], out[0:32, 0:P]), "d_free")
                    out = take_d()
                    link(ts(eb, out[:, :], -1.0, None, ALU.mult))
                    give(tt(eb, eb, out[:, :], ALU.max), "z_part")
                    give(ts(la, out[:, :], 0.0, 1.0 / 16.0, ALU.min, ALU.mult), "d_free")
                    dve.wait_ge(*me.due("z_exp"))
                    give(stt(la, en, -1.0 / 16.0, la, ALU.mult, ALU.add), "la_ready")
                    me.after("a_free", marks[("exps", t)]["a_full"])
                    q2 = bc(pt[:, Q0:Q0 + 256], 2, 1)
                    k2_ = bc(pt[:, K0:K0 + 256], 2, 1)
                    for e, s_, sc in ((eb, q2, 64.0 ** -0.5), (en, k2_, 1.0), (es, k2_, 1.0)):
                        e3 = e.rearrange("p (d n) -> p d n", d=2)
                        ins = stt(e3, s_, sc, e3, ALU.mult, ALU.mult)
                    give(ins, "exps_mul")
                    out = take_d()
                    give(V.tensor_copy(qdT[:, t, :, :], out[:, :].rearrange("p (q n) -> p q n", q=4)), "d_free")
                    out = take_s()
                    for r in range(2):
                        for d in range(2):
                            ins = V.copy_predicated(
                                attT[:, r, d, :, :], bc(cum[d].bitcast(U32), 2, 1),
                                out[:, r, 256 * d:256 * d + 256].rearrange("p (q n) -> p q n", q=2))
                    give(ins, "s_free")
                    out = take_s()
                    for c in range(2):
                        ins = V.tensor_copy(upd[:, 2 * t + c, :, :], out[:, c, :].rearrange("p (d n) -> p d n", d=2))
                    give(ins, "s_free")
                    out = take_d()
                    give(V.tensor_copy(pt[:, 0:512], out[:, :]), "d_free")
                me.after("a_free", marks["gla_tiles"]["a_full"])
                cur = [s.rearrange("p (d n) -> p d n", d=2) for s in scan_cur]
                for part, chunks in (("context", (0, 1)), ("latent", tuple(range(2, 10)))):
                    if part == "context":
                        link(V.memset(scan_cur[0], 0.0))
                    else:
                        dve.wait_ge(sem["s_in_in"], 32)
                        link(V.tensor_copy(cur[0], s_in[:, :, :]))
                    for i in range(len(chunks)):
                        a_, b_ = cur[i % 2], cur[(i + 1) % 2]
                        for d in range(2):
                            c = chunks[i] if d == 0 else chunks[-1 - i]
                            for q in range(2):
                                nq = slice(P * q, P * (q + 1))
                                link(stt(b_[:, d, nq], a_[:, d, nq], decay[:, c // 2, d, q, c % 2:c % 2 + 1],
                                         upd[:, c, d, nq], ALU.mult, ALU.add))
                            ins = V.tensor_copy(upd[:, c, d, :], a_[:, d, :])
                            if i + 1 < len(chunks) or d == 0 or part == "context":
                                link(ins)
                    if part == "context":
                        give(V.tensor_copy(s_out, cur[0]), "ctx_state")
                give(ins, "s_ready")
                for t in range(NT):
                    o = pe_[:, t, 0:512]
                    out = take_s()
                    for r in range(2):
                        o_r = o.rearrange("p (q r n) -> p q r n", q=2, r=2)[:, :, r, :]
                        ins = tt(o_r, o_r, out[:, r, 0:256].rearrange("p (q n) -> p q n", q=2), ALU.add)
                    give(ins, "s_free")
                    o4 = o.rearrange("p (h n) -> p h n", h=4)
                    link(tt(sq5, o, o, ALU.mult))
                    link(V.tensor_reduce(stat[:, 8:12], sq5.rearrange("p (h n) -> p h n", h=4), AX.X, ALU.add))
                    rstd(stat[:, 8:12], P)
                    link(tt(o4, o4, bc(stat[:, 8:12], P, 2), ALU.mult))
                    give(tt(o, o, pe_[:, t, R0:R0 + 512], ALU.mult), "oa_ready")

            def rope_into(dst, src, t, heads):
                cos, sin = rope[:, t - 1, 0, :], rope[:, t - 1, 1, :]
                tmp = sq10[:, 0:64 * heads] if layer[0] == 0 else sqo[:, 0:64 * heads]
                s5 = src.rearrange("p h (a b n) -> p h a b n", a=2, b=2)
                t5 = tmp.rearrange("p (h a b n) -> p h a b n", h=heads, a=2, b=2)
                n4 = sin.rearrange("p (a b n) -> p a b n", a=2, b=2)
                for b in range(2):
                    if heads == 1:
                        link(tt(t5[:, 0, :, b, :], s5[:, 0, :, 1 - b, :], n4[:, :, b, :], ALU.mult))
                    else:
                        link(tt(t5[:, :, :, b, :], s5[:, :, :, 1 - b, :], bc(n4[:, :, b, :], heads, 1), ALU.mult))
                t3 = tmp.rearrange("p (h n) -> p h n", h=heads)
                link(tt(dst, src, bc(cos, heads, 1), ALU.mult))
                link(tt(dst, dst, t3, ALU.add))

            def latent(src, gain):
                link(V.tensor_tensor_reduce(sq10[:, 0:256], src, src, 1.0, 0.0, ALU.mult, ALU.add, stat[:, 16:17]))
                rstd(stat[:, 16:17], 256)
                give(stt(src, src, stat[:, 16:17], gain, ALU.mult, ALU.mult), "ckv_ready")

            def copy_ckvT():
                out = take_d()
                give(V.tensor_copy(ckvT, out[:, 0:256]), "d_free")

            def mla():
                me.after("a_full", marks["oa"]["a_full"])
                g_kn = vecs[:, S_KN:S_KN + P]
                g_qn = vecs[:, S_QN:S_QN + P]
                qk3 = qk.rearrange("p (h n) -> p h n", h=NH)
                for kt in range(6):
                    if kt < NT:
                        latent(pe_[:, kt, CKV0:CKV0 + 256], vecs[:, S_CKV:S_CKV + 256])
                        kr = pe_[:, kt, KR0:KR0 + 64]
                    else:
                        dve.wait_ge(sem["ctx_in"], 32)
                        signal("ckv_ready")
                        kr = ctx_kr
                    copy_ckvT()
                    link(V.tensor_tensor_reduce(krt, kr, kr, 1.0, 0.0, ALU.mult, ALU.add, stat[:, 17:18]))
                    link(tt(krt, kr, g_kn[:, 64:128], ALU.mult))
                    if 1 <= kt < NT:
                        rope_into(krr.unsqueeze(1), krt.unsqueeze(1), kt, 1)
                    else:
                        link(V.tensor_copy(krr, krt))
                    out = take_d()
                    give(V.tensor_copy(qk3[:, :, 0:64], out[:, :].rearrange("p (h n) -> p h n", h=NH)), "d_free")
                    s3 = sq10[:, 0:512].rearrange("p (h n) -> p h n", h=NH)
                    link(tt(s3, qk3[:, :, 0:64], qk3[:, :, 0:64], ALU.mult))
                    link(V.tensor_reduce(stat[:, 24:32], s3, AX.X, ALU.add))
                    link(ts(stat[:, 24:32], stat[:, 24:32], stat[:, 17:18], None, ALU.add))
                    rstd(stat[:, 24:32], P)
                    r3 = bc(stat[:, 24:32], 64, 2)
                    link(tt(qk3[:, :, 0:64], qk3[:, :, 0:64], bc(g_kn[:, 0:64], NH, 1), ALU.mult))
                    link(tt(qk3[:, :, 0:64], qk3[:, :, 0:64], r3, ALU.mult))
                    give(tt(qk3[:, :, 64:128], bc(krr, NH, 1), r3, ALU.mult), "k_ready")
                for qt in range(NT):
                    latent(pe_[:, qt, CQ0:CQ0 + 256], vecs[:, S_CQ:S_CQ + 256])
                    copy_ckvT()
                    for g in range(2):
                        out = take_d()
                        give(V.tensor_copy(qk[:, 512 * g:512 * g + 512], out[:, :]), "d_free")
                    s3 = sq10.rearrange("p (h n) -> p h n", h=NH)
                    link(tt(s3, qk3, qk3, ALU.mult))
                    link(V.tensor_reduce(stat[:, 24:32], s3, AX.X, ALU.add))
                    rstd(stat[:, 24:32], P)
                    link(tt(qk3, qk3, bc(g_qn, NH, 1), ALU.mult))
                    ins = tt(qk3, qk3, bc(stat[:, 24:32], P, 2), ALU.mult)
                    if qt:
                        link(ins)
                        rope_into(qk3[:, :, 64:128], qk3[:, :, 64:128], qt, NH)
                        signal("q_ready")
                    else:
                        give(ins, "q_ready")
                    n = P if qt == 0 else 5 * P

                    def biggest(h):
                        out = take_s().rearrange("p a b -> p (a b)")
                        link(V.tensor_reduce(stat[:, 32 + h:33 + h], out[:, 0:n], AX.X, ALU.max))
                        give(ts(stat[:, 32 + h:33 + h], stat[:, 32 + h:33 + h], -MLA_SCALE, None, ALU.mult), "m_ready")

                    biggest(0)
                    for h in range(NH):
                        if h + 1 < NH:
                            biggest(h + 1)
                        finish_head(h, pT[:, h % 2, :], min(n, 512), att_o)

            def finish_head(h, pT_b, n, dst):
                dve.wait_ge(*me.due("p_ready"))
                if layer[0] == 0:
                    signal("s_free")
                out = take_d()
                give(V.tensor_copy(pT_b[:, 0:n], out[:, 0:n]), "d_free")
                link(V.reciprocal(stat[:, 48 + h % 2:49 + h % 2], sums[:, h:h + 1]))
                out = take_d()
                give(ts(dst[:, 64 * h:64 * h + 64], out[:, 0:64], stat[:, 48 + h % 2:49 + h % 2], None, ALU.mult),
                     "d_free")

            def head_norm(buf3, gain, heads, t, at):
                s3 = sqo[:, 0:64 * heads].rearrange("p (h n) -> p h n", h=heads)
                link(tt(s3, buf3, buf3, ALU.mult))
                link(V.tensor_reduce(stat[:, at:at + heads], s3, AX.X, ALU.add))
                rstd(stat[:, at:at + heads], 64)
                link(tt(buf3, buf3, bc(gain, heads, 1), ALU.mult))
                link(tt(buf3, buf3, bc(stat[:, at:at + heads], 64, 2), ALU.mult))
                if t:
                    rope_into(buf3, buf3, t, heads)

            def odd():
                for g in range(4):
                    out = take_d()
                    give(V.tensor_copy(yT[:, g % 2, 0:P], out[:, 0:P]), "d_free")
                    out = take_d()
                    give(V.tensor_copy(yT[:, g % 2, P:T], out[:, :]), "d_free")
                for kt in range(6):
                    if kt < NT:
                        k = po_[:, kt, KD0:KD0 + P]
                        k3 = k.rearrange("p (v n) -> p v n", v=2)
                        head_norm(k3, vecs[:, S_WKN:S_WKN + 64], 2, kt, 24)
                    else:
                        dve.wait_ge(sem["kvctx_in"], 32)
                        k3 = kctx.rearrange("p (v n) -> p v n", v=2)
                    if kt:
                        me.after("a_full", marks[("odd_k", kt - 1)]["a_full"])
                    k24 = k2.rearrange("p (v r n) -> p v r n", v=2, r=2)
                    give(V.tensor_copy(k24, bc(k3, 2, 2)), "k_ready")
                sink = vecs[:, S_SINK:S_SINK + NH]
                for qt in range(NT):
                    if qt == 0:
                        me.after("a_full", marks[("odd_k", 5)]["a_full"])
                    qn3 = qn.rearrange("p (h n) -> p h n", h=NH)
                    link(V.tensor_copy(qn, po_[:, qt, QD0:QD0 + 512]))
                    head_norm(qn3, vecs[:, S_WQN:S_WQN + 64], NH, qt, 24)
                    signal("q_ready")
                    tiles = window_tiles(qt)
                    n = P * len(tiles)
                    if qt == 0 or qt == 4:
                        parts = [(0, P, P)] if qt == 0 else [(0, 2 * P, 0), (2 * P, P, P)]
                    else:
                        parts = [(0, n, P if qt == 1 else 0)]

                    def biggest(h):
                        out = take_s().rearrange("p a b -> p (a b)")
                        s_ = soft_s[:, h % 2, :]
                        for i, (at, w, m_at) in enumerate(parts):
                            ins = stt(s_[:, at:at + w], out[:, at:at + w], WIN_SCALE, wmask[:, m_at:m_at + w],
                                      ALU.mult, ALU.add)
                            if i + 1 < len(parts):
                                link(ins)
                        give(ins, "s_free")
                        link(V.tensor_reduce(stat[:, 32 + h:33 + h], s_[:, 0:n], AX.X, ALU.max))
                        give(ts(stat[:, 32 + h:33 + h], stat[:, 32 + h:33 + h], sink[:, h:h + 1], -1.0,
                                ALU.max, ALU.mult), "m_ready")

                    biggest(0)
                    for h in range(NH):
                        if h + 1 < NH:
                            biggest(h + 1)
                        dve.wait_ge(*me.due("es_ready"))
                        link(tt(sums[:, h:h + 1], sums[:, h:h + 1], sinks[:, h:h + 1], ALU.add))
                        finish_head(h, pT2[:, h % 2, :], n, att_o2)

            def out_project(l):
                me.after("out_cache", 32 * (l + 1))
                for n in range(2):
                    for t in range(NT):
                        out = take_d()
                        g = gate[:, 0, int(t > 0), 512 * n:512 * n + 512]
                        tmp = arena[:, 8192:8704]
                        give(tt(tmp, out[:, :], g, ALU.mult), "d_free")
                        xs = x[:, t, 512 * n:512 * n + 512]
                        ins = tt(xs, xs, tmp, ALU.add)
                        if n == 0 or t < NT - 1:
                            link(ins)
                give(ins, "x_done")

            def sixteen(values, cut, idx_out, val_out):
                v8, i8 = val_out, tmp_i[:, :]
                link(V.max(v8[:, 0:8], values))
                link(V.max_index(i8[:, 0:8], v8[:, 0:8], values))
                link(V.match_replace(cut, v8[:, 0:8], values, LOWEST))
                link(V.max(v8[:, 8:16], cut))
                link(V.max_index(i8[:, 8:16], v8[:, 8:16], cut))
                link(V.tensor_copy(idx_out, i8))

            def route(l):
                fin_p3 = fin_p.bitcast(U32).rearrange("p (t h k) -> p t h k", t=NT, h=NH)
                for g in range(16):
                    h, c = g // 2, g % 2
                    out = take_s()
                    for t in range(NT):
                        sixteen(out[:, t // 4, P * (t % 4):P * (t % 4 + 1)], sc_cut, top_i5[:, t, h, c, :],
                                top_v5[:, t, h, c, :])
                    signal("s_free")
                    if c:
                        for t in range(NT):
                            cand3 = cand.rearrange("p (i j) -> p i j", i=TOPK)
                            link(tt(cand3, bc(top_v5[:, t, h, 0, :], TOPK, 2), bc(top_v5[:, t, h, 1, :], TOPK, 1), ALU.add))
                            sixteen(cand, cand_cut, fin_p3[:, t, h, :], fin_v4[:, t, h, :])
                fv3 = fin_v.rearrange("p (g k) -> p g k", k=TOPK)
                link(V.tensor_copy(sums40, fv3[:, :, 0]))
                give(tt(fv3, fv3, bc(sums40, TOPK, 2), ALU.subtract), "gate_in")
                dve.wait_ge(*me.due("gate_exp"))
                link(V.tensor_reduce(sums40, fv3, AX.X, ALU.add))
                link(V.reciprocal(sums40, sums40))
                link(tt(pick3[:, 2, :, :].rearrange("p t (h k) -> p (t h) k", h=NH), fv3, bc(sums40, TOPK, 2), ALU.mult))
                pa = posab[:, 0:640].bitcast(U32)
                pb = posab[:, 640:1280].bitcast(U32)
                link(ts(pa, fin_p.bitcast(U32), 4, None, ALU.logical_shift_right))
                link(ts(pb, fin_p.bitcast(U32), 15, None, ALU.bitwise_and))
                pos_f = qsT.rearrange("p b t -> p (b t)")
                link(V.tensor_copy(pos_f[:, 0:640], pa))
                link(V.tensor_copy(pos_f[:, 640:1280], pb))
                hot3 = hot.rearrange("p (n k) -> p n k", k=TOPK)
                hot4 = hot.rearrange("p (h n k) -> p h n k", h=NH, k=TOPK)
                for t in range(NT):
                    for c in range(2):
                        pos = pos_f[:, 640 * c + P * t:640 * c + P * (t + 1)]
                        link(tt(hot3, bc(pos, TOPK, 2), bc(iota[:, 0:TOPK], P, 1), ALU.is_equal))
                        link(tt(hot4, hot4, bc(top_i5[:, t, :, c, :], TOPK, 2), ALU.mult))
                        ins = V.tensor_reduce(pick3[:, c, t, :], hot3, AX.X, ALU.add)
                        if c == 0:
                            link(ins)
                    give(ins, "pick_ready")
                for t in range(NT):
                    out = take_d()
                    give(V.tensor_copy(pickT[:, :, P * t:P * (t + 1)],
                                       out[:, 0:3 * P].rearrange("p (k n) -> p k n", k=3)), "d_free")

            def routing_matrix(l):
                jobs = TB // 4
                per = 2
                base = total["chain_v"]
                hot0 = l * NB * jobs
                with dve.Fori(0, NB // 2) as i:
                    for b in range(2):
                        ts(cols[:, b, :, :], pickT[:, :, bass.ds(i * (2 * TB) + b * TB, TB)], 1.0, None,
                           ALU.mult).then_inc(sem["chain_v"], 1)
                        dve.wait_ge(sem["chain_v"], i * per + (base + b + 1))
                        for n in range(jobs):
                            m = b * jobs + n
                            dve.wait_ge(sem["g_full"], i * (2 * jobs) + (hot0 + m + 1))
                            for q in range(4):
                                t = 4 * n + q
                                ts(hot_i[:, m % 2, q, :], iota, cols[:, b, 0, t:t + 1], cols[:, b, 2, t:t + 1],
                                   ALU.is_equal, ALU.mult)
                                ins = ts(hot_j[:, m % 2, q, :], iota, cols[:, b, 1, t:t + 1], None, ALU.is_equal)
                            ins.then_inc(sem["hot_ready"], 1)
                        dve.wait_ge(sem["hot_ready"], i * (2 * jobs) + (hot0 + (b + 1) * jobs))
                total["chain_v"] = base + per * (NB // 2)

            def dense(l):
                H0, O0 = l * 8 * NG, l * 10 * NG
                for b in range(2):
                    dve.wait_ge(sem[f"stage_out{b}"], 16 + 16 * (l + 1) * NB // 2)
                link(V.memset(acc.rearrange("p t d -> p (t d)"), 0.0))

                def weight(b, base, g):
                    dve.wait_ge(sem[f"g_in{b}"], 16 * (l * (NG // 2) + 1) + g * 16)
                    for m in range(2 * GROUP):
                        j, half = m // 2, m % 2
                        lo, n = ((0, 12), (12, 8))[half]
                        dve.wait_ge(sem["gelu_done"], base + (m + 5))
                        part = act_[:, b, j, TB * lo:TB * (lo + n)].rearrange("p (k t) -> p k t", t=TB)
                        tt(part, part, gmat[:, b, lo:lo + n, j, :], ALU.mult).then_inc(sem["act_ready"], 1)

                def add(b, base):
                    for m in range(2 * NT):
                        t, half = m // 2, m % 2
                        dve.wait_ge(sem["o_free"], base + (m + 4))
                        dve.wait_ge(sem["o_full"], base + (m + 2))
                        part = acc[:, t, 512 * half:512 * half + 512]
                        tt(part, part, bank[(2 * (b % 2) + m) % 4][:, :], ALU.add).then_inc(sem["o_free"], 1)

                weight(0, H0, 0)
                with dve.Fori(0, NG // 2 - 1) as i:
                    weight(1, i * 16 + (H0 + 8), i)
                    add(0, i * 20 + O0)
                    weight(0, i * 16 + (H0 + 16), i + 1)
                    add(1, i * 20 + (O0 + 10))
                i = NG // 2 - 1
                weight(1, i * 16 + (H0 + 8), i)
                add(0, i * 20 + O0)
                add(1, i * 20 + (O0 + 10))
                dve.wait_ge(sem["o_free"], 4 + O0 + 10 * NG)
                for t in range(NT):
                    link(tt(acc[:, t, :], acc[:, t, :], gate[:, 1, int(t > 0), :], ALU.mult))
                    ins = tt(x[:, t, :], x[:, t, :], acc[:, t, :], ALU.add)
                    if t < NT - 1:
                        link(ins)
                give(ins, "x_done")

            layer = [0]
            dve.wait_ge(sem["const_in"], 32)
            dve.wait_ge(sem["x_in"], 16)
            dve.sem_inc(sem["o_free"], 4)
            for l in range(LAYERS):
                layer[0] = l
                ada(l)
                norm(l, 0)
                if l == 0:
                    project(EVEN_CHUNKS, pe_)
                    gla()
                    mla()
                else:
                    project(ODD_CHUNKS, po_)
                    odd()
                out_project(l)
                norm(l, 1)
                route(l)
                routing_matrix(l)
                dense(l)


def constants():
    c = np.zeros((P, C_N), np.float32)
    i = np.arange(P)
    c[:, C_ID:C_ID + P] = np.eye(P)
    c[:, C_IOTA:C_IOTA + P] = i
    same = (i[:, None] // 64) == (i[None, :] // 64)
    c[:, C_CUM:C_CUM + P] = same & (i[:, None] <= i[None, :])
    c[:, C_CUM + P:C_CUM + 2 * P] = same & (i[:, None] >= i[None, :])
    c[:, C_REST:C_REST + P] = same & (i[:, None] > i[None, :])
    c[:, C_REST + P:C_REST + 2 * P] = same & (i[:, None] < i[None, :])
    c[:64, C_IND] = 1
    c[64:, C_IND + 1] = 1
    c[0, C_SEL:C_SEL + P] = 1
    c[1, C_SEL + P:C_SEL + 2 * P] = 1
    c[:, C_ONE:C_ONE + 2] = 1
    inv = np.float32(10000.0) ** (-np.arange(16, dtype=np.float32) / np.float32(16))
    pos = np.arange(512)
    ar = (pos // GRID_W).astype(np.float32)[:, None] * inv
    ac = (pos % GRID_W).astype(np.float32)[:, None] * inv
    ang = np.concatenate([ar, ar, ac, ac], -1).astype(np.float32)
    sign = np.tile(np.repeat(np.array([-1.0, 1.0], np.float32), 16), 2)
    table = np.stack([np.cos(ang), np.sin(ang) * sign], 1).reshape(4, P, 2, 64).transpose(1, 0, 2, 3)
    c[:, C_ROPE:C_ROPE + 512] = table.reshape(P, 512)
    c[:, C_MASK:C_MASK + P] = np.where(i[None, :] >= i[:, None], 0.0, -1e30)
    c[:, C_MASK + 2 * P:C_MASK + 3 * P] = np.where(i[None, :] <= i[:, None], 0.0, -1e30)
    return c


def pool_bands():
    def full(n, w):
        t = np.arange(n)
        lo, hi = np.clip(t - w // 2, 0, n), np.clip(t - w // 2 + w, 0, n)
        m = (t[:, None] >= lo[None, :]) & (t[:, None] < hi[None, :])
        return m / (hi - lo)[None, :].astype(np.float32) - np.eye(n)
    out = np.zeros((P, 4, 6, P), np.float32)
    for g, w in enumerate(WINDOWS):
        out[:, g, 0] = full(P, w)
        m = full(4 * P, w)
        out[:, g, 1] = m[0:P, 0:P]
        out[:, g, 2] = m[P:2 * P, P:2 * P]
        out[:, g, 3] = m[3 * P:, 3 * P:]
        out[:, g, 4] = m[0:P, P:2 * P]
        out[:, g, 5] = m[2 * P:3 * P, P:2 * P]
    return out.reshape(P, 4 * 6 * P)


def slabs(w):
    k, n = w.shape
    return w.reshape(k // P, P, n).transpose(1, 0, 2).reshape(P, -1)


def kernel(**inputs):
    import concourse.bacc as bacc
    from concourse.bass_utils import run_bass_kernel_spmd

    v = {k: np.asarray(x) for k, x in inputs.items()}
    cat, rows = np.concatenate, lambda g: np.broadcast_to(g[None, :], (P, g.shape[0]))
    w_even = v["w_in_even"][0]
    order = [w_even[:, 0:1536], w_even[:, 1568:2080], w_even[:, 1536:1568], w_even[:, 2080:2144]]
    w_even = cat(order, 1)
    w_gu = np.zeros((33, 512), np.float32)
    w_gu[0:16, 0:256] = v["w_gate_up"][0, 0]
    w_gu[16:32, 256:512] = v["w_gate_up"][0, 1]
    w_gu[32] = v["b_gate_up"][0].reshape(-1)
    cond = np.stack([v["c_ctx"], v["c"][0]], 1).reshape(KD, P, 2).transpose(1, 0, 2).reshape(P, 16)
    vecs = cat([
        cond, v["g_norm"].reshape(LAYERS * 2 * KD, P).T, rows(v["g_mla_ckv"][0]), rows(v["g_mla_cq"][0]),
        rows(v["g_mla_qn"][0]), rows(v["g_mla_kn"][0]), v["g_gla_out"][0][:, None], rows(v["g_win_qn"][0]),
        rows(v["g_win_kn"][0]), rows(v["win_sink"][0]), v["pool_scale"][0].reshape(4, P).T], 1)
    assert vecs.shape[1] == S_N
    ins = {
        "const": constants(),
        "vecs": vecs,
        "x": cat([v["x_prompt"][0], v["x_sample"][0]], 0),
        "w_gu": w_gu,
        "state_in": v["state_gla"][0, 0].reshape(2, 2, 2, 64, P).transpose(3, 0, 2, 1, 4),
        "ctx_ckv": v["cache_mla_ckv"][0, 0],
        "ctx_kr": v["cache_mla_krope"][0, 0],
        "k_ctx": v["cache_win_kv"][0, 0, 0].reshape(P, P),
        "v_ctx": v["cache_win_kv"][0, 0, 1].reshape(P, P),
        "w_ada": v["w_ada"].reshape(LAYERS, KD, P, 12, 512).transpose(0, 3, 2, 1, 4).reshape(LAYERS, 12, P, 4096),
        "b_ada": v["b_ada"].reshape(LAYERS, 12, 1, 512),
        "w_mla": cat([slabs(v["w_mla_uq"][0]), slabs(v["w_mla_uk"][0]), slabs(v["w_mla_uv"][0])], 1),
        "w_band": cat([pool_bands(), v["w_pool"][0].transpose(1, 0, 2).reshape(P, 512)], 1),
        "w_out0": np.stack([slabs(v["w_out_even"][0][:, 512 * n:512 * n + 512]) for n in range(2)]),
        "w_out1": np.stack([slabs(v["w_out_odd"][0][:, 512 * n:512 * n + 512]) for n in range(2)]),
        "peer_wq": v["peer_wq"].reshape(LAYERS, KD, P, 4, 512).transpose(0, 3, 2, 1, 4).reshape(LAYERS, 4, P, 4096),
        "subkeys": v["peer_subkeys"].reshape(LAYERS, 16, NEXP, P).transpose(0, 3, 1, 2).reshape(LAYERS, P, 2048),
        "peer_u": v["peer_u"].reshape(LAYERS, NEXP, NG, GROUP, KD, P).transpose(0, 2, 5, 3, 4, 1)
                             .reshape(LAYERS, NG, P, 4096),
        "peer_v": v["peer_v"].reshape(LAYERS, NEXP, NG, GROUP * D).transpose(0, 2, 1, 3),
    }
    for n, (at, w) in enumerate(EVEN_CHUNKS):
        ins[f"w_in0_{n}"] = slabs(w_even[:, at:at + w])
    for n, (at, w) in enumerate(ODD_CHUNKS):
        ins[f"w_in1_{n}"] = slabs(v["w_in_odd"][0][:, at:at + w])
    ins = {k: np.ascontiguousarray(x) for k, x in ins.items()}
    outs = {"y_prompt": (P, D), "y_sample": (512, D), "state": (2, 4, 64, P), "ckv": (P, 256), "kr": (P, 64),
            "win": (2, P, P)}
    nc = bacc.Bacc("TRN2", target_bir_lowering=False, num_devices=1)
    aps = {k: nc.dram_tensor(f"in_{k}", x.shape, F32, kind="ExternalInput").ap() for k, x in ins.items()}
    aps |= {k: nc.dram_tensor(f"out_{k}", s, F32, kind="ExternalOutput").ap() for k, s in outs.items()}
    build_program(nc, aps)
    r = run_bass_kernel_spmd(nc, [{f"in_{k}": x for k, x in ins.items()}], core_ids=[0]).results[0]
    return (r["out_y_prompt"].reshape(1, P, D), r["out_y_sample"].reshape(1, 512, D),
            r["out_state"].reshape(1, 1, 2, 4, 64, P), r["out_ckv"].reshape(1, 1, P, 256),
            r["out_kr"].reshape(1, 1, P, 64), r["out_win"].reshape(1, 1, 2, P, 2, 64))
```

```python
from contextlib import ExitStack

import numpy as np

import concourse.bass as bass
from concourse import mybir

F32 = mybir.dt.float32
U32 = mybir.dt.uint32
F32R = mybir.dt.float32r
ACT = mybir.ActivationFunctionType
ALU = mybir.AluOpType
AX = mybir.AxisListType

P = 128
D = 1024
KD = D // P
NT = 5
T = NT * P
EPS = 1e-6
LAYERS = 2
NH = 8
TOPK = 16
NEXP = 128
GROUP = 2
NG = NEXP // GROUP
RGROUP = 2 * GROUP
NR = NEXP // RGROUP
G_AHEAD = 12
HALVES = ((0, 384), (384, 256))
TB = 32
NB = T // TB
GRID_W = 64
WINDOWS = (2, 4, 8, 16)
LOWEST = -3.0e38
MLA_SCALE = 128.0 ** -0.5
WIN_SCALE = 64.0 ** -0.5

Q0, K0, V0, R0, CQ0, CKV0, GL0, KR0, EVEN_W = 0, 256, 512, 1024, 1536, 1792, 2048, 2080, 2144
EVEN_CHUNKS = [(0, 512), (512, 512), (1024, 512), (1536, 512), (2048, 96)]
XC0, QD0, KD0, VD0, ODD_W = 0, 512, 1024, 1152, 1280
ODD_CHUNKS = [(0, 512), (512, 512), (1024, 256)]

C_ID, C_IOTA, C_CUM, C_REST, C_IND, C_SEL, C_ROPE, C_MASK = 0, 128, 256, 512, 768, 770, 1026, 1538
C_ONE = 2050
C_N = 2052
(S_C, S_GN, S_CKV, S_CQ, S_QN, S_KN, S_GO, S_WQN, S_WKN, S_SINK, S_PS) = (
    0, 16, 48, 304, 560, 688, 816, 817, 881, 945, 953)
S_N = 957


def build_program(nc, a):
    ctx = ExitStack()
    with ctx:
        def sb(name, shape, dt=F32):
            return ctx.enter_context(nc.sbuf_tensor(name, shape, dt))

        def R(ap):
            return ap.bitcast(F32R)

        start = {}

        def at_known_place(name, shape):
            t = sb(name, shape)
            start[name] = nc.sbuf_base - 4 * int(np.prod(shape[1:]))
            return t

        def rounded(name, shape, within, word):
            return nc.alloc_sbuf_tensor_at(name, shape, F32, offset=start[within] + 4 * word)

        const = sb("const", [P, C_N])
        vecs = sb("vecs", [P, S_N])
        x = sb("x", [P, NT, D])
        hT = at_known_place("hT", [P, KD, T])
        gate = at_known_place("gate", [P, 2, 2, D])
        ring = at_known_place("ring", [P, 4, 4096])
        arena = at_known_place("arena", [P, 16384])
        silu_c = sb("silu_c", [P, KD, 2])
        ada_col = sb("ada_col", [P, 2, 2, KD, 2])
        mod = sb("mod", [P, 2, KD, 2])
        stat = sb("stat", [P, 64])
        sums = sb("sums", [P, NH])
        sinks = sb("sinks", [P, NH])
        sums40 = sb("sums40", [P, NT * NH])[:, :]
        tmp_i = sb("tmp_i", [P, TOPK], U32)
        bank = [ctx.enter_context(nc.psum_tensor(f"bank{i}", [P, 512], F32)) for i in range(4)]
        pair = ctx.enter_context(nc.psum_tensor("pair", [P, 4, 512], F32))

        ident = const[:, C_ID:C_ID + P]
        iota = const[:, C_IOTA:C_IOTA + P]
        cum = [const[:, C_CUM + P * i:C_CUM + P * (i + 1)] for i in range(2)]
        rest = [const[:, C_REST + P * i:C_REST + P * (i + 1)] for i in range(2)]
        ind = const[:, C_IND:C_IND + 2]
        rope = const[:, C_ROPE:C_ROPE + 512].rearrange("p (t s d) -> p t s d", t=4, s=2)
        wmask = const[:, C_MASK:C_MASK + 512]

        def views(base, *sizes):
            out, at = [], base
            for n in sizes:
                out.append(arena[:, at:at + n])
                at += n
            assert at <= 16384
            return out

        bias_rows, ada_rows = views(12288, 1024, 1024)
        xn0, xn1, junk = views(8192, 1024, 1024, 1024)
        pe_ = arena[:, 0:NT * EVEN_W].rearrange("p (t n) -> p t n", t=NT)
        (la, eb, en, es, kiT, attT, glT, sq5, wgu) = views(
            NT * EVEN_W, 512, 512, 512, 512, 512, 1024, 128, 512, 512)
        attT = attT.rearrange("p (r d q n) -> p r d q n", r=2, d=2, q=2)
        scan_cur = views(NT * EVEN_W + 2560, 512, 512)
        s_out = es.rearrange("p (d n) -> p d n", d=2)
        spare = ring[:, 2:4, :].rearrange("p a b -> p (a b)")
        upd = spare[:, 0:5120].rearrange("p (c d n) -> p c d n", c=10, d=2)
        qdT = spare[:, 5120:7680].rearrange("p (t q n) -> p t q n", t=NT, q=4)
        s_in = spare[:, 7680:8192].rearrange("p (d n) -> p d n", d=2)
        decay = sb("decay", [P, NT, 2, 2, 2])
        kT = spare[:, 0:6144].rearrange("p (h n) -> p h n", h=NH)
        probs = spare[:, 6144:7424].rearrange("p (b n) -> p b n", b=2)
        ckvT = spare[:, 7424:7680]
        ctx_ckv = spare[:, 7680:7936]
        ctx_kr = spare[:, 7936:8000]
        krr = spare[:, 8000:8064]
        krt = spare[:, 8064:8128]
        vals, qk, qT, att_o = views(NT * EVEN_W, 6 * 512, 1024, 1024, 512)
        vals = vals.rearrange("p (t n) -> p t n", t=6)
        sq10 = arena[:, 0:1024]
        pT = arena[:, EVEN_W:EVEN_W + 1280].rearrange("p (b n) -> p b n", b=2)
        po_ = arena[:, 0:NT * ODD_W].rearrange("p (t n) -> p t n", t=NT)
        (yT, kT2, k2, qn, qT2, soft_s, probs2, pT2, kctx, vctx, sqo, att_o2) = views(
            NT * ODD_W, 1280, 1536, 256, 512, 512, 1024, 1024, 1024, 128, 128, 512, 512)
        yT = yT.rearrange("p (b n) -> p b n", b=2)
        kT2 = kT2.rearrange("p (v n) -> p v n", v=2)
        soft_s = soft_s.rearrange("p (b n) -> p b n", b=2)
        probs2 = probs2.rearrange("p (b n) -> p b n", b=2)
        pT2 = pT2.rearrange("p (b n) -> p b n", b=2)
        (pickT, top_v, top_i, subk, qsT, sc_cut, cand, cand_cut, fin_v, fin_p, hot, pick, posab) = views(
            0, 3 * T, 1280, 1280, 2048, 1280, P, 256, 256, 640, 640, 2048, 1920, 1280)
        pickT = pickT.rearrange("p (k t) -> p k t", k=3)
        top_v5 = top_v.rearrange("p (t h c k) -> p t h c k", t=NT, h=NH, c=2)
        top_i5 = top_i.rearrange("p (t h c k) -> p t h c k", t=NT, h=NH, c=2)
        subk = subk.rearrange("p (g n) -> p g n", g=16)
        qsT = qsT.rearrange("p (b t) -> p b t", b=2)
        fin_v4 = fin_v.rearrange("p (t h k) -> p t h k", t=NT, h=NH)
        pick3 = pick.rearrange("p (w t n) -> p w t n", w=3, t=NT)
        (stage, hots, cols) = views(1920, 8192, 4096, 192)
        stage = stage.rearrange("p (b j t) -> p b j t", b=2, j=P)
        hots = hots.rearrange("p (b c q n) -> p b c q n", b=4, c=2, q=4)
        cols = cols.rearrange("p (b k t) -> p b k t", b=2, k=3)
        acc, _, _, gmat = views(0, NT * D, KD * T, 2 * GROUP * T, RGROUP * T)
        acc = acc.rearrange("p (t d) -> p t d", t=NT)
        h_hi = rounded("h_hi", [P, KD, T], "arena", NT * D)
        h_lo = rounded("h_lo", [P, KD, T], "hT", 0)
        act_hi = [rounded(f"act_hi{b}", [P, GROUP, T], "arena", NT * D + KD * T + GROUP * T * b) for b in range(2)]
        act_raw = [gate[:, 0].rearrange("p c d -> p (c d)")[:, 0:GROUP * T].rearrange("p (j t) -> p j t", j=GROUP),
                   at_known_place("act_raw1", [P, GROUP, T])]
        act_lo = [rounded("act_lo0", [P, GROUP, T], "gate", 0), rounded("act_lo1", [P, GROUP, T], "act_raw1", 0)]
        gmat = gmat.rearrange("p (k j t) -> p k j t", k=NB, j=RGROUP)
        u_raw = [ring[:, 2 * b, 0:GROUP * D] for b in range(2)]
        v_raw = [ring[:, 2 * b + 1, 0:GROUP * D] for b in range(2)]
        u_lo, u_hi = ([rounded(f"u_{part}{b}", [P, GROUP * D], "ring", 2 * b * 4096 + at) for b in range(2)]
                      for part, at in (("lo", 0), ("hi", GROUP * D)))
        v_lo, v_hi = ([rounded(f"v_{part}{b}", [P, GROUP * D], "ring", (2 * b + 1) * 4096 + at) for b in range(2)]
                      for part, at in (("lo", 0), ("hi", GROUP * D)))

        names = """
        const_in x_in bias_in0 bias_in1 slot_in0 slot_in1 wgu_in s_in_in ctx_in kvctx_in subk_in
        silu_done mods_done ss_ready var_ready std_ready xn_ready
        z_part z_exp la_ready exps_mul ctx_state s_ready oa_ready
        ckv_ready k_ready q_ready m_ready p_ready es_ready x_done
        d_full d_free a_full a_free s_full s_free
        gate_in gate_exp pick_ready cols_ready hot_ready gated_a gated_p g_full g_free stage_out0 stage_out1
        u_in0 u_in1 v_in0 v_in1 g_in h_led h_split u_led u_split v_led v_split
        h_full gelu_done act_made act_led act_ready o_full o_free
        out_state out_cache out_y chain_v chain_a
        """.split()
        sem = {n: ctx.enter_context(nc.semaphore(n)) for n in names}
        total = {}

        class Turn:

            def __init__(self, eng, chain=None):
                self.eng, self.n, self.chain = eng, {}, chain

            def next(self, name):
                self.n[name] = self.n.get(name, 0) + 1
                return self.n[name]

            def due(self, name, step=1):
                return sem[name], self.next(name) * step

            def after(self, name, k):
                if k > 0:
                    self.eng.wait_ge(sem[name], k)

            def give(self, ins, name):
                ins.then_inc(sem[name], 1)
                total[name] = total.get(name, 0) + 1
                self.eng.wait_ge(sem[name], total[name])

            def link(self, ins):
                self.give(ins, self.chain)

        def bc(ap, n, at):
            ap = ap.unsqueeze(at)
            shape = [int(s) for s in ap.shape]
            shape[at] = n
            return ap.broadcast_to(shape)

        freed = {}
        marks = {}
        items = []
        per_layer = []

        for l in range(LAYERS):
            items += [a["w_ada"][l, n] for n in range(12)]
            items += [a[f"w_in{l}_{n}"] for n in range(5 if l == 0 else 3)]
            items += [a["w_mla"] if l == 0 else a["w_band"]]
            items += [a[f"w_out{l}"][n] for n in range(2)]
            items += [a["peer_wq"][l, n] for n in range(4)]
            per_layer.append(len(items))
        routing = nc.dram_tensor("routing", (NR, P, NB, RGROUP, TB), F32, kind="Internal").ap()

        def window_tiles(qt):
            return [0] if qt == 0 else [t for t in (qt - 1, qt, qt + 1) if 1 <= t < NT] + [5]

        block = ctx.enter_context(nc.Block())

        @block.tensor
        def _(pe):
            me = Turn(pe)
            mm = nc.tensor.matmul
            tr = nc.tensor.transpose
            item = [0]

            def slot():
                n = item[0]
                item[0] += 1
                pe.wait_ge(sem[f"slot_in{n % 2}"], 16 * (n // 2 + 1))
                return ring[:, n % 2, :]

            def slot_done():
                freed[item[0] - 1] = (last_stream[0], me.n[last_stream[0]])

            def mark(name):
                marks[name] = dict(me.n)

            def copied():
                pe.wait_ge(sem["d_free"], me.n["d_full"])
                pe.wait_ge(sem["a_free"], me.n["a_full"])

            last_stream = ["d_full"]

            def open_d():
                n = me.next("d_full") - 1
                me.after("d_free", n - 1)
                last_stream[0] = "d_full"
                return bank[n % 2]

            def open_a():
                n = me.next("a_full") - 1
                me.after("a_free", n - 1)
                last_stream[0] = "a_full"
                return bank[2 + n % 2]

            def open_s():
                n = me.next("s_full") - 1
                me.after("s_free", n - 1)
                return pair[:, 2 * (n % 2):2 * (n % 2) + 2, :]

            def ada(l):
                if l == 0:
                    pe.wait_ge(*me.due("silu_done"))
                    pe.wait_ge(sem["const_in"], 32)
                else:
                    pe.wait_ge(sem["o_free"], 4 + 2 * NT * NG * l)
                for n in range(12):
                    w = slot().rearrange("p (k n) -> p k n", k=KD)
                    out = open_d()
                    for k in range(KD):
                        mm(out[0:2, :], silu_c[:, k, :], w[:, k, :], start=(k == 0), stop=False)
                    i = l * 12 + n
                    pe.wait_ge(sem[f"bias_in{i % 2}"], 16 * (i // 2 + 1))
                    mm(out[0:2, :], const[0:1, C_ONE:C_ONE + 2], bias_rows[0:1, 512 * (i % 2):512 * (i % 2) + 512],
                       start=False, stop=True).then_inc(sem["d_full"], 1)
                    slot_done()
                    pe.wait_ge(sem["d_free"], me.n["d_full"])
                    row = ada_rows[0:2, 512 * (i % 2):512 * (i % 2) + 512]
                    if n // 2 in (2, 5):
                        for c in range(2):
                            mm(open_a()[:, :], const[0:2, C_SEL + P * c:C_SEL + P * (c + 1)], row,
                               start=True, stop=True).then_inc(sem["a_full"], 1)
                    else:
                        out = open_d()
                        for k in range(4):
                            last = tr(out[:, 2 * k:2 * k + 2], row[:, P * k:P * (k + 1)], ident[0:2, 0:2])
                        last.then_inc(sem["d_full"], 1)

            def norm(l, s):
                for t in range(NT):
                    pe.wait_ge(*me.due("xn_ready"))
                    xn = (xn0, xn1)[t % 2]
                    out = open_a()
                    for k in range(4, 8):
                        last = tr(out[:, P * (k - 4):P * (k - 3)], xn[:, P * k:P * (k + 1)], ident)
                    last.then_inc(sem["a_full"], 1)
                    out = open_d()
                    for k in range(4):
                        last = tr(out[:, P * k:P * (k + 1)], xn[:, P * k:P * (k + 1)], ident)
                    last.then_inc(sem["d_full"], 1)

            def project(chunks):
                copied()
                for n, (_, w) in enumerate(chunks):
                    weights = slot()[:, 0:KD * w].rearrange("p (k n) -> p k n", k=KD)
                    for t in range(NT):
                        to_d = (n * NT + t) % 2 == 0 and n != 2
                        out = open_d() if to_d else open_a()
                        for k in range(KD):
                            last = mm(out[:, 0:w], hT[:, k, P * t:P * (t + 1)], weights[:, k, :],
                                      start=(k == 0), stop=(k == KD - 1))
                        last.then_inc(sem["d_full" if to_d else "a_full"], 1)
                    slot_done()
                mark(("proj", layer[0]))

            def gla():
                copied()
                pe.wait_ge(sem["wgu_in"], 16)
                for t in range(NT):
                    pt = pe_[:, t, :]
                    tr(open_d()[0:32, 0:P], pt[:, GL0:GL0 + 32], ident).then_inc(sem["d_full"], 1)
                    pe.wait_ge(sem["d_free"], me.n["d_full"])
                    mm(open_d()[:, :], glT[0:33, :], wgu[0:33, :], start=True, stop=True).then_inc(sem["d_full"], 1)
                    pe.wait_ge(*me.due("la_ready"))
                    for mats in (cum, rest):
                        out = open_a()
                        for d in range(2):
                            last = mm(out[:, 256 * d:256 * d + 256], mats[d], la[:, 256 * d:256 * d + 256],
                                      start=True, stop=True)
                        last.then_inc(sem["a_full"], 1)
                    out = open_a()
                    for d in range(2):
                        for q in range(2):
                            last = mm(out[:, 4 * d + 2 * q:4 * d + 2 * q + 2],
                                      la[:, 256 * d + P * q:256 * d + P * (q + 1)], ind, start=True, stop=True)
                    last.then_inc(sem["a_full"], 1)
                    mark(("exps", t))
                    pe.wait_ge(*me.due("exps_mul"))
                    for src, opened, full in ((eb, open_d, "d_full"), (en, open_a, "a_full")):
                        out = opened()
                        for q in range(4):
                            last = tr(out[:, P * q:P * (q + 1)], src[:, P * q:P * (q + 1)], ident)
                        last.then_inc(sem[full], 1)
                    copied()
                    out = open_s()
                    for r in range(2):
                        for d in range(2):
                            for q in range(2):
                                h = slice(64 * r, 64 * r + 64)
                                last = mm(out[:, r, 256 * d + P * q:256 * d + P * (q + 1)],
                                          kiT[h, P * (2 * d + q):P * (2 * d + q + 1)],
                                          qdT[h, t, 2 * d + q, :], start=True, stop=True)
                    last.then_inc(sem["s_full"], 1)
                    out = open_s()
                    for c in range(2):
                        for d in range(2):
                            for h in range(4):
                                r, q = h % 2, h // 2
                                last = mm(out[64 * r:64 * r + 64, c, 256 * d + P * q:256 * d + P * (q + 1)],
                                          es[64 * c:64 * c + 64, 256 * d + 64 * h:256 * d + 64 * h + 64],
                                          pt[64 * c:64 * c + 64, V0 + P * h:V0 + P * (h + 1)],
                                          start=True, stop=True)
                    last.then_inc(sem["s_full"], 1)
                    pe.wait_ge(sem["s_free"], me.n["s_full"] - 1)
                    out = open_d()
                    for h in range(4):
                        for d in range(2):
                            last = mm(out[:, P * h:P * (h + 1)], attT[:, h % 2, d, h // 2, :],
                                      pt[:, V0 + P * h:V0 + P * (h + 1)], start=(d == 0), stop=(d == 1))
                    last.then_inc(sem["d_full"], 1)
                mark("gla_tiles")
                pe.wait_ge(*me.due("s_ready"))
                for t in range(NT):
                    out = open_s()
                    for c in range(2):
                        for r in range(2):
                            for q in range(2):
                                for d in range(2):
                                    h = slice(64 * r, 64 * r + 64)
                                    last = mm(out[64 * c:64 * c + 64, r, P * q:P * (q + 1)],
                                              qdT[h, t, 2 * d + q, 64 * c:64 * c + 64],
                                              upd[h, 2 * t + c, d, P * q:P * (q + 1)],
                                              start=(d == 0 and q == 0), stop=(d == 1), skip_group_check=True)
                    last.then_inc(sem["s_full"], 1)
                for t in range(NT):
                    pe.wait_ge(*me.due("oa_ready"))
                    out = open_a()
                    for h in range(4):
                        last = tr(out[:, P * h:P * (h + 1)], pe_[:, t, P * h:P * (h + 1)], ident)
                    last.then_inc(sem["a_full"], 1)
                mark("oa")

            def attend(q_lhs, keys):
                out = open_s().rearrange("p a b -> p (a b)")
                for k_ap, at, n in keys:
                    last = mm(out[:, at:at + n], q_lhs, k_ap, start=(at % 512 == 0), stop=True, skip_group_check=True)
                last.then_inc(sem["s_full"], 1)

            def weigh(probs_b, pT_b, tiles, v_of):
                pe.wait_ge(*me.due("p_ready"))
                n = len(tiles)
                out = open_d()
                for i in range(min(n, 4)):
                    last = tr(out[:, P * i:P * (i + 1)], probs_b[:, P * i:P * (i + 1)], ident)
                last.then_inc(sem["d_full"], 1)
                if n > 4:
                    tr(open_a()[:, 0:P], probs_b[:, 4 * P:5 * P], ident).then_inc(sem["a_full"], 1)
                copied()
                out = open_d()
                for i, kt in enumerate(tiles):
                    last = mm(out[:, 0:64], pT_b[:, P * i:P * (i + 1)], v_of(kt), start=(i == 0), stop=(i == n - 1))
                last.then_inc(sem["d_full"], 1)

            def mla():
                w = slot()
                w_uq = w[:, 0:2048].rearrange("p (k n) -> p k n", k=2)
                w_uk = w[:, 2048:3072].rearrange("p (k n) -> p k n", k=2)
                w_uv = w[:, 3072:4096].rearrange("p (k n) -> p k n", k=2)
                for kt in range(6):
                    pe.wait_ge(*me.due("ckv_ready"))
                    ckv = pe_[:, kt, CKV0:CKV0 + 256] if kt < NT else ctx_ckv
                    out = open_d()
                    for k in range(2):
                        last = tr(out[:, P * k:P * (k + 1)], ckv[:, P * k:P * (k + 1)], ident)
                    last.then_inc(sem["d_full"], 1)
                    pe.wait_ge(sem["d_free"], me.n["d_full"])
                    for wk, opened, full in ((w_uk, open_d, "d_full"), (w_uv, open_a, "a_full")):
                        out = opened()
                        for k in range(2):
                            last = mm(out[:, :], ckvT[:, P * k:P * (k + 1)], wk[:, k, :], start=(k == 0), stop=(k == 1))
                        last.then_inc(sem[full], 1)
                    pe.wait_ge(*me.due("k_ready"))
                    for g in range(2):
                        out = open_a()
                        for i in range(4):
                            h = 4 * g + i
                            last = tr(out[:, P * i:P * (i + 1)], qk[:, P * h:P * (h + 1)], ident)
                        last.then_inc(sem["a_full"], 1)
                copied()
                for qt in range(NT):
                    pe.wait_ge(*me.due("ckv_ready"))
                    out = open_d()
                    for k in range(2):
                        last = tr(out[:, P * k:P * (k + 1)], pe_[:, qt, CQ0 + P * k:CQ0 + P * (k + 1)], ident)
                    last.then_inc(sem["d_full"], 1)
                    pe.wait_ge(sem["d_free"], me.n["d_full"])
                    for g in range(2):
                        out = open_d()
                        for k in range(2):
                            last = mm(out[:, :], ckvT[:, P * k:P * (k + 1)], w_uq[:, k, 512 * g:512 * g + 512],
                                      start=(k == 0), stop=(k == 1))
                        last.then_inc(sem["d_full"], 1)
                    if qt == NT - 1:
                        slot_done()
                    pe.wait_ge(*me.due("q_ready"))
                    for g in range(2):
                        out = open_a()
                        for i in range(4):
                            h = 4 * g + i
                            last = tr(out[:, P * i:P * (i + 1)], qk[:, P * h:P * (h + 1)], ident)
                        last.then_inc(sem["a_full"], 1)
                    copied()
                    tiles = [0] if qt == 0 else [1, 2, 3, 4, 5]
                    mark(("scores", qt))

                    def scores(h):
                        q_lhs = qT[:, P * h:P * (h + 1)]
                        if qt == 0:
                            attend(q_lhs, [(kT[:, h, 0:P], 0, P)])
                        else:
                            attend(q_lhs, [(kT[:, h, P:P + 512], 0, 512), (kT[:, h, P + 512:P + 640], 512, P)])

                    scores(0)
                    for h in range(NH):
                        if h + 1 < NH:
                            scores(h + 1)
                        weigh(probs[:, h % 2, :], pT[:, h % 2, :], tiles,
                              lambda kt, h=h: vals[:, kt, 64 * h:64 * h + 64])
                    turn_out()

            def turn_out():
                copied()
                out = open_a()
                src = att_o if layer[0] == 0 else att_o2
                for i in range(4):
                    last = tr(out[:, P * i:P * (i + 1)], src[:, P * i:P * (i + 1)], ident)
                last.then_inc(sem["a_full"], 1)

            def odd():
                copied()
                w = slot()
                band = w[:, 0:3072].rearrange("p (g b n) -> p g b n", g=4, b=6)
                w_pool = w[:, 3072:3584].rearrange("p (g n) -> p g n", g=4)
                for g in range(4):
                    xc = [po_[:, t, XC0 + P * g:XC0 + P * (g + 1)] for t in range(NT)]
                    near = {0: [(0, 0)], 1: [(1, 1), (2, 5)], 2: [(1, 4), (2, 2), (3, 5)],
                            3: [(2, 4), (3, 2), (4, 5)], 4: [(3, 4), (4, 3)]}
                    out = open_d()
                    mm(out[:, 0:P], xc[0], band[:, g, 0, :], start=True, stop=True).then_inc(sem["d_full"], 1)
                    out = open_d()
                    for t in range(1, NT):
                        for i, (u, b) in enumerate(near[t]):
                            last = mm(out[:, P * (t - 1):P * t], xc[u], band[:, g, b, :],
                                      start=(i == 0), stop=(i == len(near[t]) - 1))
                    last.then_inc(sem["d_full"], 1)
                    pe.wait_ge(sem["d_free"], me.n["d_full"])
                    for at, n in ((0, 512), (512, P)):
                        mm(open_a()[:, 0:n], w_pool[:, g, :], yT[:, g % 2, at:at + n],
                           start=True, stop=True).then_inc(sem["a_full"], 1)
                slot_done()
                for kt in range(6):
                    pe.wait_ge(*me.due("k_ready"))
                    out = open_a()
                    for v in range(2):
                        last = tr(out[:, P * v:P * (v + 1)], k2[:, P * v:P * (v + 1)], ident)
                    last.then_inc(sem["a_full"], 1)
                    mark(("odd_k", kt))
                pe.wait_ge(sem["kvctx_in"], 32)
                for qt in range(NT):
                    pe.wait_ge(*me.due("q_ready"))
                    out = open_a()
                    for i in range(4):
                        last = tr(out[:, P * i:P * (i + 1)], qn[:, P * i:P * (i + 1)], ident)
                    last.then_inc(sem["a_full"], 1)
                    copied()
                    tiles = window_tiles(qt)

                    def scores(h):
                        part = slice(64 * (h % 2), 64 * (h % 2) + 64)
                        q_lhs = qT2[part, P * (h // 2):P * (h // 2 + 1)]
                        local = [t for t in tiles if t < NT]
                        keys = [(kT2[part, h // 4, P * local[0]:P * (local[-1] + 1)], 0, P * len(local))]
                        if qt:
                            keys.append((kT2[part, h // 4, P * 5:P * 6], P * len(local), P))
                        attend(q_lhs, keys)

                    scores(0)
                    for h in range(NH):
                        if h + 1 < NH:
                            scores(h + 1)
                        weigh(probs2[:, h % 2, :], pT2[:, h % 2, :], tiles,
                              lambda kt, h=h: (po_[:, kt, VD0 + 64 * (h // 4):VD0 + 64 * (h // 4) + 64] if kt < NT
                                               else vctx[:, 64 * (h // 4):64 * (h // 4) + 64]))
                    turn_out()

            def out_project():
                copied()
                for n in range(2):
                    w = slot().rearrange("p (k n) -> p k n", k=KD)
                    for t in range(NT):
                        out = open_d()
                        for k in range(KD):
                            last = mm(out[:, :], hT[:, k, P * t:P * (t + 1)], w[:, k, :], start=(k == 0), stop=(k == KD - 1))
                        last.then_inc(sem["d_full"], 1)
                    slot_done()

            def route(l):
                copied()
                pe.wait_ge(sem["subk_in"], 16 * (l + 1))
                for g in range(16):
                    if g % 4 == 0:
                        w = slot().rearrange("p (k n) -> p k n", k=KD)
                    for at, n in ((0, 512), (512, P)):
                        out = open_a()
                        for k in range(KD):
                            last = mm(out[:, 0:n], w[:, k, P * (g % 4):P * (g % 4 + 1)], hT[:, k, at:at + n],
                                      start=(k == 0), stop=(k == KD - 1))
                        last.then_inc(sem["a_full"], 1)
                    if g % 4 == 3:
                        slot_done()
                    pe.wait_ge(sem["a_free"], me.n["a_full"])
                    out = open_s()
                    for t in range(NT):
                        last = mm(out[:, t // 4, P * (t % 4):P * (t % 4 + 1)], qsT[:, g % 2, P * t:P * (t + 1)],
                                  subk[:, g, :], start=True, stop=True)
                    last.then_inc(sem["s_full"], 1)
                for t in range(NT):
                    pe.wait_ge(*me.due("pick_ready"))
                    out = open_d()
                    for w3 in range(3):
                        last = tr(out[:, P * w3:P * (w3 + 1)], pick3[:, w3, t, :], ident)
                    last.then_inc(sem["d_full"], 1)

            def routing_matrix(l):
                jobs = TB // 4
                with pe.Fori(0, NB // 2) as i:
                    for n in range(2 * jobs):
                        at = l * (NB * jobs) + n
                        pe.wait_ge(sem["gated_a"], i * (2 * jobs) + (at + 1))
                        pe.wait_ge(sem["gated_p"], i * (2 * jobs) + (at + 1))
                        pe.wait_ge(sem["g_free"], i * (2 * jobs) + (at + G_AHEAD - 3))
                        for q in range(4):
                            last = mm(pair[:, n % 4, P * q:P * (q + 1)], hots[:, n % 4, 0, q, :], hots[:, n % 4, 1, q, :],
                                      start=True, stop=True)
                        last.then_inc(sem["g_full"], 1)

            def dense(l):
                def experts(b, n):
                    pe.wait_ge(sem["u_split"], n)
                    for j in range(GROUP):
                        for half, (at, w) in enumerate(HALVES):
                            m = 2 * j + half
                            pe.wait_ge(sem["gelu_done"], (n - 1) * (2 * GROUP) + (m + 1))
                            for k in range(KD):
                                for i, (u, h) in enumerate(((u_hi, h_hi), (u_hi, h_lo), (u_lo, h_hi))):
                                    last = mm(pair[:, m % 4, 0:w], R(u[b][:, P * (KD * j + k):P * (KD * j + k + 1)]), R(h[:, k, at:at + w]),
                                              start=(k == 0 and i == 0), stop=(k == KD - 1 and i == 2))
                            last.then_inc(sem["h_full"], 1)

                def values(b, n):
                    pe.wait_ge(sem["v_split"], n)
                    pe.wait_ge(sem["act_ready"], n * GROUP)
                    for m in range(2 * NT):
                        t, half = m // 2, m % 2
                        pe.wait_ge(sem["o_free"], (n - 1) * (2 * NT) + (m + 1))
                        for j in range(GROUP):
                            for i, (w, v) in enumerate(((act_hi, v_hi), (act_hi, v_lo), (act_lo, v_hi))):
                                last = mm(bank[(2 * b + m) % 4][:, :], R(w[b][:, j, P * t:P * (t + 1)]),
                                          R(v[b][:, D * j + 512 * half:D * j + 512 * half + 512]),
                                          start=(j == 0 and i == 0), stop=(j == GROUP - 1 and i == 2))
                        last.then_inc(sem["o_full"], 1)

                n0 = l * NG + 1
                pe.wait_ge(sem["g_free"], G_AHEAD + (l + 1) * T // 4)
                pe.wait_ge(sem["h_split"], KD * (l + 1))
                experts(0, n0)
                with pe.Fori(0, NG // 2 - 1) as i:
                    experts(1, i * 2 + (n0 + 1))
                    values(0, i * 2 + n0)
                    experts(0, i * 2 + (n0 + 2))
                    values(1, i * 2 + (n0 + 1))
                experts(1, n0 + NG - 1)
                values(0, n0 + NG - 2)
                values(1, n0 + NG - 1)

            pe.sem_inc(sem["g_full"], 4)
            pe.sem_inc(sem["o_full"], 1)
            layer = [0]
            for l in range(LAYERS):
                layer[0] = l
                ada(l)
                norm(l, 0)
                if l == 0:
                    project(EVEN_CHUNKS)
                    gla()
                    mla()
                else:
                    project(ODD_CHUNKS)
                    odd()
                out_project()
                norm(l, 1)
                route(l)
                routing_matrix(l)
                dense(l)

        @block.scalar
        def _(act):
            me = Turn(act, "chain_a")
            do = nc.scalar.activation
            link, give = me.link, me.give

            def take_a():
                n = me.next("a_full")
                act.wait_ge(sem["a_full"], n)
                return bank[2 + (n - 1) % 2]

            def copy_a(dst, w=512, func=ACT.Copy, **how):
                out = take_a()
                src = out[0:int(dst.shape[0]), 0:w]
                if len(dst.shape) == 3:
                    src = src.rearrange("p (k n) -> p k n", k=int(dst.shape[1]))
                give(do(dst, src, func, **how), "a_free")

            def root(n, at):
                act.wait_ge(*me.due("var_ready"))
                give(do(stat[:, at:at + n], stat[:, at:at + n], ACT.Sqrt), "std_ready")

            def ada(l):
                for kind in (2, 5):
                    for n in range(2):
                        for c in range(2):
                            copy_a(gate[:, kind // 3, c, 512 * n:512 * n + 512])

            def norm(l, s):
                if l == 0 and s == 0:
                    act.wait_ge(sem["x_in"], 16)
                else:
                    act.wait_ge(*me.due("x_done"))
                for t in range(NT):
                    ins = do(junk, x[:, t, :], ACT.Square, accum_out=stat[:, t:t + 1])
                    if t < NT - 1:
                        link(ins)
                give(ins, "ss_ready")
                root(NT, 0)
                act.wait_ge(*me.due("mods_done"))
                for t in range(NT):
                    c = int(t > 0)
                    out = take_a()
                    for k in range(4, 8):
                        ins = do(hT[:, k, P * t:P * (t + 1)], out[:, P * (k - 4):P * (k - 3)], ACT.Identity,
                                 bias=ada_col[:, s, 0, k, c:c + 1], scale=mod[:, s, k, c:c + 1])
                    give(ins, "a_free")

            def project(chunks, dst):
                for n, (at, w) in enumerate(chunks):
                    for t in range(NT):
                        if not ((n * NT + t) % 2 == 0 and n != 2):
                            copy_a(dst[:, t, at:at + w], w, ACT.Silu if at == R0 and dst is pe_ else ACT.Copy)

            def gla():
                for t in range(NT):
                    act.wait_ge(*me.due("z_part"))
                    link(do(en, eb, ACT.Exp, scale=-1.0))
                    give(do(en, en, ACT.Ln, bias=1.0), "z_exp")
                    out = take_a()
                    do(eb, out[:, :], ACT.Exp)
                    give(do(en, out[:, :], ACT.Exp, scale=-1.0), "a_free")
                    out = take_a()
                    give(do(es, out[:, :], ACT.Exp), "a_free")
                    out = take_a()
                    give(do(decay[:, t].rearrange("p d q c -> p (d q c)"), out[:, 0:8], ACT.Exp), "a_free")
                    copy_a(kiT)
                for t in range(NT):
                    root(4, 8)
                for t in range(NT):
                    copy_a(hT[:, 0:4, P * t:P * (t + 1)], scale=vecs[:, S_GO:S_GO + 1])

            def mla():
                me.after("out_state", 64)
                for kt in range(6):
                    if kt < NT:
                        root(1, 16)
                    copy_a(vals[:, kt, :])
                    root(8, 24)
                    for g in range(2):
                        copy_a(kT[:, 4 * g:4 * g + 4, P * kt:P * (kt + 1)])
                for qt in range(NT):
                    root(1, 16)
                    root(8, 24)
                    for g in range(2):
                        copy_a(qT[:, 512 * g:512 * g + 512])
                    n = P if qt == 0 else 5 * P

                    def soften(h):
                        act.wait_ge(*me.due("m_ready"))
                        at = 2 * ((marks[("scores", qt)]["s_full"] + h) % 2)
                        out = pair[:, at:at + 2, :].rearrange("p a b -> p (a b)")
                        give(do(probs[:, h % 2, 0:n], out[:, 0:n], ACT.Exp, bias=stat[:, 32 + h:33 + h],
                                scale=MLA_SCALE, accum_out=sums[:, h:h + 1]), "p_ready")

                    soften(0)
                    for h in range(NH):
                        if h + 1 < NH:
                            soften(h + 1)
                        if n > 512:
                            copy_a(pT[:, h % 2, 512:640], P)
                    copy_a(hT[:, 4:8, P * qt:P * (qt + 1)])

            def odd():
                for g in range(4):
                    scale = vecs[:, S_PS + g:S_PS + g + 1]
                    for at, n in ((0, 512), (512, P)):
                        copy_a(hT[:, g, at:at + n], n, scale=scale)
                for kt in range(6):
                    if kt < NT:
                        root(2, 24)
                    copy_a(kT2[:, :, P * kt:P * (kt + 1)], 256)
                for qt in range(NT):
                    root(8, 24)
                    copy_a(qT2)
                    n = P * len(window_tiles(qt))

                    def soften(h):
                        act.wait_ge(*me.due("m_ready"))
                        bias = stat[:, 32 + h:33 + h]
                        give(do(probs2[:, h % 2, 0:n], soft_s[:, h % 2, 0:n], ACT.Exp, bias=bias,
                                accum_out=sums[:, h:h + 1]), "p_ready")
                        give(do(sinks[:, h:h + 1], vecs[:, S_SINK + h:S_SINK + h + 1], ACT.Exp, bias=bias), "es_ready")

                    for h in range(NH):
                        soften(h)
                    copy_a(hT[:, 4:8, P * qt:P * (qt + 1)])

            def route():
                for g in range(16):
                    copy_a(qsT[:, g % 2, 0:512])
                    copy_a(qsT[:, g % 2, 512:640], P)
                act.wait_ge(*me.due("gate_in"))
                give(do(fin_v, fin_v, ACT.Exp), "gate_exp")

            def routing_matrix(l):
                jobs = TB // 4
                at = l * NB * jobs
                with act.Fori(0, NB // 2) as i:
                    for b in range(2):
                        act.wait_ge(sem[f"stage_out{b}"], i * 16 + 16 * (l * (NB // 2) + 1))


                        def scale_hots(n):
                            m = b * jobs + n
                            act.wait_ge(sem["hot_ready"], i * (2 * jobs) + (at + m + 1))
                            for q in range(2):
                                ins = do(hots[:, m % 4, 0, q, :], hots[:, m % 4, 0, q, :], ACT.Copy,
                                         scale=cols[:, b, 2, 4 * n + q:4 * n + q + 1])
                            ins.then_inc(sem["gated_a"], 1)

                        scale_hots(0)
                        scale_hots(1)
                        for n in range(jobs):
                            m = b * jobs + n
                            if n + 2 < jobs:
                                scale_hots(n + 2)
                            act.wait_ge(sem["g_full"], i * (2 * jobs) + (at + m + 5))
                            do(stage[:, b, :, 4 * n:4 * n + 4], pair[:, m % 4, :].rearrange("p (q j) -> p j q", q=4),
                               ACT.Copy).then_inc(sem["g_free"], 1)

            def split_u(b, n):
                act.wait_ge(sem[f"u_in{b}"], (n + (1 - b)) * 8)
                do(R(u_hi[b][:, :]), u_raw[b], ACT.Copy).then_inc(sem["u_led"], 1)

            def split_v(b, n):
                act.wait_ge(sem[f"v_in{b}"], (n + (1 - b)) * 8)
                do(R(v_hi[b][:, :]), v_raw[b], ACT.Copy).then_inc(sem["v_led"], 1)

            def first_tables(l):
                split_u(0, l * NG + 1)
                split_u(1, l * NG + 2)
                split_v(0, l * NG + 1)

            def dense(l):
                def gelu(b, n):
                    if type(n) is not int or n > l * NG + 2:
                        act.wait_ge(sem["o_full"], (n - 2) * (2 * NT) + 1)
                    for m in range(2 * GROUP):
                        if m == GROUP and (type(n) is not int or n > l * NG + 1):
                            split_v(b, n)
                        at, w = HALVES[m % 2]
                        act.wait_ge(sem["h_full"], (n - 1) * (2 * GROUP) + (m + 1))
                        do(act_raw[b][:, m // 2, at:at + w], pair[:, m % 4, 0:w], ACT.Gelu).then_inc(sem["gelu_done"], 1)

                n0 = l * NG + 1
                for b in range(2):
                    act.wait_ge(sem[f"stage_out{b}"], 16 + 16 * (l + 1) * NB // 2)
                for k in range(KD):
                    do(R(h_hi[:, k, :]), hT[:, k, :], ACT.Copy).then_inc(sem["h_led"], 1)
                gelu(0, n0)
                with act.Fori(0, NG // 2 - 1) as i:
                    split_u(0, i * 2 + (n0 + 2))
                    gelu(1, i * 2 + (n0 + 1))
                    split_u(1, i * 2 + (n0 + 3))
                    gelu(0, i * 2 + (n0 + 2))
                gelu(1, n0 + NG - 1)

            act.sem_inc(sem["g_free"], G_AHEAD)
            act.sem_inc(sem["gelu_done"], 4)
            act.wait_ge(sem["const_in"], 32)
            give(do(silu_c.rearrange("p k c -> p (k c)"), vecs[:, S_C:S_C + 16], ACT.Silu), "silu_done")
            for l in range(LAYERS):
                ada(l)
                norm(l, 0)
                if l == 0:
                    project(EVEN_CHUNKS, pe_)
                    gla()
                    mla()
                else:
                    project(ODD_CHUNKS, po_)
                    odd()
                norm(l, 1)
                route()
                first_tables(l)
                routing_matrix(l)
                dense(l)

        @block.sync
        def _(sp):
            sp.sem_inc(sem["stage_out0"], 16)
            sp.sem_inc(sem["stage_out1"], 16)

            def after(name, k):
                if k > 0:
                    sp.wait_ge(sem[name], k)

            def load(n):
                l = 0 if n < per_layer[0] else 1
                if n - 2 >= (0 if l == 0 else per_layer[0]):
                    after(*freed[n - 2])
                src = items[n]
                w = int(src.shape[1])
                sp.dma_start(ring[:, n % 2, 0:w], src).then_inc(sem[f"slot_in{n % 2}"], 16)

            for l in range(LAYERS):
                first = 0 if l == 0 else per_layer[0]
                if l:
                    sp.wait_ge(sem["x_done"], 2)
                for n in range(first, per_layer[l]):
                    if n < first + 12:
                        i = l * 12 + n - first
                        if n - first >= 2:
                            after(*freed[n - 2])
                        sp.dma_start(bias_rows[0:1, 512 * (i % 2):512 * (i % 2) + 512],
                                     a["b_ada"][l, n - first]).then_inc(sem[f"bias_in{i % 2}"], 16)
                    load(n)
                after(*freed[per_layer[l] - 2])
                sp.dma_start(u_raw[0], a["peer_u"][l, 0]).then_inc(sem["u_in0"], 16)
                sp.dma_start(u_raw[1], a["peer_u"][l, 1]).then_inc(sem["u_in1"], 16)
                sp.dma_start(v_raw[1], a["peer_v"][l, 1]).then_inc(sem["v_in1"], 16)
                after(*freed[per_layer[l] - 1])
                sp.dma_start(v_raw[0], a["peer_v"][l, 0]).then_inc(sem["v_in0"], 16)
                jobs = TB // 4
                with sp.Fori(0, NB // 2) as i:
                    for b in range(2):
                        sp.wait_ge(sem["g_free"], i * (2 * jobs) + (G_AHEAD + l * NB * jobs + jobs * (b + 1)))
                        sp.dma_start(routing[:, :, bass.ds(i * 2 + b, 1), :, :].rearrange("g p k j t -> p g (k j t)"),
                                     stage[:, b, :, :].rearrange("p (g j) t -> p g (j t)", g=NR)
                                     ).then_inc(sem[f"stage_out{b}"], 16)
                for b in range(2):
                    sp.wait_ge(sem[f"stage_out{b}"], 16 + 16 * (l + 1) * NB // 2)
                def load_routing(r):
                    src = routing[r].rearrange("p k j t -> p (k j t)") if type(r) is int else \
                        routing[bass.ds(r, 1)].rearrange("g p k j t -> p (g k j t)")
                    sp.dma_start(gmat.rearrange("p k j t -> p (k j t)"), src).then_inc(sem["g_in"], 16)

                def load_u(b, g):
                    sp.wait_ge(sem["h_full"], (g - 1) * (2 * GROUP) + l * NG * 2 * GROUP)
                    sp.dma_start(u_raw[b], table("peer_u", g)).then_inc(sem[f"u_in{b}"], 16)

                def load_v(b, g):
                    sp.wait_ge(sem["o_full"], (g - 1) * (2 * NT) + (l * NG * 2 * NT + 1))
                    sp.dma_start(v_raw[b], table("peer_v", g)).then_inc(sem[f"v_in{b}"], 16)

                def table(name, g):
                    return a[name][l, g] if type(g) is int else a[name][l, bass.ds(g, 1)].rearrange("g p n -> p (g n)")

                load_routing(0)
                load_u(0, 2)
                with sp.Fori(0, NG // 2 - 2) as i:
                    load_u(1, i * 2 + 3)
                    sp.wait_ge(sem["act_made"], i * (2 * GROUP) + GROUP * (l * NG + 2))
                    load_routing(i + 1)
                    load_v(0, i * 2 + 2)
                    load_u(0, i * 2 + 4)
                    load_v(1, i * 2 + 3)
                load_u(1, NG - 1)
                sp.wait_ge(sem["act_made"], GROUP * (l * NG + NG - 2))
                load_routing(NR - 1)
                load_v(0, NG - 2)
                load_v(1, NG - 1)
            sp.wait_ge(sem["x_done"], 4)
            sp.dma_start(a["y_prompt"], x[:, 0, :]).then_inc(sem["out_y"], 16)
            sp.dma_start(a["y_sample"].rearrange("(t p) d -> p t d", p=P), x[:, 1:NT, :]).then_inc(sem["out_y"], 16)
            sp.wait_ge(sem["out_y"], 32)

        @block.gpsimd
        def _(pool):
            def routing_matrix(l):
                jobs = TB // 4
                with pool.Fori(0, NB // 2) as i:
                    for b in range(2):
                        for n in range(jobs):
                            m = b * jobs + n
                            pool.wait_ge(sem["hot_ready"], i * (2 * jobs) + (l * NB * jobs + m + 1))
                            rows = hots[:, m % 4, 0, 2:4, :]
                            nc.gpsimd.tensor_tensor(rows, rows, bc(cols[:, b, 2, 4 * n + 2:4 * n + 4], P, 2),
                                                    ALU.mult).then_inc(sem["gated_p"], 1)

            pool.dma_start(const[:, :], a["const"]).then_inc(sem["const_in"], 16)
            pool.dma_start(vecs[:, :], a["vecs"]).then_inc(sem["const_in"], 16)
            pool.dma_start(x[:, :, :], a["x"].rearrange("(t p) d -> p t d", p=P)).then_inc(sem["x_in"], 16)
            pool.dma_start(wgu[0:33, :], a["w_gu"]).then_inc(sem["wgu_in"], 16)
            for r in range(2):
                pool.dma_start(s_in[64 * r:64 * r + 64, :, :].rearrange("k d (q v) -> k d q v", q=2),
                               a["state_in"][:, :, r]).then_inc(sem["s_in_in"], 16)
            pool.wait_ge(sem["ctx_state"], 1)
            for d in range(2):
                for r in range(2):
                    pool.dma_start(a["state"][d].rearrange("(q r) k v -> r k q v", r=2)[r],
                                   s_out[64 * r:64 * r + 64, d, :].rearrange("k (q v) -> k q v", q=2)
                                   ).then_inc(sem["out_state"], 16)
            pool.wait_ge(sem["s_ready"], 1)
            pool.dma_start(ctx_ckv, a["ctx_ckv"]).then_inc(sem["ctx_in"], 16)
            pool.dma_start(ctx_kr, a["ctx_kr"]).then_inc(sem["ctx_in"], 16)
            pool.wait_ge(sem["ckv_ready"], 1)
            pool.dma_start(a["ckv"], pe_[:, 0, CKV0:CKV0 + 256]).then_inc(sem["out_cache"], 16)
            pool.dma_start(a["kr"], pe_[:, 0, KR0:KR0 + 64]).then_inc(sem["out_cache"], 16)
            for l in range(LAYERS):
                if l == 1:
                    pool.wait_ge(sem["k_ready"], 7)
                    pool.dma_start(kctx, a["k_ctx"]).then_inc(sem["kvctx_in"], 16)
                    pool.dma_start(vctx, a["v_ctx"]).then_inc(sem["kvctx_in"], 16)
                    pool.dma_start(a["win"][0], po_[:, 0, KD0:KD0 + P]).then_inc(sem["out_cache"], 16)
                    pool.dma_start(a["win"][1], po_[:, 0, VD0:VD0 + P]).then_inc(sem["out_cache"], 16)
                pool.wait_ge(sem["x_done"], 2 * l + 1)
                pool.dma_start(subk.rearrange("p g n -> p (g n)"), a["subkeys"][l]).then_inc(sem["subk_in"], 16)
                routing_matrix(l)
            pool.wait_ge(sem["out_state"], 64)
            pool.wait_ge(sem["out_cache"], 64)

        @block.vector
        def _(dve):
            me = Turn(dve, "chain_v")
            V = nc.vector
            tt, ts, stt = V.tensor_tensor, V.tensor_scalar, V.scalar_tensor_tensor
            link, give = me.link, me.give

            def take_d():
                n = me.next("d_full")
                dve.wait_ge(sem["d_full"], n)
                return bank[(n - 1) % 2]

            def take_s():
                n = me.next("s_full")
                dve.wait_ge(sem["s_full"], n)
                return pair[:, 2 * ((n - 1) % 2):2 * ((n - 1) % 2) + 2, :]

            def signal(name):
                dve.sem_inc(sem[name], 1)
                total[name] = total.get(name, 0) + 1

            def rstd(ss, n):
                give(ts(ss, ss, 1.0 / n, EPS, ALU.mult, ALU.add), "var_ready")
                dve.wait_ge(*me.due("std_ready"))
                link(V.reciprocal(ss, ss))

            def ada(l):
                for n in range(12):
                    i = l * 12 + n
                    out = take_d()
                    row = ada_rows[0:2, 512 * (i % 2):512 * (i % 2) + 512]
                    give(V.tensor_copy(row, out[0:2, :]), "d_free")
                    kind = n // 2
                    if kind not in (2, 5):
                        out = take_d()
                        s, w = (0, kind) if kind < 2 else (1, kind - 3)
                        give(V.tensor_copy(ada_col[:, s, w, 4 * (n % 2):4 * (n % 2) + 4, :],
                                           out[:, 0:8].rearrange("p (k c) -> p k c", k=4)), "d_free")
                for s in range(2):
                    g = vecs[:, S_GN + 16 * l + 8 * s:S_GN + 16 * l + 8 * s + 8]
                    give(stt(mod[:, s, :, :], ada_col[:, s, 1, :, :], 1.0, bc(g, 2, 2), ALU.add, ALU.mult),
                         "mods_done")

            def norm(l, s):
                dve.wait_ge(*me.due("ss_ready"))
                rstd(stat[:, 0:NT], D)
                for t in range(NT):
                    give(ts((xn0, xn1)[t % 2], x[:, t, :], stat[:, t:t + 1], None, ALU.mult), "xn_ready")
                    if t:
                        evac_norm(s, t - 1)
                evac_norm(s, NT - 1)

            def evac_norm(s, t):
                out = take_d()
                c = int(t > 0)
                for k in range(4):
                    ins = ts(hT[:, k, P * t:P * (t + 1)], out[:, P * k:P * (k + 1)], mod[:, s, k, c:c + 1],
                             ada_col[:, s, 0, k, c:c + 1], ALU.mult, ALU.add)
                give(ins, "d_free")

            def project(chunks, dst):
                for n, (at, w) in enumerate(chunks):
                    for t in range(NT):
                        if (n * NT + t) % 2 == 0 and n != 2:
                            out = take_d()
                            give(V.tensor_copy(dst[:, t, at:at + w], out[:, 0:w]), "d_free")
                me.after("a_free", marks[("proj", layer[0])]["a_full"])

            def gla():
                link(V.memset(attT.rearrange("p r d q n -> p (r d q n)"), 0.0))
                link(V.memset(glT[32:33, :], 1.0))
                for t in range(NT):
                    pt = pe_[:, t, :]
                    out = take_d()
                    give(V.tensor_copy(glT[0:32, :], out[0:32, 0:P]), "d_free")
                    out = take_d()
                    link(ts(eb, out[:, :], -1.0, None, ALU.mult))
                    give(tt(eb, eb, out[:, :], ALU.max), "z_part")
                    give(ts(la, out[:, :], 0.0, 1.0 / 16.0, ALU.min, ALU.mult), "d_free")
                    dve.wait_ge(*me.due("z_exp"))
                    give(stt(la, en, -1.0 / 16.0, la, ALU.mult, ALU.add), "la_ready")
                    me.after("a_free", marks[("exps", t)]["a_full"])
                    q2 = bc(pt[:, Q0:Q0 + 256], 2, 1)
                    k2_ = bc(pt[:, K0:K0 + 256], 2, 1)
                    for e, s_, sc in ((eb, q2, 64.0 ** -0.5), (en, k2_, 1.0), (es, k2_, 1.0)):
                        e3 = e.rearrange("p (d n) -> p d n", d=2)
                        ins = stt(e3, s_, sc, e3, ALU.mult, ALU.mult)
                    give(ins, "exps_mul")
                    out = take_d()
                    give(V.tensor_copy(qdT[:, t, :, :], out[:, :].rearrange("p (q n) -> p q n", q=4)), "d_free")
                    out = take_s()
                    for r in range(2):
                        for d in range(2):
                            ins = V.copy_predicated(
                                attT[:, r, d, :, :], bc(cum[d].bitcast(U32), 2, 1),
                                out[:, r, 256 * d:256 * d + 256].rearrange("p (q n) -> p q n", q=2))
                    give(ins, "s_free")
                    out = take_s()
                    for c in range(2):
                        ins = V.tensor_copy(upd[:, 2 * t + c, :, :], out[:, c, :].rearrange("p (d n) -> p d n", d=2))
                    give(ins, "s_free")
                    out = take_d()
                    give(V.tensor_copy(pt[:, 0:512], out[:, :]), "d_free")
                me.after("a_free", marks["gla_tiles"]["a_full"])
                cur = [s.rearrange("p (d n) -> p d n", d=2) for s in scan_cur]
                for part, chunks in (("context", (0, 1)), ("latent", tuple(range(2, 10)))):
                    if part == "context":
                        link(V.memset(scan_cur[0], 0.0))
                    else:
                        dve.wait_ge(sem["s_in_in"], 32)
                        link(V.tensor_copy(cur[0], s_in[:, :, :]))
                    for i in range(len(chunks)):
                        a_, b_ = cur[i % 2], cur[(i + 1) % 2]
                        for d in range(2):
                            c = chunks[i] if d == 0 else chunks[-1 - i]
                            for q in range(2):
                                nq = slice(P * q, P * (q + 1))
                                link(stt(b_[:, d, nq], a_[:, d, nq], decay[:, c // 2, d, q, c % 2:c % 2 + 1],
                                         upd[:, c, d, nq], ALU.mult, ALU.add))
                            ins = V.tensor_copy(upd[:, c, d, :], a_[:, d, :])
                            if i + 1 < len(chunks) or d == 0 or part == "context":
                                link(ins)
                    if part == "context":
                        give(V.tensor_copy(s_out, cur[0]), "ctx_state")
                give(ins, "s_ready")
                for t in range(NT):
                    o = pe_[:, t, 0:512]
                    out = take_s()
                    for r in range(2):
                        o_r = o.rearrange("p (q r n) -> p q r n", q=2, r=2)[:, :, r, :]
                        ins = tt(o_r, o_r, out[:, r, 0:256].rearrange("p (q n) -> p q n", q=2), ALU.add)
                    give(ins, "s_free")
                    o4 = o.rearrange("p (h n) -> p h n", h=4)
                    link(tt(sq5, o, o, ALU.mult))
                    link(V.tensor_reduce(stat[:, 8:12], sq5.rearrange("p (h n) -> p h n", h=4), AX.X, ALU.add))
                    rstd(stat[:, 8:12], P)
                    link(tt(o4, o4, bc(stat[:, 8:12], P, 2), ALU.mult))
                    give(tt(o, o, pe_[:, t, R0:R0 + 512], ALU.mult), "oa_ready")

            def rope_into(dst, src, t, heads):
                cos, sin = rope[:, t - 1, 0, :], rope[:, t - 1, 1, :]
                tmp = sq10[:, 0:64 * heads] if layer[0] == 0 else sqo[:, 0:64 * heads]
                s5 = src.rearrange("p h (a b n) -> p h a b n", a=2, b=2)
                t5 = tmp.rearrange("p (h a b n) -> p h a b n", h=heads, a=2, b=2)
                n4 = sin.rearrange("p (a b n) -> p a b n", a=2, b=2)
                for b in range(2):
                    if heads == 1:
                        link(tt(t5[:, 0, :, b, :], s5[:, 0, :, 1 - b, :], n4[:, :, b, :], ALU.mult))
                    else:
                        link(tt(t5[:, :, :, b, :], s5[:, :, :, 1 - b, :], bc(n4[:, :, b, :], heads, 1), ALU.mult))
                t3 = tmp.rearrange("p (h n) -> p h n", h=heads)
                link(tt(dst, src, bc(cos, heads, 1), ALU.mult))
                link(tt(dst, dst, t3, ALU.add))

            def latent(src, gain):
                link(V.tensor_tensor_reduce(sq10[:, 0:256], src, src, 1.0, 0.0, ALU.mult, ALU.add, stat[:, 16:17]))
                rstd(stat[:, 16:17], 256)
                give(stt(src, src, stat[:, 16:17], gain, ALU.mult, ALU.mult), "ckv_ready")

            def copy_ckvT():
                out = take_d()
                give(V.tensor_copy(ckvT, out[:, 0:256]), "d_free")

            def mla():
                me.after("a_full", marks["oa"]["a_full"])
                g_kn = vecs[:, S_KN:S_KN + P]
                g_qn = vecs[:, S_QN:S_QN + P]
                qk3 = qk.rearrange("p (h n) -> p h n", h=NH)
                for kt in range(6):
                    if kt < NT:
                        latent(pe_[:, kt, CKV0:CKV0 + 256], vecs[:, S_CKV:S_CKV + 256])
                        kr = pe_[:, kt, KR0:KR0 + 64]
                    else:
                        dve.wait_ge(sem["ctx_in"], 32)
                        signal("ckv_ready")
                        kr = ctx_kr
                    copy_ckvT()
                    link(V.tensor_tensor_reduce(krt, kr, kr, 1.0, 0.0, ALU.mult, ALU.add, stat[:, 17:18]))
                    link(tt(krt, kr, g_kn[:, 64:128], ALU.mult))
                    if 1 <= kt < NT:
                        rope_into(krr.unsqueeze(1), krt.unsqueeze(1), kt, 1)
                    else:
                        link(V.tensor_copy(krr, krt))
                    out = take_d()
                    give(V.tensor_copy(qk3[:, :, 0:64], out[:, :].rearrange("p (h n) -> p h n", h=NH)), "d_free")
                    s3 = sq10[:, 0:512].rearrange("p (h n) -> p h n", h=NH)
                    link(tt(s3, qk3[:, :, 0:64], qk3[:, :, 0:64], ALU.mult))
                    link(V.tensor_reduce(stat[:, 24:32], s3, AX.X, ALU.add))
                    link(ts(stat[:, 24:32], stat[:, 24:32], stat[:, 17:18], None, ALU.add))
                    rstd(stat[:, 24:32], P)
                    r3 = bc(stat[:, 24:32], 64, 2)
                    link(tt(qk3[:, :, 0:64], qk3[:, :, 0:64], bc(g_kn[:, 0:64], NH, 1), ALU.mult))
                    link(tt(qk3[:, :, 0:64], qk3[:, :, 0:64], r3, ALU.mult))
                    give(tt(qk3[:, :, 64:128], bc(krr, NH, 1), r3, ALU.mult), "k_ready")
                for qt in range(NT):
                    latent(pe_[:, qt, CQ0:CQ0 + 256], vecs[:, S_CQ:S_CQ + 256])
                    copy_ckvT()
                    for g in range(2):
                        out = take_d()
                        give(V.tensor_copy(qk[:, 512 * g:512 * g + 512], out[:, :]), "d_free")
                    s3 = sq10.rearrange("p (h n) -> p h n", h=NH)
                    link(tt(s3, qk3, qk3, ALU.mult))
                    link(V.tensor_reduce(stat[:, 24:32], s3, AX.X, ALU.add))
                    rstd(stat[:, 24:32], P)
                    link(tt(qk3, qk3, bc(g_qn, NH, 1), ALU.mult))
                    ins = tt(qk3, qk3, bc(stat[:, 24:32], P, 2), ALU.mult)
                    if qt:
                        link(ins)
                        rope_into(qk3[:, :, 64:128], qk3[:, :, 64:128], qt, NH)
                        signal("q_ready")
                    else:
                        give(ins, "q_ready")
                    n = P if qt == 0 else 5 * P

                    def biggest(h):
                        out = take_s().rearrange("p a b -> p (a b)")
                        link(V.tensor_reduce(stat[:, 32 + h:33 + h], out[:, 0:n], AX.X, ALU.max))
                        give(ts(stat[:, 32 + h:33 + h], stat[:, 32 + h:33 + h], -MLA_SCALE, None, ALU.mult), "m_ready")

                    biggest(0)
                    for h in range(NH):
                        if h + 1 < NH:
                            biggest(h + 1)
                        finish_head(h, pT[:, h % 2, :], min(n, 512), att_o)

            def finish_head(h, pT_b, n, dst):
                dve.wait_ge(*me.due("p_ready"))
                if layer[0] == 0:
                    signal("s_free")
                out = take_d()
                give(V.tensor_copy(pT_b[:, 0:n], out[:, 0:n]), "d_free")
                link(V.reciprocal(stat[:, 48 + h % 2:49 + h % 2], sums[:, h:h + 1]))
                out = take_d()
                give(ts(dst[:, 64 * h:64 * h + 64], out[:, 0:64], stat[:, 48 + h % 2:49 + h % 2], None, ALU.mult),
                     "d_free")

            def head_norm(buf3, gain, heads, t, at):
                s3 = sqo[:, 0:64 * heads].rearrange("p (h n) -> p h n", h=heads)
                link(tt(s3, buf3, buf3, ALU.mult))
                link(V.tensor_reduce(stat[:, at:at + heads], s3, AX.X, ALU.add))
                rstd(stat[:, at:at + heads], 64)
                link(tt(buf3, buf3, bc(gain, heads, 1), ALU.mult))
                link(tt(buf3, buf3, bc(stat[:, at:at + heads], 64, 2), ALU.mult))
                if t:
                    rope_into(buf3, buf3, t, heads)

            def odd():
                for g in range(4):
                    out = take_d()
                    give(V.tensor_copy(yT[:, g % 2, 0:P], out[:, 0:P]), "d_free")
                    out = take_d()
                    give(V.tensor_copy(yT[:, g % 2, P:T], out[:, :]), "d_free")
                for kt in range(6):
                    if kt < NT:
                        k = po_[:, kt, KD0:KD0 + P]
                        k3 = k.rearrange("p (v n) -> p v n", v=2)
                        head_norm(k3, vecs[:, S_WKN:S_WKN + 64], 2, kt, 24)
                    else:
                        dve.wait_ge(sem["kvctx_in"], 32)
                        k3 = kctx.rearrange("p (v n) -> p v n", v=2)
                    if kt:
                        me.after("a_full", marks[("odd_k", kt - 1)]["a_full"])
                    k24 = k2.rearrange("p (v r n) -> p v r n", v=2, r=2)
                    give(V.tensor_copy(k24, bc(k3, 2, 2)), "k_ready")
                sink = vecs[:, S_SINK:S_SINK + NH]
                for qt in range(NT):
                    if qt == 0:
                        me.after("a_full", marks[("odd_k", 5)]["a_full"])
                    qn3 = qn.rearrange("p (h n) -> p h n", h=NH)
                    link(V.tensor_copy(qn, po_[:, qt, QD0:QD0 + 512]))
                    head_norm(qn3, vecs[:, S_WQN:S_WQN + 64], NH, qt, 24)
                    signal("q_ready")
                    tiles = window_tiles(qt)
                    n = P * len(tiles)
                    if qt == 0 or qt == 4:
                        parts = [(0, P, P)] if qt == 0 else [(0, 2 * P, 0), (2 * P, P, P)]
                    else:
                        parts = [(0, n, P if qt == 1 else 0)]

                    def biggest(h):
                        out = take_s().rearrange("p a b -> p (a b)")
                        s_ = soft_s[:, h % 2, :]
                        for i, (at, w, m_at) in enumerate(parts):
                            ins = stt(s_[:, at:at + w], out[:, at:at + w], WIN_SCALE, wmask[:, m_at:m_at + w],
                                      ALU.mult, ALU.add)
                            if i + 1 < len(parts):
                                link(ins)
                        give(ins, "s_free")
                        link(V.tensor_reduce(stat[:, 32 + h:33 + h], s_[:, 0:n], AX.X, ALU.max))
                        give(ts(stat[:, 32 + h:33 + h], stat[:, 32 + h:33 + h], sink[:, h:h + 1], -1.0,
                                ALU.max, ALU.mult), "m_ready")

                    biggest(0)
                    for h in range(NH):
                        if h + 1 < NH:
                            biggest(h + 1)
                        dve.wait_ge(*me.due("es_ready"))
                        link(tt(sums[:, h:h + 1], sums[:, h:h + 1], sinks[:, h:h + 1], ALU.add))
                        finish_head(h, pT2[:, h % 2, :], n, att_o2)

            def out_project(l):
                me.after("out_cache", 32 * (l + 1))
                for n in range(2):
                    for t in range(NT):
                        out = take_d()
                        g = gate[:, 0, int(t > 0), 512 * n:512 * n + 512]
                        tmp = arena[:, 8192:8704]
                        give(tt(tmp, out[:, :], g, ALU.mult), "d_free")
                        xs = x[:, t, 512 * n:512 * n + 512]
                        ins = tt(xs, xs, tmp, ALU.add)
                        if n == 0 or t < NT - 1:
                            link(ins)
                give(ins, "x_done")

            def sixteen(values, cut, idx_out, val_out):
                v8, i8 = val_out, tmp_i[:, :]
                link(V.max(v8[:, 0:8], values))
                link(V.max_index(i8[:, 0:8], v8[:, 0:8], values))
                link(V.match_replace(cut, v8[:, 0:8], values, LOWEST))
                link(V.max(v8[:, 8:16], cut))
                link(V.max_index(i8[:, 8:16], v8[:, 8:16], cut))
                link(V.tensor_copy(idx_out, i8))

            def route(l):
                fin_p3 = fin_p.bitcast(U32).rearrange("p (t h k) -> p t h k", t=NT, h=NH)
                for g in range(16):
                    h, c = g // 2, g % 2
                    out = take_s()
                    for t in range(NT):
                        sixteen(out[:, t // 4, P * (t % 4):P * (t % 4 + 1)], sc_cut, top_i5[:, t, h, c, :],
                                top_v5[:, t, h, c, :])
                    signal("s_free")
                    if c:
                        for t in range(NT):
                            cand3 = cand.rearrange("p (i j) -> p i j", i=TOPK)
                            link(tt(cand3, bc(top_v5[:, t, h, 0, :], TOPK, 2), bc(top_v5[:, t, h, 1, :], TOPK, 1), ALU.add))
                            sixteen(cand, cand_cut, fin_p3[:, t, h, :], fin_v4[:, t, h, :])
                fv3 = fin_v.rearrange("p (g k) -> p g k", k=TOPK)
                link(V.tensor_copy(sums40, fv3[:, :, 0]))
                give(tt(fv3, fv3, bc(sums40, TOPK, 2), ALU.subtract), "gate_in")
                dve.wait_ge(*me.due("gate_exp"))
                link(V.tensor_reduce(sums40, fv3, AX.X, ALU.add))
                link(V.reciprocal(sums40, sums40))
                link(tt(pick3[:, 2, :, :].rearrange("p t (h k) -> p (t h) k", h=NH), fv3, bc(sums40, TOPK, 2), ALU.mult))
                pa = posab[:, 0:640].bitcast(U32)
                pb = posab[:, 640:1280].bitcast(U32)
                link(ts(pa, fin_p.bitcast(U32), 4, None, ALU.logical_shift_right))
                link(ts(pb, fin_p.bitcast(U32), 15, None, ALU.bitwise_and))
                pos_f = qsT.rearrange("p b t -> p (b t)")
                link(V.tensor_copy(pos_f[:, 0:640], pa))
                link(V.tensor_copy(pos_f[:, 640:1280], pb))
                hot3 = hot.rearrange("p (n k) -> p n k", k=TOPK)
                hot4 = hot.rearrange("p (h n k) -> p h n k", h=NH, k=TOPK)
                for t in range(NT):
                    for c in range(2):
                        pos = pos_f[:, 640 * c + P * t:640 * c + P * (t + 1)]
                        link(tt(hot3, bc(pos, TOPK, 2), bc(iota[:, 0:TOPK], P, 1), ALU.is_equal))
                        link(tt(hot4, hot4, bc(top_i5[:, t, :, c, :], TOPK, 2), ALU.mult))
                        ins = V.tensor_reduce(pick3[:, c, t, :], hot3, AX.X, ALU.add)
                        if c == 0:
                            link(ins)
                    give(ins, "pick_ready")
                for t in range(NT):
                    out = take_d()
                    give(V.tensor_copy(pickT[:, :, P * t:P * (t + 1)],
                                       out[:, 0:3 * P].rearrange("p (k n) -> p k n", k=3)), "d_free")

            def routing_matrix(l):
                jobs = TB // 4
                hot0 = l * NB * jobs
                with dve.Fori(0, NB // 2) as i:
                    for b in range(2):
                        dve.wait_ge(sem["g_free"], i * (2 * jobs) + (hot0 + jobs * (b - 1) + G_AHEAD))
                        ts(cols[:, b, :, :], pickT[:, :, bass.ds(i * (2 * TB) + b * TB, TB)], 1.0, None,
                           ALU.mult).then_inc(sem["cols_ready"], 1)
                        dve.wait_ge(sem["cols_ready"], i * 2 + (l * NB + b + 1))
                        for n in range(jobs):
                            m = b * jobs + n
                            dve.wait_ge(sem["g_full"], i * (2 * jobs) + (hot0 + m + 1))
                            tt(hots[:, m % 4], bc(cols[:, b, 0:2, 4 * n:4 * n + 4], P, 3),
                               bc(bc(iota, 4, 1), 2, 1), ALU.is_equal).then_inc(sem["hot_ready"], 1)

            def dense(l):
                def split_u(b, n):
                    dve.wait_ge(sem["u_led"], n)
                    tt(R(u_lo[b][:, :]), u_raw[b], u_hi[b][:, :], ALU.subtract).then_inc(sem["u_split"], 1)

                def split_v(b, n):
                    dve.wait_ge(sem["v_led"], n)
                    tt(R(v_lo[b][:, :]), v_raw[b], v_hi[b][:, :], ALU.subtract).then_inc(sem["v_split"], 1)

                def weight(b, n, j):
                    dve.wait_ge(sem["gelu_done"], (n - 1) * (2 * GROUP) + (2 * j + 6))
                    part = act_raw[b][:, j, :]
                    part3 = part.rearrange("p (k t) -> p k t", t=TB)
                    c = (n - 1) * GROUP + (j + 1)
                    tt(part3, part3, gmat[:, :, GROUP * b + j, :], ALU.mult).then_inc(sem["act_made"], 1)
                    dve.wait_ge(sem["act_made"], c)
                    V.tensor_copy(R(act_hi[b][:, j, :]), part).then_inc(sem["act_led"], 1)
                    dve.wait_ge(sem["act_led"], c)
                    tt(R(act_lo[b][:, j, :]), part, act_hi[b][:, j, :], ALU.subtract).then_inc(sem["act_ready"], 1)

                def add(b, n):
                    for m in range(2 * NT):
                        t, half = m // 2, m % 2
                        dve.wait_ge(sem["o_free"], (n - 1) * (2 * NT) + (m + 4))
                        dve.wait_ge(sem["o_full"], (n - 1) * (2 * NT) + (m + 2))
                        part = acc[:, t, 512 * half:512 * half + 512]
                        tt(part, part, bank[(2 * b + m) % 4][:, :], ALU.add).then_inc(sem["o_free"], 1)

                n0 = l * NG + 1
                split_u(0, n0)
                for k in range(KD):
                    dve.wait_ge(sem["h_led"], KD * l + k + 1)
                    tt(R(h_lo[:, k, :]), hT[:, k, :], h_hi[:, k, :], ALU.subtract).then_inc(sem["h_split"], 1)
                split_u(1, n0 + 1)
                for b in range(2):
                    dve.wait_ge(sem[f"stage_out{b}"], 16 + 16 * (l + 1) * NB // 2)
                link(V.memset(acc.rearrange("p t d -> p (t d)"), 0.0))
                dve.wait_ge(sem["g_in"], 16 * (l * NR + 1))
                weight(0, n0, 0)
                split_v(0, n0)
                weight(0, n0, 1)
                with dve.Fori(0, NG // 2 - 1) as i:
                    split_u(0, i * 2 + (n0 + 2))
                    weight(1, i * 2 + (n0 + 1), 0)
                    split_v(1, i * 2 + (n0 + 1))
                    weight(1, i * 2 + (n0 + 1), 1)
                    add(0, i * 2 + n0)
                    split_u(1, i * 2 + (n0 + 3))
                    dve.wait_ge(sem["g_in"], i * 16 + 16 * (l * NR + 2))
                    weight(0, i * 2 + (n0 + 2), 0)
                    split_v(0, i * 2 + (n0 + 2))
                    weight(0, i * 2 + (n0 + 2), 1)
                    add(1, i * 2 + (n0 + 1))
                n = n0 + NG - 2
                weight(1, n + 1, 0)
                split_v(1, n + 1)
                weight(1, n + 1, 1)
                add(0, n)
                add(1, n + 1)
                dve.wait_ge(sem["o_free"], 4 + (l + 1) * 2 * NT * NG)
                for t in range(NT):
                    link(tt(acc[:, t, :], acc[:, t, :], gate[:, 1, int(t > 0), :], ALU.mult))
                    ins = tt(x[:, t, :], x[:, t, :], acc[:, t, :], ALU.add)
                    if t < NT - 1:
                        link(ins)
                give(ins, "x_done")

            layer = [0]
            dve.wait_ge(sem["const_in"], 32)
            dve.wait_ge(sem["x_in"], 16)
            dve.sem_inc(sem["o_free"], 4)
            for l in range(LAYERS):
                layer[0] = l
                ada(l)
                norm(l, 0)
                if l == 0:
                    project(EVEN_CHUNKS, pe_)
                    gla()
                    mla()
                else:
                    project(ODD_CHUNKS, po_)
                    odd()
                out_project(l)
                norm(l, 1)
                route(l)
                routing_matrix(l)
                dense(l)


def constants():
    c = np.zeros((P, C_N), np.float32)
    i = np.arange(P)
    c[:, C_ID:C_ID + P] = np.eye(P)
    c[:, C_IOTA:C_IOTA + P] = i
    same = (i[:, None] // 64) == (i[None, :] // 64)
    c[:, C_CUM:C_CUM + P] = same & (i[:, None] <= i[None, :])
    c[:, C_CUM + P:C_CUM + 2 * P] = same & (i[:, None] >= i[None, :])
    c[:, C_REST:C_REST + P] = same & (i[:, None] > i[None, :])
    c[:, C_REST + P:C_REST + 2 * P] = same & (i[:, None] < i[None, :])
    c[:64, C_IND] = 1
    c[64:, C_IND + 1] = 1
    c[0, C_SEL:C_SEL + P] = 1
    c[1, C_SEL + P:C_SEL + 2 * P] = 1
    c[:, C_ONE:C_ONE + 2] = 1
    inv = np.float32(10000.0) ** (-np.arange(16, dtype=np.float32) / np.float32(16))
    pos = np.arange(512)
    ar = (pos // GRID_W).astype(np.float32)[:, None] * inv
    ac = (pos % GRID_W).astype(np.float32)[:, None] * inv
    ang = np.concatenate([ar, ar, ac, ac], -1).astype(np.float32)
    sign = np.tile(np.repeat(np.array([-1.0, 1.0], np.float32), 16), 2)
    table = np.stack([np.cos(ang), np.sin(ang) * sign], 1).reshape(4, P, 2, 64).transpose(1, 0, 2, 3)
    c[:, C_ROPE:C_ROPE + 512] = table.reshape(P, 512)
    c[:, C_MASK:C_MASK + P] = np.where(i[None, :] >= i[:, None], 0.0, -1e30)
    c[:, C_MASK + 2 * P:C_MASK + 3 * P] = np.where(i[None, :] <= i[:, None], 0.0, -1e30)
    return c


def pool_bands():
    def full(n, w):
        t = np.arange(n)
        lo, hi = np.clip(t - w // 2, 0, n), np.clip(t - w // 2 + w, 0, n)
        m = (t[:, None] >= lo[None, :]) & (t[:, None] < hi[None, :])
        return m / (hi - lo)[None, :].astype(np.float32) - np.eye(n)
    out = np.zeros((P, 4, 6, P), np.float32)
    for g, w in enumerate(WINDOWS):
        out[:, g, 0] = full(P, w)
        m = full(4 * P, w)
        out[:, g, 1] = m[0:P, 0:P]
        out[:, g, 2] = m[P:2 * P, P:2 * P]
        out[:, g, 3] = m[3 * P:, 3 * P:]
        out[:, g, 4] = m[0:P, P:2 * P]
        out[:, g, 5] = m[2 * P:3 * P, P:2 * P]
    return out.reshape(P, 4 * 6 * P)


def slabs(w):
    k, n = w.shape
    return w.reshape(k // P, P, n).transpose(1, 0, 2).reshape(P, -1)


def kernel(**inputs):
    import concourse.bacc as bacc
    from concourse.bass_utils import run_bass_kernel_spmd

    v = {k: np.asarray(x) for k, x in inputs.items()}
    cat, rows = np.concatenate, lambda g: np.broadcast_to(g[None, :], (P, g.shape[0]))
    w_even = v["w_in_even"][0]
    order = [w_even[:, 0:1536], w_even[:, 1568:2080], w_even[:, 1536:1568], w_even[:, 2080:2144]]
    w_even = cat(order, 1)
    w_gu = np.zeros((33, 512), np.float32)
    w_gu[0:16, 0:256] = v["w_gate_up"][0, 0]
    w_gu[16:32, 256:512] = v["w_gate_up"][0, 1]
    w_gu[32] = v["b_gate_up"][0].reshape(-1)
    cond = np.stack([v["c_ctx"], v["c"][0]], 1).reshape(KD, P, 2).transpose(1, 0, 2).reshape(P, 16)
    vecs = cat([
        cond, v["g_norm"].reshape(LAYERS * 2 * KD, P).T, rows(v["g_mla_ckv"][0]), rows(v["g_mla_cq"][0]),
        rows(v["g_mla_qn"][0]), rows(v["g_mla_kn"][0]), v["g_gla_out"][0][:, None], rows(v["g_win_qn"][0]),
        rows(v["g_win_kn"][0]), rows(v["win_sink"][0]), v["pool_scale"][0].reshape(4, P).T], 1)
    assert vecs.shape[1] == S_N
    ins = {
        "const": constants(),
        "vecs": vecs,
        "x": cat([v["x_prompt"][0], v["x_sample"][0]], 0),
        "w_gu": w_gu,
        "state_in": v["state_gla"][0, 0].reshape(2, 2, 2, 64, P).transpose(3, 0, 2, 1, 4),
        "ctx_ckv": v["cache_mla_ckv"][0, 0],
        "ctx_kr": v["cache_mla_krope"][0, 0],
        "k_ctx": v["cache_win_kv"][0, 0, 0].reshape(P, P),
        "v_ctx": v["cache_win_kv"][0, 0, 1].reshape(P, P),
        "w_ada": v["w_ada"].reshape(LAYERS, KD, P, 12, 512).transpose(0, 3, 2, 1, 4).reshape(LAYERS, 12, P, 4096),
        "b_ada": v["b_ada"].reshape(LAYERS, 12, 1, 512),
        "w_mla": cat([slabs(v["w_mla_uq"][0]), slabs(v["w_mla_uk"][0]), slabs(v["w_mla_uv"][0])], 1),
        "w_band": cat([pool_bands(), v["w_pool"][0].transpose(1, 0, 2).reshape(P, 512)], 1),
        "w_out0": np.stack([slabs(v["w_out_even"][0][:, 512 * n:512 * n + 512]) for n in range(2)]),
        "w_out1": np.stack([slabs(v["w_out_odd"][0][:, 512 * n:512 * n + 512]) for n in range(2)]),
        "peer_wq": v["peer_wq"].reshape(LAYERS, KD, P, 4, 512).transpose(0, 3, 2, 1, 4).reshape(LAYERS, 4, P, 4096),
        "subkeys": v["peer_subkeys"].reshape(LAYERS, 16, NEXP, P).transpose(0, 3, 1, 2).reshape(LAYERS, P, 2048),
        "peer_u": v["peer_u"].reshape(LAYERS, NEXP, NG, GROUP, KD, P).transpose(0, 2, 5, 3, 4, 1)
                             .reshape(LAYERS, NG, P, GROUP * D),
        "peer_v": v["peer_v"].reshape(LAYERS, NEXP, NG, GROUP * D).transpose(0, 2, 1, 3),
    }
    for n, (at, w) in enumerate(EVEN_CHUNKS):
        ins[f"w_in0_{n}"] = slabs(w_even[:, at:at + w])
    for n, (at, w) in enumerate(ODD_CHUNKS):
        ins[f"w_in1_{n}"] = slabs(v["w_in_odd"][0][:, at:at + w])
    ins = {k: np.ascontiguousarray(x) for k, x in ins.items()}
    outs = {"y_prompt": (P, D), "y_sample": (512, D), "state": (2, 4, 64, P), "ckv": (P, 256), "kr": (P, 64),
            "win": (2, P, P)}
    nc = bacc.Bacc("TRN2", target_bir_lowering=False, num_devices=1)
    aps = {k: nc.dram_tensor(f"in_{k}", x.shape, F32, kind="ExternalInput").ap() for k, x in ins.items()}
    aps |= {k: nc.dram_tensor(f"out_{k}", s, F32, kind="ExternalOutput").ap() for k, s in outs.items()}
    build_program(nc, aps)
    r = run_bass_kernel_spmd(nc, [{f"in_{k}": x for k, x in ins.items()}], core_ids=[0]).results[0]
    return (r["out_y_prompt"].reshape(1, P, D), r["out_y_sample"].reshape(1, 512, D),
            r["out_state"].reshape(1, 1, 2, 4, 64, P), r["out_ckv"].reshape(1, 1, P, 256),
            r["out_kr"].reshape(1, 1, P, 64), r["out_win"].reshape(1, 1, 2, P, 2, 64))
```

```python
from contextlib import ExitStack

import numpy as np

import concourse.bass as bass
from concourse import mybir

F32 = mybir.dt.float32
U32 = mybir.dt.uint32
F32R = mybir.dt.float32r
ACT = mybir.ActivationFunctionType
ALU = mybir.AluOpType
AX = mybir.AxisListType

P = 128
D = 1024
KD = D // P
NT = 5
T = NT * P
EPS = 1e-6
LAYERS = 2
NH = 8
TOPK = 16
NEXP = 128
GROUP = 2
NG = NEXP // GROUP
RGROUP = 2 * GROUP
NR = NEXP // RGROUP
G_AHEAD = 12
HALVES = ((0, 384), (384, 256))
PAIRS = ((0, 2, 16), (2, 6, 8), (8, 8, 1))
NPAIR = sum(n * w for _, n, w in PAIRS)
TB = 32
NB = T // TB
GRID_W = 64
WINDOWS = (2, 4, 8, 16)
LOWEST = -3.0e38
MLA_SCALE = 128.0 ** -0.5
WIN_SCALE = 64.0 ** -0.5

Q0, K0, V0, R0, CQ0, CKV0, GL0, KR0, EVEN_W = 0, 256, 512, 1024, 1536, 1792, 2048, 2080, 2144
EVEN_CHUNKS = [(0, 512), (512, 512), (1024, 512), (1536, 512), (2048, 96)]
XC0, QD0, KD0, VD0, ODD_W = 0, 512, 1024, 1152, 1280
ODD_CHUNKS = [(0, 512), (512, 512), (1024, 256)]

C_ID, C_IOTA, C_CUM, C_REST, C_IND, C_SEL, C_ROPE, C_MASK = 0, 128, 256, 512, 768, 770, 1026, 1538
C_ONE, C_START = 2050, 2052
C_N = 2068
(S_C, S_GN, S_CKV, S_CQ, S_QN, S_KN, S_GO, S_WQN, S_WKN, S_SINK, S_PS) = (
    0, 16, 48, 304, 560, 688, 816, 817, 881, 945, 953)
S_N = 957


def build_program(nc, a):
    ctx = ExitStack()
    with ctx:
        def sb(name, shape, dt=F32):
            return ctx.enter_context(nc.sbuf_tensor(name, shape, dt))

        def R(ap):
            return ap.bitcast(F32R)

        start = {}

        def at_known_place(name, shape):
            t = sb(name, shape)
            start[name] = nc.sbuf_base - 4 * int(np.prod(shape[1:]))
            return t

        def rounded(name, shape, within, word):
            return nc.alloc_sbuf_tensor_at(name, shape, F32, offset=start[within] + 4 * word)

        const = sb("const", [P, C_N])
        vecs = sb("vecs", [P, S_N])
        x = sb("x", [P, NT, D])
        hT = at_known_place("hT", [P, KD, T])
        gate = at_known_place("gate", [P, 2, 2, D])
        ring = at_known_place("ring", [P, 4, 4096])
        arena = at_known_place("arena", [P, 16384])
        silu_c = sb("silu_c", [P, KD, 2])
        ada_col = sb("ada_col", [P, 2, 2, KD, 2])
        mod = sb("mod", [P, 2, KD, 2])
        stat = sb("stat", [P, 64])
        sums = sb("sums", [P, NH])
        sinks = sb("sinks", [P, NH])
        sums40 = sb("sums40", [P, NT * NH])[:, :]
        tmp_i = sb("tmp_i", [P, NT, TOPK], U32)
        bank = [ctx.enter_context(nc.psum_tensor(f"bank{i}", [P, 512], F32)) for i in range(4)]
        pair = ctx.enter_context(nc.psum_tensor("pair", [P, 4, 512], F32))

        starts = const[:, C_START:C_START + TOPK]
        ident = const[:, C_ID:C_ID + P]
        iota = const[:, C_IOTA:C_IOTA + P]
        cum = [const[:, C_CUM + P * i:C_CUM + P * (i + 1)] for i in range(2)]
        rest = [const[:, C_REST + P * i:C_REST + P * (i + 1)] for i in range(2)]
        ind = const[:, C_IND:C_IND + 2]
        rope = const[:, C_ROPE:C_ROPE + 512].rearrange("p (t s d) -> p t s d", t=4, s=2)
        wmask = const[:, C_MASK:C_MASK + 512]

        def views(base, *sizes):
            out, at = [], base
            for n in sizes:
                out.append(arena[:, at:at + n])
                at += n
            assert at <= 16384
            return out

        bias_rows, ada_rows = views(12288, 1024, 1024)
        bias_next, rows_next = (gate[:, 0, c, :] for c in range(2))
        xn0, xn1, junk = views(8192, 1024, 1024, 1024)
        pe_ = arena[:, 0:NT * EVEN_W].rearrange("p (t n) -> p t n", t=NT)
        (eb, en, es, kiT, attT, glT, sq5, wgu) = views(
            NT * EVEN_W, 512, 512, 512, 512, 1024, T, 512, 512)
        idle = hT[:, :, :].rearrange("p k t -> p (k t)")
        la, exps = idle[:, 0:NT * 512].rearrange("p (t n) -> p t n", t=NT), [
            (eb, en, es), tuple(idle[:, NT * 512 + 512 * i:NT * 512 + 512 * i + 512] for i in range(3))]
        zb = [idle[:, NT * 512 + 1536 + 512 * i:NT * 512 + 2048 + 512 * i] for i in range(2)]
        attT = attT.rearrange("p (r d q n) -> p r d q n", r=2, d=2, q=2)
        scan_cur = views(NT * EVEN_W + 2048, 512, 512)
        s_out = es.rearrange("p (d n) -> p d n", d=2)
        spare = ring[:, 2:4, :].rearrange("p a b -> p (a b)")
        upd = spare[:, 0:5120].rearrange("p (c d n) -> p c d n", c=10, d=2)
        qdT = spare[:, 5120:7680].rearrange("p (t q n) -> p t q n", t=NT, q=4)
        s_in = spare[:, 7680:8192].rearrange("p (d n) -> p d n", d=2)
        decay = sb("decay", [P, NT, 2, 2, 2])
        kT = spare[:, 0:6144].rearrange("p (h n) -> p h n", h=NH)
        probs = spare[:, 6144:7424].rearrange("p (b n) -> p b n", b=2)
        ckvT = spare[:, 7424:7680]
        ctx_ckv = spare[:, 7680:7936]
        ctx_kr = spare[:, 7936:8000]
        krr = spare[:, 8000:8064]
        krt = spare[:, 8064:8128]
        vals, qk, qT, att_o = views(NT * EVEN_W, 6 * 512, 1024, 1024, 512)
        vals = vals.rearrange("p (t n) -> p t n", t=6)
        sq10 = arena[:, 0:1024]
        pT = arena[:, EVEN_W:EVEN_W + 1280].rearrange("p (b n) -> p b n", b=2)
        po_ = arena[:, 0:NT * ODD_W].rearrange("p (t n) -> p t n", t=NT)
        (yT, kT2, k2, qn, qT2, soft_s, probs2, pT2, kctx, vctx, sqo, att_o2) = views(
            NT * ODD_W, 1280, 1536, 256, 512, 512, 1024, 1024, 1024, 128, 128, 512, 512)
        yT = yT.rearrange("p (b n) -> p b n", b=2)
        kT2 = kT2.rearrange("p (v n) -> p v n", v=2)
        soft_s = soft_s.rearrange("p (b n) -> p b n", b=2)
        probs2 = probs2.rearrange("p (b n) -> p b n", b=2)
        pT2 = pT2.rearrange("p (b n) -> p b n", b=2)
        (pickT, top_v, top_i, subk, qsT, cand, cand_cut, fin_v, fin_p, hot, pick, place, place_u, past, steps) = views(
            0, 3 * T, 1280, 1280, 2048, 1280, NT * NPAIR, NT * P, 640, 640, NT * 256, 1920, 80, 80, 80, 80)
        pickT = pickT.rearrange("p (k t) -> p k t", k=3)
        top_v5 = top_v.rearrange("p (t h c k) -> p t h c k", t=NT, h=NH, c=2)
        top_i5 = top_i.rearrange("p (t h c k) -> p t h c k", t=NT, h=NH, c=2)
        subk = subk.rearrange("p (g n) -> p g n", g=16)
        qsT = qsT.rearrange("p (b t) -> p b t", b=2)
        fin_v4 = fin_v.rearrange("p (t h k) -> p t h k", t=NT, h=NH)
        pick3 = pick.rearrange("p (w t n) -> p w t n", w=3, t=NT)
        hot = hot.rearrange("p (t k n) -> p t k n", t=NT, k=TOPK)
        cand, cand_cut = (c.rearrange("p (t n) -> p t n", t=NT) for c in (cand, cand_cut))
        place, past, steps = (b.rearrange("p (t k) -> p t k", t=NT) for b in (place, past, steps))
        place_u = place_u.bitcast(U32).rearrange("p (t k) -> p t k", t=NT)
        (stage, hots, cols) = views(1920, 8192, 4096, 192)
        stage = stage.rearrange("p (b j t) -> p b j t", b=2, j=P)
        hots = hots.rearrange("p (b c q n) -> p b c q n", b=4, c=2, q=4)
        cols = cols.rearrange("p (b k t) -> p b k t", b=2, k=3)
        acc, _, _, gmat = views(0, NT * D, KD * T, 2 * GROUP * T, RGROUP * T)
        acc = acc.rearrange("p (t d) -> p t d", t=NT)
        h_hi = rounded("h_hi", [P, KD, T], "arena", NT * D)
        h_lo = rounded("h_lo", [P, KD, T], "hT", 0)
        act_hi = [rounded(f"act_hi{b}", [P, GROUP, T], "arena", NT * D + KD * T + GROUP * T * b) for b in range(2)]
        act_raw = [gate[:, 0].rearrange("p c d -> p (c d)")[:, 0:GROUP * T].rearrange("p (j t) -> p j t", j=GROUP),
                   at_known_place("act_raw1", [P, GROUP, T])]
        act_lo = [rounded("act_lo0", [P, GROUP, T], "gate", 0), rounded("act_lo1", [P, GROUP, T], "act_raw1", 0)]
        gmat = gmat.rearrange("p (k j t) -> p k j t", k=NB, j=RGROUP)
        u_raw = [ring[:, 2 * b, 0:GROUP * D] for b in range(2)]
        v_raw = [ring[:, 2 * b + 1, 0:GROUP * D] for b in range(2)]
        u_lo, u_hi = ([rounded(f"u_{part}{b}", [P, GROUP * D], "ring", 2 * b * 4096 + at) for b in range(2)]
                      for part, at in (("lo", 0), ("hi", GROUP * D)))
        v_lo, v_hi = ([rounded(f"v_{part}{b}", [P, GROUP * D], "ring", (2 * b + 1) * 4096 + at) for b in range(2)]
                      for part, at in (("lo", 0), ("hi", GROUP * D)))

        names = """
        const_in x_in bias_in0 bias_in1 bias_in2 bias_in3 slot_in0 slot_in1 slot_in2 slot_in3
        wgu_in s_in_in ctx_in kvctx_in subk_in
        silu_done row_ready row_out0 row_out1 cols_in gates_in mods_done ss_ready var_ready std_ready xn_ready
        z_part z_exp la_ready exps_mul ctx_state s_ready oa_ready
        ckv_ready k_ready q_ready m_ready p_ready es_ready x_done
        d_full d_free a_full a_free s_full s_free
        gate_in gate_exp pick_ready cols_ready hot_ready gated_a gated_p g_full g_free stage_out0 stage_out1
        u_in0 u_in1 v_in0 v_in1 g_in h_led h_split u_led u_split v_led v_split
        h_full gelu_done act_made act_led act_ready o_full o_free
        out_state out_cache out_y chain_v chain_a
        """.split()
        sem = {n: ctx.enter_context(nc.semaphore(n)) for n in names}
        total = {}

        class Turn:

            def __init__(self, eng, chain=None):
                self.eng, self.n, self.chain = eng, {}, chain

            def next(self, name):
                self.n[name] = self.n.get(name, 0) + 1
                return self.n[name]

            def due(self, name, step=1):
                return sem[name], self.next(name) * step

            def after(self, name, k):
                if k > 0:
                    self.eng.wait_ge(sem[name], k)

            def give(self, ins, name):
                ins.then_inc(sem[name], 1)
                total[name] = total.get(name, 0) + 1
                self.eng.wait_ge(sem[name], total[name])

            def link(self, ins):
                self.give(ins, self.chain)

        def bc(ap, n, at):
            ap = ap.unsqueeze(at)
            shape = [int(s) for s in ap.shape]
            shape[at] = n
            return ap.broadcast_to(shape)

        freed = {}
        marks = {}
        items = []
        per_layer = []

        for l in range(LAYERS):
            if l == 0:
                items += [a["w_ada"][l, n] for n in range(12)]
            items += [a[f"w_in{l}_{n}"] for n in range(5 if l == 0 else 3)]
            items += [a["w_mla"] if l == 0 else a["w_band"]]
            items += [a[f"w_out{l}"][n] for n in range(2)]
            items += [a["peer_wq"][l, n] for n in range(4)]
            per_layer.append(len(items))
        freed_next = []
        mod_rows = nc.dram_tensor("mod_rows", (2, 6 * D), F32, kind="Internal").ap()
        routing = nc.dram_tensor("routing", (NR, P, NB, RGROUP, TB), F32, kind="Internal").ap()

        def window_tiles(qt):
            return [0] if qt == 0 else [t for t in (qt - 1, qt, qt + 1) if 1 <= t < NT] + [5]

        block = ctx.enter_context(nc.Block())

        @block.tensor
        def _(pe):
            me = Turn(pe)
            mm = nc.tensor.matmul
            tr = nc.tensor.transpose
            item = [0]

            def slot():
                n = item[0]
                item[0] += 1
                pe.wait_ge(sem[f"slot_in{n % 2}"], 16 * (n // 2 + 1))
                return ring[:, n % 2, :]

            def slot_done():
                freed[item[0] - 1] = (last_stream[0], me.n[last_stream[0]])

            def mark(name):
                marks[name] = dict(me.n)

            def copied():
                pe.wait_ge(sem["d_free"], me.n["d_full"])
                pe.wait_ge(sem["a_free"], me.n["a_full"])

            last_stream = ["d_full"]

            def open_d():
                n = me.next("d_full") - 1
                me.after("d_free", n - 1)
                last_stream[0] = "d_full"
                return bank[n % 2]

            def open_a():
                n = me.next("a_full") - 1
                me.after("a_free", n - 1)
                last_stream[0] = "a_full"
                return bank[2 + n % 2]

            def open_s():
                n = me.next("s_full") - 1
                me.after("s_free", n - 1)
                return pair[:, 2 * (n % 2):2 * (n % 2) + 2, :]

            def modulation(out, w, bias, arrived):
                for k in range(KD):
                    mm(out[0:2, :], silu_c[:, k, :], w[:, k, :], start=(k == 0), stop=False)
                pe.wait_ge(*arrived)
                return mm(out[0:2, :], const[0:1, C_ONE:C_ONE + 2], bias, start=False, stop=True)

            def next_modulation(n):
                pe.wait_ge(sem[f"slot_in{2 + n % 2}"], 16 * (n // 2 + 1))
                modulation(open_a(), ring[:, 2 + n % 2, :].rearrange("p (k n) -> p k n", k=KD),
                           bias_next[0:1, 512 * (n % 2):512 * (n % 2) + 512],
                           (sem[f"bias_in{2 + n % 2}"], 16 * (n // 2 + 1))).then_inc(sem["a_full"], 1)
                freed_next.append(me.n["a_full"])

            def ada():
                row_at = {}

                def spread(n):
                    row = ada_rows[0:2, 512 * (n % 2):512 * (n % 2) + 512]
                    pe.wait_ge(sem["d_free"], row_at[n])
                    if n // 2 in (2, 5):
                        for c in range(2):
                            mm(open_a()[:, :], const[0:2, C_SEL + P * c:C_SEL + P * (c + 1)], row,
                               start=True, stop=True).then_inc(sem["a_full"], 1)
                    else:
                        out = open_d()
                        for k in range(4):
                            last = tr(out[:, 2 * k:2 * k + 2], row[:, P * k:P * (k + 1)], ident[0:2, 0:2])
                        last.then_inc(sem["d_full"], 1)

                pe.wait_ge(*me.due("silu_done"))
                pe.wait_ge(sem["const_in"], 32)
                for n in range(12):
                    w = slot().rearrange("p (k n) -> p k n", k=KD)
                    out = open_d()
                    half = slice(512 * (n % 2), 512 * (n % 2) + 512)
                    modulation(out, w, bias_rows[0:1, half],
                               (sem[f"bias_in{n % 2}"], 16 * (n // 2 + 1))).then_inc(sem["d_full"], 1)
                    slot_done()
                    row_at[n] = me.n["d_full"]
                    if n:
                        spread(n - 1)
                spread(11)

            def norm(l, s):
                for t in range(NT):
                    pe.wait_ge(*me.due("xn_ready"))
                    xn = (xn0, xn1)[t % 2]
                    out = open_a()
                    for k in range(4, 8):
                        last = tr(out[:, P * (k - 4):P * (k - 3)], xn[:, P * k:P * (k + 1)], ident)
                    last.then_inc(sem["a_full"], 1)
                    out = open_d()
                    for k in range(4):
                        last = tr(out[:, P * k:P * (k + 1)], xn[:, P * k:P * (k + 1)], ident)
                    last.then_inc(sem["d_full"], 1)

            def project(chunks):
                copied()
                for n, (_, w) in enumerate(chunks):
                    weights = slot()[:, 0:KD * w].rearrange("p (k n) -> p k n", k=KD)
                    for t in range(NT):
                        to_d = (n * NT + t) % 2 == 0 and n != 2
                        out = open_d() if to_d else open_a()
                        for k in range(KD):
                            last = mm(out[:, 0:w], hT[:, k, P * t:P * (t + 1)], weights[:, k, :],
                                      start=(k == 0), stop=(k == KD - 1))
                        last.then_inc(sem["d_full" if to_d else "a_full"], 1)
                    slot_done()
                mark(("proj", layer[0]))

            def gla():
                copied()
                pe.wait_ge(sem["wgu_in"], 16)
                for tiles in ((0, 1, 2, 3), (4,)):
                    out = open_d()
                    for i, t in enumerate(tiles):
                        last = tr(out[0:32, P * i:P * (i + 1)], pe_[:, t, GL0:GL0 + 32], ident)
                    last.then_inc(sem["d_full"], 1)
                pe.wait_ge(sem["d_free"], me.n["d_full"])
                for t in range(NT):
                    mm(open_d()[:, :], glT[0:33, P * t:P * (t + 1)], wgu[0:33, :],
                       start=True, stop=True).then_inc(sem["d_full"], 1)

                def decays(t):
                    pe.wait_ge(*me.due("la_ready"))
                    for mats in (cum, rest):
                        out = open_a()
                        for d in range(2):
                            last = mm(out[:, 256 * d:256 * d + 256], mats[d], la[:, t, 256 * d:256 * d + 256],
                                      start=True, stop=True)
                        last.then_inc(sem["a_full"], 1)
                    out = open_a()
                    for d in range(2):
                        for q in range(2):
                            last = mm(out[:, 4 * d + 2 * q:4 * d + 2 * q + 2],
                                      la[:, t, 256 * d + P * q:256 * d + P * (q + 1)], ind, start=True, stop=True)
                    last.then_inc(sem["a_full"], 1)
                    mark(("exps", t))

                decays(0)
                for t in range(NT):
                    pt = pe_[:, t, :]
                    eb, en, es = exps[t % 2]
                    if t + 1 < NT:
                        decays(t + 1)
                    pe.wait_ge(*me.due("exps_mul"))
                    for src, opened, full in ((eb, open_d, "d_full"), (en, open_a, "a_full")):
                        out = opened()
                        for q in range(4):
                            last = tr(out[:, P * q:P * (q + 1)], src[:, P * q:P * (q + 1)], ident)
                        last.then_inc(sem[full], 1)
                    copied()
                    out = open_s()
                    for r in range(2):
                        for d in range(2):
                            for q in range(2):
                                h = slice(64 * r, 64 * r + 64)
                                last = mm(out[:, r, 256 * d + P * q:256 * d + P * (q + 1)],
                                          kiT[h, P * (2 * d + q):P * (2 * d + q + 1)],
                                          qdT[h, t, 2 * d + q, :], start=True, stop=True)
                    last.then_inc(sem["s_full"], 1)
                    out = open_s()
                    for c in range(2):
                        for d in range(2):
                            for h in range(4):
                                r, q = h % 2, h // 2
                                last = mm(out[64 * r:64 * r + 64, c, 256 * d + P * q:256 * d + P * (q + 1)],
                                          es[64 * c:64 * c + 64, 256 * d + 64 * h:256 * d + 64 * h + 64],
                                          pt[64 * c:64 * c + 64, V0 + P * h:V0 + P * (h + 1)],
                                          start=True, stop=True)
                    last.then_inc(sem["s_full"], 1)
                    pe.wait_ge(sem["s_free"], me.n["s_full"] - 1)
                    out = open_d()
                    for h in range(4):
                        for d in range(2):
                            last = mm(out[:, P * h:P * (h + 1)], attT[:, h % 2, d, h // 2, :],
                                      pt[:, V0 + P * h:V0 + P * (h + 1)], start=(d == 0), stop=(d == 1))
                    last.then_inc(sem["d_full"], 1)
                mark("gla_tiles")
                pe.wait_ge(*me.due("s_ready"))
                for t in range(NT):
                    out = open_s()
                    for c in range(2):
                        for r in range(2):
                            for q in range(2):
                                for d in range(2):
                                    h = slice(64 * r, 64 * r + 64)
                                    last = mm(out[64 * c:64 * c + 64, r, P * q:P * (q + 1)],
                                              qdT[h, t, 2 * d + q, 64 * c:64 * c + 64],
                                              upd[h, 2 * t + c, d, P * q:P * (q + 1)],
                                              start=(d == 0 and q == 0), stop=(d == 1), skip_group_check=True)
                    last.then_inc(sem["s_full"], 1)
                for t in range(NT):
                    pe.wait_ge(*me.due("oa_ready"))
                    out = open_a()
                    for h in range(4):
                        last = tr(out[:, P * h:P * (h + 1)], pe_[:, t, P * h:P * (h + 1)], ident)
                    last.then_inc(sem["a_full"], 1)
                mark("oa")

            def attend(q_lhs, keys):
                out = open_s().rearrange("p a b -> p (a b)")
                for k_ap, at, n in keys:
                    last = mm(out[:, at:at + n], q_lhs, k_ap, start=(at % 512 == 0), stop=True, skip_group_check=True)
                last.then_inc(sem["s_full"], 1)

            def heads(scores, probs_of, pT_of, tiles, v_of, between=None):
                n = len(tiles)
                turned = {}

                def turn(h):
                    pe.wait_ge(*me.due("p_ready"))
                    out = open_d()
                    for i in range(min(n, 4)):
                        last = tr(out[:, P * i:P * (i + 1)], probs_of(h)[:, P * i:P * (i + 1)], ident)
                    last.then_inc(sem["d_full"], 1)
                    if n > 4:
                        tr(open_a()[:, 0:P], probs_of(h)[:, 4 * P:5 * P], ident).then_inc(sem["a_full"], 1)
                    turned[h] = dict(me.n)

                def product(h):
                    pe.wait_ge(sem["d_free"], turned[h]["d_full"])
                    if n > 4:
                        pe.wait_ge(sem["a_free"], turned[h]["a_full"])
                    out = open_d()
                    for i, kt in enumerate(tiles):
                        last = mm(out[:, 0:64], pT_of(h)[:, P * i:P * (i + 1)], v_of(kt, h), start=(i == 0), stop=(i == n - 1))
                    last.then_inc(sem["d_full"], 1)

                scores(0)
                scores(1)
                turn(0)
                for h in range(NH):
                    if h + 2 < NH:
                        scores(h + 2)
                    if h + 1 < NH:
                        turn(h + 1)
                    product(h)
                    if between:
                        between(h)

            def mla():
                w = slot()
                w_uq = w[:, 0:2048].rearrange("p (k n) -> p k n", k=2)
                w_uk = w[:, 2048:3072].rearrange("p (k n) -> p k n", k=2)
                w_uv = w[:, 3072:4096].rearrange("p (k n) -> p k n", k=2)
                def keys_and_values(kt):
                    pe.wait_ge(*(me.due("ckv_ready") if kt < NT else (sem["ctx_in"], 32)))
                    ckv = pe_[:, kt, CKV0:CKV0 + 256] if kt < NT else ctx_ckv
                    out = open_d()
                    for k in range(2):
                        last = tr(out[:, P * k:P * (k + 1)], ckv[:, P * k:P * (k + 1)], ident)
                    last.then_inc(sem["d_full"], 1)
                    pe.wait_ge(sem["d_free"], me.n["d_full"])
                    for wk, opened, full in ((w_uk, open_d, "d_full"), (w_uv, open_a, "a_full")):
                        out = opened()
                        for k in range(2):
                            last = mm(out[:, :], ckvT[:, P * k:P * (k + 1)], wk[:, k, :], start=(k == 0), stop=(k == 1))
                        last.then_inc(sem[full], 1)

                keys_and_values(0)
                for kt in range(6):
                    if kt + 1 < 6:
                        keys_and_values(kt + 1)
                    pe.wait_ge(*me.due("k_ready"))
                    for g in range(2):
                        out = open_a()
                        for i in range(4):
                            h = 4 * g + i
                            last = tr(out[:, P * i:P * (i + 1)], qk[:, P * h:P * (h + 1)], ident)
                        last.then_inc(sem["a_full"], 1)
                    mark(("keys", kt))
                copied()
                turned_at = {}

                def queries(qt, part):
                    if part == 0:
                        pe.wait_ge(*me.due("ckv_ready"))
                        out = open_d()
                        for k in range(2):
                            last = tr(out[:, P * k:P * (k + 1)], pe_[:, qt, CQ0 + P * k:CQ0 + P * (k + 1)], ident)
                        last.then_inc(sem["d_full"], 1)
                        turned_at[qt] = me.n["d_full"]
                    elif part < 3:
                        at = 512 * (part - 1)
                        pe.wait_ge(sem["d_free"], turned_at[qt])
                        out = open_d()
                        for k in range(2):
                            last = mm(out[:, :], ckvT[:, P * k:P * (k + 1)], w_uq[:, k, at:at + 512],
                                      start=(k == 0), stop=(k == 1))
                        last.then_inc(sem["d_full"], 1)
                        if qt == NT - 1 and part == 2:
                            slot_done()

                for part in range(3):
                    queries(0, part)
                for qt in range(NT):
                    pe.wait_ge(*me.due("q_ready"))
                    for g in range(2):
                        out = open_a()
                        for i in range(4):
                            h = 4 * g + i
                            last = tr(out[:, P * i:P * (i + 1)], qk[:, P * h:P * (h + 1)], ident)
                        last.then_inc(sem["a_full"], 1)
                    copied()
                    tiles = [0] if qt == 0 else [1, 2, 3, 4, 5]
                    mark(("scores", qt))

                    def scores(h):
                        q_lhs = qT[:, P * h:P * (h + 1)]
                        if qt == 0:
                            attend(q_lhs, [(kT[:, h, 0:P], 0, P)])
                        else:
                            attend(q_lhs, [(kT[:, h, P:P + 512], 0, 512), (kT[:, h, P + 512:P + 640], 512, P)])

                    heads(scores, lambda h: probs[:, h % 2, :], lambda h: pT[:, h % 2, :], tiles,
                          lambda kt, h: vals[:, kt, 64 * h:64 * h + 64],
                          (lambda h: queries(qt + 1, h)) if qt + 1 < NT else None)
                    turn_out()

            def turn_out():
                copied()
                out = open_a()
                src = att_o if layer[0] == 0 else att_o2
                for i in range(4):
                    last = tr(out[:, P * i:P * (i + 1)], src[:, P * i:P * (i + 1)], ident)
                last.then_inc(sem["a_full"], 1)

            def odd():
                copied()
                w = slot()
                band = w[:, 0:3072].rearrange("p (g b n) -> p g b n", g=4, b=6)
                w_pool = w[:, 3072:3584].rearrange("p (g n) -> p g n", g=4)
                for g in range(4):
                    xc = [po_[:, t, XC0 + P * g:XC0 + P * (g + 1)] for t in range(NT)]
                    near = {0: [(0, 0)], 1: [(1, 1), (2, 5)], 2: [(1, 4), (2, 2), (3, 5)],
                            3: [(2, 4), (3, 2), (4, 5)], 4: [(3, 4), (4, 3)]}
                    out = open_d()
                    mm(out[:, 0:P], xc[0], band[:, g, 0, :], start=True, stop=True).then_inc(sem["d_full"], 1)
                    out = open_d()
                    for t in range(1, NT):
                        for i, (u, b) in enumerate(near[t]):
                            last = mm(out[:, P * (t - 1):P * t], xc[u], band[:, g, b, :],
                                      start=(i == 0), stop=(i == len(near[t]) - 1))
                    last.then_inc(sem["d_full"], 1)
                    pe.wait_ge(sem["d_free"], me.n["d_full"])
                    for at, n in ((0, 512), (512, P)):
                        mm(open_a()[:, 0:n], w_pool[:, g, :], yT[:, g % 2, at:at + n],
                           start=True, stop=True).then_inc(sem["a_full"], 1)
                slot_done()
                for kt in range(6):
                    pe.wait_ge(*me.due("k_ready"))
                    out = open_a()
                    for v in range(2):
                        last = tr(out[:, P * v:P * (v + 1)], k2[:, P * v:P * (v + 1)], ident)
                    last.then_inc(sem["a_full"], 1)
                    mark(("odd_k", kt))
                pe.wait_ge(sem["kvctx_in"], 32)
                for qt in range(NT):
                    pe.wait_ge(*me.due("q_ready"))
                    out = open_a()
                    for i in range(4):
                        last = tr(out[:, P * i:P * (i + 1)], qn[:, P * i:P * (i + 1)], ident)
                    last.then_inc(sem["a_full"], 1)
                    copied()
                    tiles = window_tiles(qt)

                    def scores(h):
                        part = slice(64 * (h % 2), 64 * (h % 2) + 64)
                        q_lhs = qT2[part, P * (h // 2):P * (h // 2 + 1)]
                        local = [t for t in tiles if t < NT]
                        keys = [(kT2[part, h // 4, P * local[0]:P * (local[-1] + 1)], 0, P * len(local))]
                        if qt:
                            keys.append((kT2[part, h // 4, P * 5:P * 6], P * len(local), P))
                        attend(q_lhs, keys)

                    heads(scores, lambda h: probs2[:, h % 2, :], lambda h: pT2[:, h % 2, :], tiles,
                          lambda kt, h: (po_[:, kt, VD0 + 64 * (h // 4):VD0 + 64 * (h // 4) + 64] if kt < NT
                                         else vctx[:, 64 * (h // 4):64 * (h // 4) + 64]))
                    turn_out()

            def out_project():
                copied()
                for n in range(2):
                    w = slot().rearrange("p (k n) -> p k n", k=KD)
                    for t in range(NT):
                        out = open_d()
                        for k in range(KD):
                            last = mm(out[:, :], hT[:, k, P * t:P * (t + 1)], w[:, k, :], start=(k == 0), stop=(k == KD - 1))
                        last.then_inc(sem["d_full"], 1)
                    slot_done()

            def route(l):
                copied()
                pe.wait_ge(sem["subk_in"], 16 * (l + 1))
                for g in range(16):
                    if g % 4 == 0:
                        w = slot().rearrange("p (k n) -> p k n", k=KD)
                    for at, n in ((0, 512), (512, P)):
                        out = open_a()
                        for k in range(KD):
                            last = mm(out[:, 0:n], w[:, k, P * (g % 4):P * (g % 4 + 1)], hT[:, k, at:at + n],
                                      start=(k == 0), stop=(k == KD - 1))
                        last.then_inc(sem["a_full"], 1)
                    if g % 4 == 3:
                        slot_done()
                    pe.wait_ge(sem["a_free"], me.n["a_full"])
                    out = open_s()
                    for t in range(NT):
                        last = mm(out[:, t // 4, P * (t % 4):P * (t % 4 + 1)], qsT[:, g % 2, P * t:P * (t + 1)],
                                  subk[:, g, :], start=True, stop=True)
                    last.then_inc(sem["s_full"], 1)
                    if l == 0 and 0 <= g - 2 < 12:
                        next_modulation(g - 2)
                pe.wait_ge(*me.due("pick_ready"))
                for t in range(NT):
                    out = open_d()
                    for w3 in range(3):
                        last = tr(out[:, P * w3:P * (w3 + 1)], pick3[:, w3, t, :], ident)
                    last.then_inc(sem["d_full"], 1)

            def routing_matrix(l):
                jobs = TB // 4
                with pe.Fori(0, NB // 2) as i:
                    for n in range(2 * jobs):
                        at = l * (NB * jobs) + n
                        pe.wait_ge(sem["gated_a"], i * (2 * jobs) + (at + 1))
                        pe.wait_ge(sem["gated_p"], i * (2 * jobs) + (at + 1))
                        pe.wait_ge(sem["g_free"], i * (2 * jobs) + (at + G_AHEAD - 3))
                        for q in range(4):
                            last = mm(pair[:, n % 4, P * q:P * (q + 1)], hots[:, n % 4, 0, q, :], hots[:, n % 4, 1, q, :],
                                      start=True, stop=True)
                        last.then_inc(sem["g_full"], 1)

            def dense(l):
                def experts(b, n):
                    pe.wait_ge(sem["u_split"], n)
                    for j in range(GROUP):
                        for half, (at, w) in enumerate(HALVES):
                            m = 2 * j + half
                            pe.wait_ge(sem["gelu_done"], (n - 1) * (2 * GROUP) + (m + 1))
                            for k in range(KD):
                                for i, (u, h) in enumerate(((u_hi, h_hi), (u_hi, h_lo), (u_lo, h_hi))):
                                    last = mm(pair[:, m % 4, 0:w], R(u[b][:, P * (KD * j + k):P * (KD * j + k + 1)]), R(h[:, k, at:at + w]),
                                              start=(k == 0 and i == 0), stop=(k == KD - 1 and i == 2))
                            last.then_inc(sem["h_full"], 1)

                def values(b, n):
                    pe.wait_ge(sem["v_split"], n)
                    pe.wait_ge(sem["act_ready"], n * GROUP)
                    for m in range(2 * NT):
                        t, half = m // 2, m % 2
                        pe.wait_ge(sem["o_free"], (n - 1) * (2 * NT) + (m + 1))
                        for j in range(GROUP):
                            for i, (w, v) in enumerate(((act_hi, v_hi), (act_hi, v_lo), (act_lo, v_hi))):
                                last = mm(bank[(2 * b + m) % 4][:, :], R(w[b][:, j, P * t:P * (t + 1)]),
                                          R(v[b][:, D * j + 512 * half:D * j + 512 * half + 512]),
                                          start=(j == 0 and i == 0), stop=(j == GROUP - 1 and i == 2))
                        last.then_inc(sem["o_full"], 1)

                n0 = l * NG + 1
                pe.wait_ge(sem["g_free"], G_AHEAD + (l + 1) * T // 4)
                pe.wait_ge(sem["h_split"], KD * (l + 1))
                experts(0, n0)
                with pe.Fori(0, NG // 2 - 1) as i:
                    experts(1, i * 2 + (n0 + 1))
                    values(0, i * 2 + n0)
                    experts(0, i * 2 + (n0 + 2))
                    values(1, i * 2 + (n0 + 1))
                experts(1, n0 + NG - 1)
                values(0, n0 + NG - 2)
                values(1, n0 + NG - 1)

            pe.sem_inc(sem["g_full"], 4)
            pe.sem_inc(sem["o_full"], 1)
            layer = [0]
            for l in range(LAYERS):
                layer[0] = l
                if l == 0:
                    ada()
                else:
                    pe.wait_ge(sem["o_free"], 4 + 2 * NT * NG * l)
                norm(l, 0)
                if l == 0:
                    project(EVEN_CHUNKS)
                    gla()
                    mla()
                else:
                    project(ODD_CHUNKS)
                    odd()
                out_project()
                norm(l, 1)
                route(l)
                routing_matrix(l)
                dense(l)

        @block.scalar
        def _(act):
            me = Turn(act, "chain_a")
            do = nc.scalar.activation
            link, give = me.link, me.give

            def take_a():
                n = me.next("a_full")
                act.wait_ge(sem["a_full"], n)
                return bank[2 + (n - 1) % 2]

            def copy_a(dst, w=512, func=ACT.Copy, **how):
                out = take_a()
                src = out[0:int(dst.shape[0]), 0:w]
                if len(dst.shape) == 3:
                    src = src.rearrange("p (k n) -> p k n", k=int(dst.shape[1]))
                give(do(dst, src, func, **how), "a_free")

            def signal(name):
                act.sem_inc(sem[name], 1)

            def root(n, at):
                act.wait_ge(*me.due("var_ready"))
                give(do(stat[:, at:at + n], stat[:, at:at + n], ACT.Sqrt), "std_ready")

            def ada():
                for kind in (2, 5):
                    for n in range(2):
                        for c in range(2):
                            copy_a(gate[:, kind // 3, c, 512 * n:512 * n + 512])

            def norm_sums(l, s):
                if l == 0 and s == 0:
                    act.wait_ge(sem["x_in"], 16)
                else:
                    act.wait_ge(*me.due("x_done"))
                for t in range(NT):
                    ins = do(junk, x[:, t, :], ACT.Square, accum_out=stat[:, t:t + 1])
                    if t < NT - 1:
                        link(ins)
                give(ins, "ss_ready")
                root(NT, 0)

            def norm(l, s):
                if l or s:
                    norm_sums(l, s)
                act.wait_ge(*me.due("mods_done"))
                for t in range(NT):
                    c = int(t > 0)
                    out = take_a()
                    for k in range(4, 8):
                        ins = do(hT[:, k, P * t:P * (t + 1)], out[:, P * (k - 4):P * (k - 3)], ACT.Identity,
                                 bias=ada_col[:, s, 0, k, c:c + 1], scale=mod[:, s, k, c:c + 1])
                    give(ins, "a_free")

            def project(chunks, dst):
                for n, (at, w) in enumerate(chunks):
                    for t in range(NT):
                        if not ((n * NT + t) % 2 == 0 and n != 2):
                            copy_a(dst[:, t, at:at + w], w, ACT.Silu if at == R0 and dst is pe_ else ACT.Copy)

            def gla():
                for t in range(NT):
                    act.wait_ge(*me.due("z_part"))
                    z = zb[t % 2]
                    link(do(z, z, ACT.Exp, scale=-1.0))
                    give(do(z, z, ACT.Ln, bias=1.0), "z_exp")

                def decays(t):
                    eb, en, es = exps[t % 2]
                    out = take_a()
                    do(eb, out[:, :], ACT.Exp)
                    give(do(en, out[:, :], ACT.Exp, scale=-1.0), "a_free")
                    out = take_a()
                    give(do(es, out[:, :], ACT.Exp), "a_free")
                    out = take_a()
                    give(do(decay[:, t].rearrange("p d q c -> p (d q c)"), out[:, 0:8], ACT.Exp), "a_free")

                decays(0)
                for t in range(NT):
                    if t + 1 < NT:
                        decays(t + 1)
                    copy_a(kiT)
                for t in range(NT):
                    root(4, 8)
                for t in range(NT):
                    copy_a(hT[:, 0:4, P * t:P * (t + 1)], scale=vecs[:, S_GO:S_GO + 1])

            def mla():
                root(2 * NT, 50)
                me.after("out_state", 64)
                copy_a(vals[:, 0, :])
                for kt in range(6):
                    if kt + 1 < 6:
                        copy_a(vals[:, kt + 1, :])
                    root(8, 24)
                    for g in range(2):
                        copy_a(kT[:, 4 * g:4 * g + 4, P * kt:P * (kt + 1)])
                root(8, 24)
                for qt in range(NT):
                    for g in range(2):
                        copy_a(qT[:, 512 * g:512 * g + 512])
                    n = P if qt == 0 else 5 * P

                    def soften(h):
                        act.wait_ge(*me.due("m_ready"))
                        at = 2 * ((marks[("scores", qt)]["s_full"] + h) % 2)
                        out = pair[:, at:at + 2, :].rearrange("p a b -> p (a b)")
                        give(do(probs[:, h % 2, 0:n], out[:, 0:n], ACT.Exp, bias=stat[:, 32 + h:33 + h],
                                scale=MLA_SCALE, accum_out=sums[:, h:h + 1]), "p_ready")

                    soften(0)
                    soften(1)
                    for h in range(NH):
                        if n > 512:
                            copy_a(pT[:, h % 2, 512:640], P)
                        if h + 2 < NH:
                            soften(h + 2)
                        if h == 3 and qt + 1 < NT:
                            root(8, 24)
                    copy_a(hT[:, 4:8, P * qt:P * (qt + 1)])

            def odd():
                for g in range(4):
                    scale = vecs[:, S_PS + g:S_PS + g + 1]
                    for at, n in ((0, 512), (512, P)):
                        copy_a(hT[:, g, at:at + n], n, scale=scale)
                for kt in range(6):
                    if kt < NT:
                        root(2, 24)
                    copy_a(kT2[:, :, P * kt:P * (kt + 1)], 256)
                root(8, 24)
                for qt in range(NT):
                    copy_a(qT2)
                    n = P * len(window_tiles(qt))

                    def soften(h):
                        act.wait_ge(*me.due("m_ready"))
                        bias = stat[:, 32 + h:33 + h]
                        give(do(probs2[:, h % 2, 0:n], soft_s[:, h % 2, 0:n], ACT.Exp, bias=bias,
                                accum_out=sums[:, h:h + 1]), "p_ready")
                        give(do(sinks[:, h:h + 1], vecs[:, S_SINK + h:S_SINK + h + 1], ACT.Exp, bias=bias), "es_ready")

                    for h in range(NH):
                        soften(h)
                        if h == 5 and qt + 1 < NT:
                            root(8, 24)
                    copy_a(hT[:, 4:8, P * qt:P * (qt + 1)])

            def route(l):
                for g in range(16):
                    copy_a(qsT[:, g % 2, 0:512])
                    copy_a(qsT[:, g % 2, 512:640], P)
                    n = g - 2
                    if l == 0 and 0 <= n < 12:
                        me.after(f"row_out{n % 2}", 16 * (n // 2))
                        copy_a(rows_next[0:2, 512 * (n % 2):512 * (n % 2) + 512])
                        signal("row_ready")
                act.wait_ge(*me.due("gate_in"))
                give(do(fin_v, fin_v, ACT.Exp), "gate_exp")

            def routing_matrix(l):
                jobs = TB // 4
                at = l * NB * jobs
                with act.Fori(0, NB // 2) as i:
                    for b in range(2):
                        act.wait_ge(sem[f"stage_out{b}"], i * 16 + 16 * (l * (NB // 2) + 1))


                        def scale_hots(n):
                            m = b * jobs + n
                            act.wait_ge(sem["hot_ready"], i * (2 * jobs) + (at + m + 1))
                            for q in range(2):
                                ins = do(hots[:, m % 4, 0, q, :], hots[:, m % 4, 0, q, :], ACT.Copy,
                                         scale=cols[:, b, 2, 4 * n + q:4 * n + q + 1])
                            ins.then_inc(sem["gated_a"], 1)

                        scale_hots(0)
                        scale_hots(1)
                        for n in range(jobs):
                            m = b * jobs + n
                            if n + 2 < jobs:
                                scale_hots(n + 2)
                            act.wait_ge(sem["g_full"], i * (2 * jobs) + (at + m + 5))
                            do(stage[:, b, :, 4 * n:4 * n + 4], pair[:, m % 4, :].rearrange("p (q j) -> p j q", q=4),
                               ACT.Copy).then_inc(sem["g_free"], 1)

            def split_u(b, n):
                act.wait_ge(sem[f"u_in{b}"], (n + (1 - b)) * 8)
                do(R(u_hi[b][:, :]), u_raw[b], ACT.Copy).then_inc(sem["u_led"], 1)

            def split_v(b, n):
                act.wait_ge(sem[f"v_in{b}"], (n + (1 - b)) * 8)
                do(R(v_hi[b][:, :]), v_raw[b], ACT.Copy).then_inc(sem["v_led"], 1)

            def first_tables(l):
                split_u(0, l * NG + 1)
                split_u(1, l * NG + 2)
                split_v(0, l * NG + 1)

            def dense(l):
                def gelu(b, n, first=False):
                    if not first:
                        act.wait_ge(sem["o_full"], (n - 2) * (2 * NT) + 1)
                    for m in range(2 * GROUP):
                        if m == GROUP and not first:
                            split_v(b, n)
                        at, w = HALVES[m % 2]
                        act.wait_ge(sem["h_full"], (n - 1) * (2 * GROUP) + (m + 1))
                        do(act_raw[b][:, m // 2, at:at + w], pair[:, m % 4, 0:w], ACT.Gelu).then_inc(sem["gelu_done"], 1)

                n0 = l * NG + 1
                for b in range(2):
                    act.wait_ge(sem[f"stage_out{b}"], 16 + 16 * (l + 1) * NB // 2)
                for k in range(KD):
                    do(R(h_hi[:, k, :]), hT[:, k, :], ACT.Copy).then_inc(sem["h_led"], 1)
                gelu(0, n0, first=True)
                with act.Fori(0, NG // 2 - 1) as i:
                    split_u(0, i * 2 + (n0 + 2))
                    gelu(1, i * 2 + (n0 + 1))
                    split_u(1, i * 2 + (n0 + 3))
                    gelu(0, i * 2 + (n0 + 2))
                gelu(1, n0 + NG - 1)

            act.sem_inc(sem["g_free"], G_AHEAD)
            act.sem_inc(sem["gelu_done"], 4)
            act.wait_ge(sem["const_in"], 32)
            give(do(silu_c.rearrange("p k c -> p (k c)"), vecs[:, S_C:S_C + 16], ACT.Silu), "silu_done")
            for l in range(LAYERS):
                if l == 0:
                    norm_sums(0, 0)
                    ada()
                norm(l, 0)
                if l == 0:
                    project(EVEN_CHUNKS, pe_)
                    gla()
                    mla()
                else:
                    project(ODD_CHUNKS, po_)
                    odd()
                norm(l, 1)
                route(l)
                first_tables(l)
                routing_matrix(l)
                dense(l)

        @block.sync
        def _(sp):
            sp.sem_inc(sem["stage_out0"], 16)
            sp.sem_inc(sem["stage_out1"], 16)

            def after(name, k):
                if k > 0:
                    sp.wait_ge(sem[name], k)

            def load(n):
                l = 0 if n < per_layer[0] else 1
                if n - 2 >= (0 if l == 0 else per_layer[0]):
                    after(*freed[n - 2])
                src = items[n]
                w = int(src.shape[1])
                sp.dma_start(ring[:, n % 2, 0:w], src).then_inc(sem[f"slot_in{n % 2}"], 16)

            for l in range(LAYERS):
                first = 0 if l == 0 else per_layer[0]
                if l:
                    sp.wait_ge(sem["x_done"], 2)
                for n in range(first, per_layer[l]):
                    if n < 12:
                        if n >= 2:
                            after(*freed[n - 2])
                        sp.dma_start(bias_rows[0:1, 512 * (n % 2):512 * (n % 2) + 512],
                                     a["b_ada"][l, n]).then_inc(sem[f"bias_in{n % 2}"], 16)
                    load(n)
                after(*freed[per_layer[l] - 2])
                sp.dma_start(u_raw[0], a["peer_u"][l, 0]).then_inc(sem["u_in0"], 16)
                if l == 0:
                    after("a_full", freed_next[11])
                sp.dma_start(u_raw[1], a["peer_u"][l, 1]).then_inc(sem["u_in1"], 16)
                sp.dma_start(v_raw[1], a["peer_v"][l, 1]).then_inc(sem["v_in1"], 16)
                after(*freed[per_layer[l] - 1])
                sp.dma_start(v_raw[0], a["peer_v"][l, 0]).then_inc(sem["v_in0"], 16)
                jobs = TB // 4
                with sp.Fori(0, NB // 2) as i:
                    for b in range(2):
                        sp.wait_ge(sem["g_free"], i * (2 * jobs) + (G_AHEAD + l * NB * jobs + jobs * (b + 1)))
                        sp.dma_start(routing[:, :, bass.ds(i * 2 + b, 1), :, :].rearrange("g p k j t -> p g (k j t)"),
                                     stage[:, b, :, :].rearrange("p (g j) t -> p g (j t)", g=NR)
                                     ).then_inc(sem[f"stage_out{b}"], 16)
                for b in range(2):
                    sp.wait_ge(sem[f"stage_out{b}"], 16 + 16 * (l + 1) * NB // 2)
                def load_routing(r):
                    sp.dma_start(gmat.rearrange("p k j t -> p (k j t)"),
                                 routing[bass.ds(r, 1)].rearrange("g p k j t -> p (g k j t)")).then_inc(sem["g_in"], 16)

                def load_u(b, g):
                    sp.wait_ge(sem["h_full"], (g - 1) * (2 * GROUP) + l * NG * 2 * GROUP)
                    sp.dma_start(u_raw[b], table("peer_u", g)).then_inc(sem[f"u_in{b}"], 16)

                def load_v(b, g):
                    sp.wait_ge(sem["o_full"], (g - 1) * (2 * NT) + (l * NG * 2 * NT + 1))
                    sp.dma_start(v_raw[b], table("peer_v", g)).then_inc(sem[f"v_in{b}"], 16)

                def table(name, g):
                    return a[name][l, bass.ds(g, 1)].rearrange("g p n -> p (g n)")

                load_routing(0)
                load_u(0, 2)
                with sp.Fori(0, NG // 2 - 2) as i:
                    load_u(1, i * 2 + 3)
                    sp.wait_ge(sem["act_made"], i * (2 * GROUP) + GROUP * (l * NG + 2))
                    load_routing(i + 1)
                    load_v(0, i * 2 + 2)
                    load_u(0, i * 2 + 4)
                    load_v(1, i * 2 + 3)
                load_u(1, NG - 1)
                sp.wait_ge(sem["act_made"], GROUP * (l * NG + NG - 2))
                load_routing(NR - 1)
                load_v(0, NG - 2)
                load_v(1, NG - 1)
            sp.wait_ge(sem["x_done"], 4)
            sp.dma_start(a["y_prompt"], x[:, 0, :]).then_inc(sem["out_y"], 16)
            sp.dma_start(a["y_sample"].rearrange("(t p) d -> p t d", p=P), x[:, 1:NT, :]).then_inc(sem["out_y"], 16)
            sp.wait_ge(sem["out_y"], 32)

        @block.gpsimd
        def _(pool):
            def routing_matrix(l):
                jobs = TB // 4
                with pool.Fori(0, NB // 2) as i:
                    for b in range(2):
                        for n in range(jobs):
                            m = b * jobs + n
                            pool.wait_ge(sem["hot_ready"], i * (2 * jobs) + (l * NB * jobs + m + 1))
                            rows = hots[:, m % 4, 0, 2:4, :]
                            nc.gpsimd.tensor_tensor(rows, rows, bc(cols[:, b, 2, 4 * n + 2:4 * n + 4], P, 2),
                                                    ALU.mult).then_inc(sem["gated_p"], 1)

            def next_modulation():
                def row_out(n):
                    pool.wait_ge(sem["row_ready"], n + 1)
                    pool.dma_start(mod_rows[:, 512 * n:512 * n + 512],
                                   rows_next[0:2, 512 * (n % 2):512 * (n % 2) + 512]).then_inc(sem[f"row_out{n % 2}"], 16)

                for n in range(12):
                    if n >= 2:
                        pool.wait_ge(sem["a_full"], freed_next[n - 2])
                    pool.dma_start(bias_next[0:1, 512 * (n % 2):512 * (n % 2) + 512],
                                   a["b_ada"][1, n]).then_inc(sem[f"bias_in{2 + n % 2}"], 16)
                    pool.dma_start(ring[:, 2 + n % 2, :], a["w_ada"][1, n]).then_inc(sem[f"slot_in{2 + n % 2}"], 16)
                    if n >= 2:
                        row_out(n - 2)
                row_out(10)
                row_out(11)
                for b in range(2):
                    pool.wait_ge(sem[f"row_out{b}"], 16 * 6)
                for s in range(2):
                    for w in range(2):
                        at = (3 * s + w) * D
                        for c in range(2):
                            pool.dma_start(ada_col[:, s, w, :, c], mod_rows[c, at:at + D].rearrange("(k p) -> p k", p=P),
                                           allow_slow_non_contiguous=True).then_inc(sem["cols_in"], 16)

            pool.dma_start(const[:, :], a["const"]).then_inc(sem["const_in"], 16)
            pool.dma_start(vecs[:, :], a["vecs"]).then_inc(sem["const_in"], 16)
            pool.dma_start(x[:, :, :], a["x"].rearrange("(t p) d -> p t d", p=P)).then_inc(sem["x_in"], 16)
            pool.dma_start(wgu[0:33, :], a["w_gu"]).then_inc(sem["wgu_in"], 16)
            for r in range(2):
                pool.dma_start(s_in[64 * r:64 * r + 64, :, :].rearrange("k d (q v) -> k d q v", q=2),
                               a["state_in"][:, :, r]).then_inc(sem["s_in_in"], 16)
            pool.wait_ge(sem["ctx_state"], 1)
            for d in range(2):
                for r in range(2):
                    pool.dma_start(a["state"][d].rearrange("(q r) k v -> r k q v", r=2)[r],
                                   s_out[64 * r:64 * r + 64, d, :].rearrange("k (q v) -> k q v", q=2)
                                   ).then_inc(sem["out_state"], 16)
            pool.wait_ge(sem["s_ready"], 1)
            pool.dma_start(ctx_ckv, a["ctx_ckv"]).then_inc(sem["ctx_in"], 16)
            pool.dma_start(ctx_kr, a["ctx_kr"]).then_inc(sem["ctx_in"], 16)
            pool.wait_ge(sem["ckv_ready"], 1)
            pool.dma_start(a["ckv"], pe_[:, 0, CKV0:CKV0 + 256]).then_inc(sem["out_cache"], 16)
            pool.dma_start(a["kr"], pe_[:, 0, KR0:KR0 + 64]).then_inc(sem["out_cache"], 16)
            for l in range(LAYERS):
                if l == 1:
                    pool.wait_ge(sem["x_done"], 2)
                    for s in range(2):
                        for c in range(2):
                            src = mod_rows[c:c + 1, (3 * s + 2) * D:(3 * s + 3) * D]
                            pool.dma_start(gate[:, s, c, :], src.broadcast_to((P, D))).then_inc(sem["gates_in"], 16)
                    pool.wait_ge(sem["k_ready"], 7)
                    pool.dma_start(kctx, a["k_ctx"]).then_inc(sem["kvctx_in"], 16)
                    pool.dma_start(vctx, a["v_ctx"]).then_inc(sem["kvctx_in"], 16)
                    pool.dma_start(a["win"][0], po_[:, 0, KD0:KD0 + P]).then_inc(sem["out_cache"], 16)
                    pool.dma_start(a["win"][1], po_[:, 0, VD0:VD0 + P]).then_inc(sem["out_cache"], 16)
                pool.wait_ge(sem["x_done"], 2 * l + 1)
                pool.dma_start(subk.rearrange("p g n -> p (g n)"), a["subkeys"][l]).then_inc(sem["subk_in"], 16)
                if l == 0:
                    next_modulation()
                routing_matrix(l)
            pool.wait_ge(sem["out_state"], 64)
            pool.wait_ge(sem["out_cache"], 64)

        @block.vector
        def _(dve):
            me = Turn(dve, "chain_v")
            V = nc.vector
            tt, ts, stt = V.tensor_tensor, V.tensor_scalar, V.scalar_tensor_tensor
            link, give = me.link, me.give

            def take_d():
                n = me.next("d_full")
                dve.wait_ge(sem["d_full"], n)
                return bank[(n - 1) % 2]

            def take_s():
                n = me.next("s_full")
                dve.wait_ge(sem["s_full"], n)
                return pair[:, 2 * ((n - 1) % 2):2 * ((n - 1) % 2) + 2, :]

            def signal(name):
                dve.sem_inc(sem[name], 1)
                total[name] = total.get(name, 0) + 1

            def rstd(ss, n):
                mean(ss, n)
                inverse_root(ss)

            def mean(ss, n):
                give(ts(ss, ss, 1.0 / n, EPS, ALU.mult, ALU.add), "var_ready")

            def inverse_root(ss):
                dve.wait_ge(*me.due("std_ready"))
                link(V.reciprocal(ss, ss))

            def ada():
                def column(n):
                    kind = n // 2
                    if kind not in (2, 5):
                        out = take_d()
                        s, w = (0, kind) if kind < 2 else (1, kind - 3)
                        give(V.tensor_copy(ada_col[:, s, w, 4 * (n % 2):4 * (n % 2) + 4, :],
                                           out[:, 0:8].rearrange("p (k c) -> p k c", k=4)), "d_free")

                for n in range(12):
                    out = take_d()
                    give(V.tensor_copy(ada_rows[0:2, 512 * (n % 2):512 * (n % 2) + 512], out[0:2, :]), "d_free")
                    if n:
                        column(n - 1)
                column(11)

            def gains(l):
                for s in range(2):
                    g = vecs[:, S_GN + 16 * l + 8 * s:S_GN + 16 * l + 8 * s + 8]
                    give(stt(mod[:, s, :, :], ada_col[:, s, 1, :, :], 1.0, bc(g, 2, 2), ALU.add, ALU.mult),
                         "mods_done")

            def norm_roots():
                dve.wait_ge(*me.due("ss_ready"))
                rstd(stat[:, 0:NT], D)

            def norm(l, s):
                if l or s:
                    norm_roots()
                for t in range(NT):
                    give(ts((xn0, xn1)[t % 2], x[:, t, :], stat[:, t:t + 1], None, ALU.mult), "xn_ready")
                    if t:
                        evac_norm(s, t - 1)
                evac_norm(s, NT - 1)

            def evac_norm(s, t):
                out = take_d()
                c = int(t > 0)
                for k in range(4):
                    ins = ts(hT[:, k, P * t:P * (t + 1)], out[:, P * k:P * (k + 1)], mod[:, s, k, c:c + 1],
                             ada_col[:, s, 0, k, c:c + 1], ALU.mult, ALU.add)
                give(ins, "d_free")

            def project(chunks, dst):
                for n, (at, w) in enumerate(chunks):
                    for t in range(NT):
                        if (n * NT + t) % 2 == 0 and n != 2:
                            out = take_d()
                            give(V.tensor_copy(dst[:, t, at:at + w], out[:, 0:w]), "d_free")
                me.after("a_free", marks[("proj", layer[0])]["a_full"])

            def gla():
                link(V.memset(attT.rearrange("p r d q n -> p (r d q n)"), 0.0))
                link(V.memset(glT[32:33, :], 1.0))
                for at, n in ((0, 4 * P), (4 * P, P)):
                    out = take_d()
                    give(V.tensor_copy(glT[0:32, at:at + n], out[0:32, 0:n]), "d_free")

                def gates(t):
                    dve.wait_ge(*me.due("z_exp"))
                    give(stt(la[:, t], zb[t % 2], -1.0 / 16.0, la[:, t], ALU.mult, ALU.add), "la_ready")

                for t in range(NT):
                    out = take_d()
                    z = zb[t % 2]
                    link(ts(z, out[:, :], -1.0, None, ALU.mult))
                    give(tt(z, z, out[:, :], ALU.max), "z_part")
                    give(ts(la[:, t], out[:, :], 0.0, 1.0 / 16.0, ALU.min, ALU.mult), "d_free")
                    if t:
                        gates(t - 1)
                gates(NT - 1)

                def decayed(t):
                    pt = pe_[:, t, :]
                    eb, en, es = exps[t % 2]
                    me.after("a_free", marks[("exps", t)]["a_full"])
                    q2 = bc(pt[:, Q0:Q0 + 256], 2, 1)
                    k2_ = bc(pt[:, K0:K0 + 256], 2, 1)
                    for e, s_, sc in ((eb, q2, 64.0 ** -0.5), (en, k2_, 1.0), (es, k2_, 1.0)):
                        e3 = e.rearrange("p (d n) -> p d n", d=2)
                        ins = stt(e3, s_, sc, e3, ALU.mult, ALU.mult)
                    give(ins, "exps_mul")

                decayed(0)
                for t in range(NT):
                    pt = pe_[:, t, :]
                    out = take_d()
                    give(V.tensor_copy(qdT[:, t, :, :], out[:, :].rearrange("p (q n) -> p q n", q=4)), "d_free")
                    out = take_s()
                    for r in range(2):
                        for d in range(2):
                            ins = V.copy_predicated(
                                attT[:, r, d, :, :], bc(cum[d].bitcast(U32), 2, 1),
                                out[:, r, 256 * d:256 * d + 256].rearrange("p (q n) -> p q n", q=2))
                    give(ins, "s_free")
                    out = take_s()
                    for c in range(2):
                        ins = V.tensor_copy(upd[:, 2 * t + c, :, :], out[:, c, :].rearrange("p (d n) -> p d n", d=2))
                    give(ins, "s_free")
                    if t + 1 < NT:
                        decayed(t + 1)
                    out = take_d()
                    give(V.tensor_copy(pt[:, 0:512], out[:, :]), "d_free")
                me.after("a_free", marks["gla_tiles"]["a_full"])
                cur = [s.rearrange("p (d n) -> p d n", d=2) for s in scan_cur]
                for part, chunks in (("context", (0, 1)), ("latent", tuple(range(2, 10)))):
                    if part == "context":
                        link(V.memset(scan_cur[0], 0.0))
                    else:
                        dve.wait_ge(sem["s_in_in"], 32)
                        link(V.tensor_copy(cur[0], s_in[:, :, :]))
                    for i in range(len(chunks)):
                        a_, b_ = cur[i % 2], cur[(i + 1) % 2]
                        at = (chunks[i], chunks[-1 - i])
                        for d, c in enumerate(at):
                            for q in range(2):
                                nq = slice(P * q, P * (q + 1))
                                ins = stt(b_[:, d, nq], a_[:, d, nq], decay[:, c // 2, d, q, c % 2:c % 2 + 1],
                                          upd[:, c, d, nq], ALU.mult, ALU.add)
                        link(ins)
                        for d, c in enumerate(at):
                            ins = V.tensor_copy(upd[:, c, d, :], a_[:, d, :])
                        if i + 1 < len(chunks) or part == "context":
                            link(ins)
                    if part == "context":
                        give(V.tensor_copy(s_out, cur[0]), "ctx_state")
                give(ins, "s_ready")
                for t in range(NT):
                    o = pe_[:, t, 0:512]
                    out = take_s()
                    for r in range(2):
                        o_r = o.rearrange("p (q r n) -> p q r n", q=2, r=2)[:, :, r, :]
                        ins = tt(o_r, o_r, out[:, r, 0:256].rearrange("p (q n) -> p q n", q=2), ALU.add)
                    give(ins, "s_free")
                    o4 = o.rearrange("p (h n) -> p h n", h=4)
                    link(tt(sq5, o, o, ALU.mult))
                    link(V.tensor_reduce(stat[:, 8:12], sq5.rearrange("p (h n) -> p h n", h=4), AX.X, ALU.add))
                    rstd(stat[:, 8:12], P)
                    link(tt(o4, o4, bc(stat[:, 8:12], P, 2), ALU.mult))
                    give(tt(o, o, pe_[:, t, R0:R0 + 512], ALU.mult), "oa_ready")

            def rope_into(dst, src, t, heads):
                cos, sin = rope[:, t - 1, 0, :], rope[:, t - 1, 1, :]
                tmp = sq10[:, 0:64 * heads] if layer[0] == 0 else sqo[:, 0:64 * heads]
                s5 = src.rearrange("p h (a b n) -> p h a b n", a=2, b=2)
                t5 = tmp.rearrange("p (h a b n) -> p h a b n", h=heads, a=2, b=2)
                n4 = sin.rearrange("p (a b n) -> p a b n", a=2, b=2)
                for b in range(2):
                    if heads == 1:
                        link(tt(t5[:, 0, :, b, :], s5[:, 0, :, 1 - b, :], n4[:, :, b, :], ALU.mult))
                    else:
                        link(tt(t5[:, :, :, b, :], s5[:, :, :, 1 - b, :], bc(n4[:, :, b, :], heads, 1), ALU.mult))
                t3 = tmp.rearrange("p (h n) -> p h n", h=heads)
                link(tt(dst, src, bc(cos, heads, 1), ALU.mult))
                link(tt(dst, dst, t3, ALU.add))

            def latents():
                parts = [(pe_[:, t, at:at + 256], gain) for at, gain in ((CKV0, S_CKV), (CQ0, S_CQ)) for t in range(NT)]
                for i, (src, _) in enumerate(parts):
                    link(V.tensor_tensor_reduce(sq5[:, 0:256], src, src, 1.0, 0.0, ALU.mult, ALU.add,
                                                stat[:, 50 + i:51 + i]))
                rstd(stat[:, 50:50 + 2 * NT], 256)
                for i, (src, gain) in enumerate(parts):
                    give(stt(src, src, stat[:, 50 + i:51 + i], vecs[:, gain:gain + 256], ALU.mult, ALU.mult),
                         "ckv_ready")

            def copy_ckvT():
                out = take_d()
                give(V.tensor_copy(ckvT, out[:, 0:256]), "d_free")

            def mla():
                latents()
                me.after("a_full", marks["oa"]["a_full"])
                g_kn = vecs[:, S_KN:S_KN + P]
                g_qn = vecs[:, S_QN:S_QN + P]
                qk3 = qk.rearrange("p (h n) -> p h n", h=NH)
                copy_ckvT()
                for kt in range(6):
                    if kt < NT:
                        kr = pe_[:, kt, KR0:KR0 + 64]
                    else:
                        dve.wait_ge(sem["ctx_in"], 32)
                        kr = ctx_kr
                    if kt:
                        me.after("a_full", marks[("keys", kt - 1)]["a_full"])
                    out = take_d()
                    give(V.tensor_copy(qk3[:, :, 0:64], out[:, :].rearrange("p (h n) -> p h n", h=NH)), "d_free")
                    if kt + 1 < 6:
                        copy_ckvT()
                    link(V.tensor_tensor_reduce(krt, kr, kr, 1.0, 0.0, ALU.mult, ALU.add, stat[:, 17:18]))
                    link(tt(krt, kr, g_kn[:, 64:128], ALU.mult))
                    if 1 <= kt < NT:
                        rope_into(krr.unsqueeze(1), krt.unsqueeze(1), kt, 1)
                    else:
                        link(V.tensor_copy(krr, krt))
                    s3 = sq10[:, 0:512].rearrange("p (h n) -> p h n", h=NH)
                    link(tt(s3, qk3[:, :, 0:64], qk3[:, :, 0:64], ALU.mult))
                    link(V.tensor_reduce(stat[:, 24:32], s3, AX.X, ALU.add))
                    link(ts(stat[:, 24:32], stat[:, 24:32], stat[:, 17:18], None, ALU.add))
                    rstd(stat[:, 24:32], P)
                    r3 = bc(stat[:, 24:32], 64, 2)
                    link(tt(qk3[:, :, 0:64], qk3[:, :, 0:64], bc(g_kn[:, 0:64], NH, 1), ALU.mult))
                    link(tt(qk3[:, :, 0:64], qk3[:, :, 0:64], r3, ALU.mult))
                    give(tt(qk3[:, :, 64:128], bc(krr, NH, 1), r3, ALU.mult), "k_ready")

                def queries(qt, part):
                    if part == 0:
                        copy_ckvT()
                    elif part < 3:
                        out = take_d()
                        give(V.tensor_copy(qk[:, 512 * (part - 1):512 * part], out[:, :]), "d_free")
                    elif part == 3:
                        s3 = sq10.rearrange("p (h n) -> p h n", h=NH)
                        link(tt(s3, qk3, qk3, ALU.mult))
                        link(V.tensor_reduce(stat[:, 24:32], s3, AX.X, ALU.add))
                        mean(stat[:, 24:32], P)
                    elif part == 4:
                        inverse_root(stat[:, 24:32])
                        link(tt(qk3, qk3, bc(g_qn, NH, 1), ALU.mult))
                        link(tt(qk3, qk3, bc(stat[:, 24:32], P, 2), ALU.mult))
                    elif part == 5:
                        if qt:
                            rope_into(qk3[:, :, 64:128], qk3[:, :, 64:128], qt, NH)
                        signal("q_ready")

                for part in range(6):
                    queries(0, part)
                for qt in range(NT):
                    n = P if qt == 0 else 5 * P

                    def biggest(h):
                        out = take_s().rearrange("p a b -> p (a b)")
                        link(V.tensor_reduce(stat[:, 32 + h:33 + h], out[:, 0:n], AX.X, ALU.max))
                        give(ts(stat[:, 32 + h:33 + h], stat[:, 32 + h:33 + h], -MLA_SCALE, None, ALU.mult), "m_ready")

                    heads(biggest, lambda h: pT[:, h % 2, 0:min(n, 512)], att_o,
                          (lambda h: queries(qt + 1, h)) if qt + 1 < NT else None)

            def heads(biggest, pT_of, dst, between):

                def turned(h):
                    dve.wait_ge(*me.due("p_ready"))
                    if layer[0] == 0:
                        signal("s_free")
                    else:
                        dve.wait_ge(*me.due("es_ready"))
                    out = take_d()
                    pT_b = pT_of(h)
                    give(V.tensor_copy(pT_b, out[:, 0:int(pT_b.shape[1])]), "d_free")
                    if layer[0]:
                        link(tt(sums[:, h:h + 1], sums[:, h:h + 1], sinks[:, h:h + 1], ALU.add))

                biggest(0)
                biggest(1)
                turned(0)
                for h in range(NH):
                    if h + 2 < NH:
                        biggest(h + 2)
                    link(V.reciprocal(stat[:, 48 + h % 2:49 + h % 2], sums[:, h:h + 1]))
                    if h + 1 < NH:
                        turned(h + 1)
                    out = take_d()
                    give(ts(dst[:, 64 * h:64 * h + 64], out[:, 0:64], stat[:, 48 + h % 2:49 + h % 2], None, ALU.mult),
                         "d_free")
                    if between:
                        between(h)

            def head_norm(buf3, gain, heads, t, at):
                s3 = sqo[:, 0:64 * heads].rearrange("p (h n) -> p h n", h=heads)
                link(tt(s3, buf3, buf3, ALU.mult))
                link(V.tensor_reduce(stat[:, at:at + heads], s3, AX.X, ALU.add))
                rstd(stat[:, at:at + heads], 64)
                link(tt(buf3, buf3, bc(gain, heads, 1), ALU.mult))
                link(tt(buf3, buf3, bc(stat[:, at:at + heads], 64, 2), ALU.mult))
                if t:
                    rope_into(buf3, buf3, t, heads)

            def odd():
                for g in range(4):
                    out = take_d()
                    give(V.tensor_copy(yT[:, g % 2, 0:P], out[:, 0:P]), "d_free")
                    out = take_d()
                    give(V.tensor_copy(yT[:, g % 2, P:T], out[:, :]), "d_free")
                for kt in range(6):
                    if kt < NT:
                        k = po_[:, kt, KD0:KD0 + P]
                        k3 = k.rearrange("p (v n) -> p v n", v=2)
                        head_norm(k3, vecs[:, S_WKN:S_WKN + 64], 2, kt, 24)
                    else:
                        dve.wait_ge(sem["kvctx_in"], 32)
                        k3 = kctx.rearrange("p (v n) -> p v n", v=2)
                    if kt:
                        me.after("a_full", marks[("odd_k", kt - 1)]["a_full"])
                    k24 = k2.rearrange("p (v r n) -> p v r n", v=2, r=2)
                    give(V.tensor_copy(k24, bc(k3, 2, 2)), "k_ready")
                sink = vecs[:, S_SINK:S_SINK + NH]
                qn3 = qn.rearrange("p (h n) -> p h n", h=NH)

                def queries(qt, part):
                    if part == 2:
                        link(V.tensor_copy(qn, po_[:, qt, QD0:QD0 + 512]))
                    elif part == 3:
                        s3 = sqo.rearrange("p (h n) -> p h n", h=NH)
                        link(tt(s3, qn3, qn3, ALU.mult))
                        link(V.tensor_reduce(stat[:, 24:32], s3, AX.X, ALU.add))
                        mean(stat[:, 24:32], 64)
                    elif part == 4:
                        inverse_root(stat[:, 24:32])
                        link(tt(qn3, qn3, bc(vecs[:, S_WQN:S_WQN + 64], NH, 1), ALU.mult))
                        link(tt(qn3, qn3, bc(stat[:, 24:32], 64, 2), ALU.mult))
                    elif part == 5:
                        if qt:
                            rope_into(qn3, qn3, qt, NH)
                        signal("q_ready")

                me.after("a_full", marks[("odd_k", 5)]["a_full"])
                for part in range(6):
                    queries(0, part)
                for qt in range(NT):
                    tiles = window_tiles(qt)
                    n = P * len(tiles)
                    if qt == 0 or qt == 4:
                        parts = [(0, P, P)] if qt == 0 else [(0, 2 * P, 0), (2 * P, P, P)]
                    else:
                        parts = [(0, n, P if qt == 1 else 0)]

                    def biggest(h):
                        out = take_s().rearrange("p a b -> p (a b)")
                        s_ = soft_s[:, h % 2, :]
                        for i, (at, w, m_at) in enumerate(parts):
                            ins = stt(s_[:, at:at + w], out[:, at:at + w], WIN_SCALE, wmask[:, m_at:m_at + w],
                                      ALU.mult, ALU.add)
                            if i + 1 < len(parts):
                                link(ins)
                        give(ins, "s_free")
                        link(V.tensor_reduce(stat[:, 32 + h:33 + h], s_[:, 0:n], AX.X, ALU.max))
                        give(ts(stat[:, 32 + h:33 + h], stat[:, 32 + h:33 + h], sink[:, h:h + 1], -1.0,
                                ALU.max, ALU.mult), "m_ready")

                    heads(biggest, lambda h: pT2[:, h % 2, 0:n], att_o2,
                          (lambda h: queries(qt + 1, h)) if qt + 1 < NT else None)

            def out_project(l):
                me.after("out_cache", 32 * (l + 1))
                if l:
                    dve.wait_ge(sem["gates_in"], 16 * 4)
                for n in range(2):
                    for t in range(NT):
                        out = take_d()
                        g = gate[:, 0, int(t > 0), 512 * n:512 * n + 512]
                        tmp = arena[:, 8192:8704]
                        give(tt(tmp, out[:, :], g, ALU.mult), "d_free")
                        xs = x[:, t, 512 * n:512 * n + 512]
                        ins = tt(xs, xs, tmp, ALU.add)
                        if n == 0 or t < NT - 1:
                            link(ins)
                give(ins, "x_done")

            def sixteen(values, cut, idx, top):
                steps = (lambda t: V.max(top(t)[:, 0:8], values(t)),
                         lambda t: V.max_index(idx(t)[:, 0:8], top(t)[:, 0:8], values(t)),
                         lambda t: V.match_replace(cut(t), top(t)[:, 0:8], values(t), LOWEST),
                         lambda t: V.max(top(t)[:, 8:16], cut(t)),
                         lambda t: V.max_index(idx(t)[:, 8:16], top(t)[:, 8:16], cut(t)))
                for i, step in enumerate(steps):
                    for t in range(NT):
                        if i:
                            dve.wait_ge(sem["chain_v"], total["chain_v"] - (NT - 1))
                        step(t).then_inc(sem["chain_v"], 1)
                        total["chain_v"] += 1
                dve.wait_ge(sem["chain_v"], total["chain_v"])

            def route(l):
                fin_p3 = fin_p.bitcast(U32).rearrange("p (t h k) -> p t h k", t=NT, h=NH)
                for g in range(16):
                    h, c = g // 2, g % 2
                    out = take_s()
                    sixteen(lambda t: out[:, t // 4, P * (t % 4):P * (t % 4 + 1)], lambda t: cand_cut[:, t, 0:P],
                            lambda t: tmp_i[:, t, :], lambda t: top_v5[:, t, h, c, :])
                    signal("s_free")
                    link(V.tensor_copy(top_i5[:, :, h, c, :], tmp_i[:, :, :]))
                    if c:
                        at = 0
                        for row, n, w in PAIRS:
                            ins = tt(cand[:, :, at:at + n * w].rearrange("p t (i j) -> p t i j", i=n),
                                     bc(top_v5[:, :, h, 0, row:row + n], w, 3),
                                     bc(top_v5[:, :, h, 1, 0:w], n, 2), ALU.add)
                            at += n * w
                        link(ins)
                        sixteen(lambda t: cand[:, t, :], lambda t: cand_cut[:, t, 0:NPAIR],
                                lambda t: fin_p3[:, t, h, :], lambda t: fin_v4[:, t, h, :])
                        places = fin_p3[:, :, h, :]
                        link(V.tensor_copy(place, places))
                        V.tensor_copy(steps[:, :, 0:1], top_i5[:, :, h, 0, 0:1])
                        tt(steps[:, :, 1:TOPK], top_i5[:, :, h, 0, 1:TOPK], top_i5[:, :, h, 0, 0:TOPK - 1], ALU.subtract)
                        link(tt(hot, bc(place, TOPK, 3), bc(bc(starts, TOPK, 1), NT, 1), ALU.is_ge))
                        link(tt(hot, hot, bc(steps, TOPK, 2), ALU.mult))
                        link(V.tensor_reduce(pick3[:, 0, :, TOPK * h:TOPK * (h + 1)], hot, AX.X, ALU.add))
                        at = [n * w for _, n, w in PAIRS]
                        link(ts(past, place, float(at[0]), float(PAIRS[1][2] - PAIRS[0][2]), ALU.is_ge, ALU.mult))
                        link(ts(place, place, float(at[0] + at[1]), float(PAIRS[2][2] - PAIRS[1][2]), ALU.is_ge, ALU.mult))
                        link(stt(place_u, past, float(PAIRS[0][2] - 1), place, ALU.add, ALU.add))
                        link(tt(place_u, place_u, places, ALU.bitwise_and))
                        link(V.tensor_copy(place, place_u))
                        link(tt(hot, bc(place, TOPK, 3), bc(bc(iota[:, 0:TOPK], TOPK, 1), NT, 1), ALU.is_equal))
                        link(tt(hot, hot, bc(top_i5[:, :, h, 1, :], TOPK, 2), ALU.mult))
                        link(V.tensor_reduce(pick3[:, 1, :, TOPK * h:TOPK * (h + 1)], hot, AX.X, ALU.add))
                fv3 = fin_v.rearrange("p (g k) -> p g k", k=TOPK)
                link(V.tensor_copy(sums40, fv3[:, :, 0]))
                give(tt(fv3, fv3, bc(sums40, TOPK, 2), ALU.subtract), "gate_in")
                dve.wait_ge(*me.due("gate_exp"))
                link(V.tensor_reduce(sums40, fv3, AX.X, ALU.add))
                link(V.reciprocal(sums40, sums40))
                give(tt(pick3[:, 2, :, :].rearrange("p t (h k) -> p (t h) k", h=NH), fv3, bc(sums40, TOPK, 2), ALU.mult),
                     "pick_ready")
                for t in range(NT):
                    out = take_d()
                    give(V.tensor_copy(pickT[:, :, P * t:P * (t + 1)],
                                       out[:, 0:3 * P].rearrange("p (k n) -> p k n", k=3)), "d_free")

            def routing_matrix(l):
                jobs = TB // 4
                hot0 = l * NB * jobs
                with dve.Fori(0, NB // 2) as i:
                    for b in range(2):
                        dve.wait_ge(sem["g_free"], i * (2 * jobs) + (hot0 + jobs * (b - 1) + G_AHEAD))
                        ts(cols[:, b, :, :], pickT[:, :, bass.ds(i * (2 * TB) + b * TB, TB)], 1.0, None,
                           ALU.mult).then_inc(sem["cols_ready"], 1)
                        dve.wait_ge(sem["cols_ready"], i * 2 + (l * NB + b + 1))
                        for n in range(jobs):
                            m = b * jobs + n
                            dve.wait_ge(sem["g_full"], i * (2 * jobs) + (hot0 + m + 1))
                            tt(hots[:, m % 4], bc(cols[:, b, 0:2, 4 * n:4 * n + 4], P, 3),
                               bc(bc(iota, 4, 1), 2, 1), ALU.is_equal).then_inc(sem["hot_ready"], 1)

            def dense(l):
                def split_u(b, n):
                    dve.wait_ge(sem["u_led"], n)
                    tt(R(u_lo[b][:, :]), u_raw[b], u_hi[b][:, :], ALU.subtract).then_inc(sem["u_split"], 1)

                def split_v(b, n):
                    dve.wait_ge(sem["v_led"], n)
                    tt(R(v_lo[b][:, :]), v_raw[b], v_hi[b][:, :], ALU.subtract).then_inc(sem["v_split"], 1)

                def weight(b, n, j):
                    dve.wait_ge(sem["gelu_done"], (n - 1) * (2 * GROUP) + (2 * j + 6))
                    part = act_raw[b][:, j, :]
                    part3 = part.rearrange("p (k t) -> p k t", t=TB)
                    c = (n - 1) * GROUP + (j + 1)
                    tt(part3, part3, gmat[:, :, GROUP * b + j, :], ALU.mult).then_inc(sem["act_made"], 1)
                    dve.wait_ge(sem["act_made"], c)
                    V.tensor_copy(R(act_hi[b][:, j, :]), part).then_inc(sem["act_led"], 1)
                    dve.wait_ge(sem["act_led"], c)
                    tt(R(act_lo[b][:, j, :]), part, act_hi[b][:, j, :], ALU.subtract).then_inc(sem["act_ready"], 1)

                def add(b, n):
                    for m in range(2 * NT):
                        t, half = m // 2, m % 2
                        dve.wait_ge(sem["o_free"], (n - 1) * (2 * NT) + (m + 4))
                        dve.wait_ge(sem["o_full"], (n - 1) * (2 * NT) + (m + 2))
                        part = acc[:, t, 512 * half:512 * half + 512]
                        tt(part, part, bank[(2 * b + m) % 4][:, :], ALU.add).then_inc(sem["o_free"], 1)

                n0 = l * NG + 1
                split_u(0, n0)
                for k in range(KD):
                    dve.wait_ge(sem["h_led"], KD * l + k + 1)
                    tt(R(h_lo[:, k, :]), hT[:, k, :], h_hi[:, k, :], ALU.subtract).then_inc(sem["h_split"], 1)
                split_u(1, n0 + 1)
                for b in range(2):
                    dve.wait_ge(sem[f"stage_out{b}"], 16 + 16 * (l + 1) * NB // 2)
                link(V.memset(acc.rearrange("p t d -> p (t d)"), 0.0))
                dve.wait_ge(sem["g_in"], 16 * (l * NR + 1))
                weight(0, n0, 0)
                split_v(0, n0)
                weight(0, n0, 1)
                with dve.Fori(0, NG // 2 - 1) as i:
                    split_u(0, i * 2 + (n0 + 2))
                    weight(1, i * 2 + (n0 + 1), 0)
                    split_v(1, i * 2 + (n0 + 1))
                    weight(1, i * 2 + (n0 + 1), 1)
                    add(0, i * 2 + n0)
                    split_u(1, i * 2 + (n0 + 3))
                    dve.wait_ge(sem["g_in"], i * 16 + 16 * (l * NR + 2))
                    weight(0, i * 2 + (n0 + 2), 0)
                    split_v(0, i * 2 + (n0 + 2))
                    weight(0, i * 2 + (n0 + 2), 1)
                    add(1, i * 2 + (n0 + 1))
                n = n0 + NG - 2
                weight(1, n + 1, 0)
                split_v(1, n + 1)
                weight(1, n + 1, 1)
                add(0, n)
                add(1, n + 1)
                dve.wait_ge(sem["o_free"], 4 + (l + 1) * 2 * NT * NG)
                for t in range(NT):
                    link(tt(acc[:, t, :], acc[:, t, :], gate[:, 1, int(t > 0), :], ALU.mult))
                    ins = tt(x[:, t, :], x[:, t, :], acc[:, t, :], ALU.add)
                    if t < NT - 1:
                        link(ins)
                give(ins, "x_done")

            layer = [0]
            dve.wait_ge(sem["const_in"], 32)
            dve.wait_ge(sem["x_in"], 16)
            dve.sem_inc(sem["o_free"], 4)
            for l in range(LAYERS):
                layer[0] = l
                if l == 0:
                    norm_roots()
                    ada()
                else:
                    dve.wait_ge(sem["cols_in"], 16 * 8)
                gains(l)
                norm(l, 0)
                if l == 0:
                    project(EVEN_CHUNKS, pe_)
                    gla()
                    mla()
                else:
                    project(ODD_CHUNKS, po_)
                    odd()
                out_project(l)
                norm(l, 1)
                route(l)
                routing_matrix(l)
                dense(l)


def constants():
    c = np.zeros((P, C_N), np.float32)
    i = np.arange(P)
    c[:, C_ID:C_ID + P] = np.eye(P)
    c[:, C_IOTA:C_IOTA + P] = i
    same = (i[:, None] // 64) == (i[None, :] // 64)
    c[:, C_CUM:C_CUM + P] = same & (i[:, None] <= i[None, :])
    c[:, C_CUM + P:C_CUM + 2 * P] = same & (i[:, None] >= i[None, :])
    c[:, C_REST:C_REST + P] = same & (i[:, None] > i[None, :])
    c[:, C_REST + P:C_REST + 2 * P] = same & (i[:, None] < i[None, :])
    c[:64, C_IND] = 1
    c[64:, C_IND + 1] = 1
    c[0, C_SEL:C_SEL + P] = 1
    c[1, C_SEL + P:C_SEL + 2 * P] = 1
    c[:, C_ONE:C_ONE + 2] = 1
    c[:, C_START:C_START + TOPK] = np.cumsum([0] + [w for _, n, w in PAIRS for _ in range(n)])[:TOPK]
    inv = np.float32(10000.0) ** (-np.arange(16, dtype=np.float32) / np.float32(16))
    pos = np.arange(512)
    ar = (pos // GRID_W).astype(np.float32)[:, None] * inv
    ac = (pos % GRID_W).astype(np.float32)[:, None] * inv
    ang = np.concatenate([ar, ar, ac, ac], -1).astype(np.float32)
    sign = np.tile(np.repeat(np.array([-1.0, 1.0], np.float32), 16), 2)
    table = np.stack([np.cos(ang), np.sin(ang) * sign], 1).reshape(4, P, 2, 64).transpose(1, 0, 2, 3)
    c[:, C_ROPE:C_ROPE + 512] = table.reshape(P, 512)
    c[:, C_MASK:C_MASK + P] = np.where(i[None, :] >= i[:, None], 0.0, -1e30)
    c[:, C_MASK + 2 * P:C_MASK + 3 * P] = np.where(i[None, :] <= i[:, None], 0.0, -1e30)
    return c


def pool_bands():
    def full(n, w):
        t = np.arange(n)
        lo, hi = np.clip(t - w // 2, 0, n), np.clip(t - w // 2 + w, 0, n)
        m = (t[:, None] >= lo[None, :]) & (t[:, None] < hi[None, :])
        return m / (hi - lo)[None, :].astype(np.float32) - np.eye(n)
    out = np.zeros((P, 4, 6, P), np.float32)
    for g, w in enumerate(WINDOWS):
        out[:, g, 0] = full(P, w)
        m = full(4 * P, w)
        out[:, g, 1] = m[0:P, 0:P]
        out[:, g, 2] = m[P:2 * P, P:2 * P]
        out[:, g, 3] = m[3 * P:, 3 * P:]
        out[:, g, 4] = m[0:P, P:2 * P]
        out[:, g, 5] = m[2 * P:3 * P, P:2 * P]
    return out.reshape(P, 4 * 6 * P)


def slabs(w):
    k, n = w.shape
    return w.reshape(k // P, P, n).transpose(1, 0, 2).reshape(P, -1)


def kernel(**inputs):
    import concourse.bacc as bacc
    from concourse.bass_utils import run_bass_kernel_spmd

    v = {k: np.asarray(x) for k, x in inputs.items()}
    cat, rows = np.concatenate, lambda g: np.broadcast_to(g[None, :], (P, g.shape[0]))
    w_even = v["w_in_even"][0]
    order = [w_even[:, 0:1536], w_even[:, 1568:2080], w_even[:, 1536:1568], w_even[:, 2080:2144]]
    w_even = cat(order, 1)
    w_gu = np.zeros((33, 512), np.float32)
    w_gu[0:16, 0:256] = v["w_gate_up"][0, 0]
    w_gu[16:32, 256:512] = v["w_gate_up"][0, 1]
    w_gu[32] = v["b_gate_up"][0].reshape(-1)
    cond = np.stack([v["c_ctx"], v["c"][0]], 1).reshape(KD, P, 2).transpose(1, 0, 2).reshape(P, 16)
    vecs = cat([
        cond, v["g_norm"].reshape(LAYERS * 2 * KD, P).T, rows(v["g_mla_ckv"][0]), rows(v["g_mla_cq"][0]),
        rows(v["g_mla_qn"][0]), rows(v["g_mla_kn"][0]), v["g_gla_out"][0][:, None], rows(v["g_win_qn"][0]),
        rows(v["g_win_kn"][0]), rows(v["win_sink"][0]), v["pool_scale"][0].reshape(4, P).T], 1)
    assert vecs.shape[1] == S_N
    ins = {
        "const": constants(),
        "vecs": vecs,
        "x": cat([v["x_prompt"][0], v["x_sample"][0]], 0),
        "w_gu": w_gu,
        "state_in": v["state_gla"][0, 0].reshape(2, 2, 2, 64, P).transpose(3, 0, 2, 1, 4),
        "ctx_ckv": v["cache_mla_ckv"][0, 0],
        "ctx_kr": v["cache_mla_krope"][0, 0],
        "k_ctx": v["cache_win_kv"][0, 0, 0].reshape(P, P),
        "v_ctx": v["cache_win_kv"][0, 0, 1].reshape(P, P),
        "w_ada": v["w_ada"].reshape(LAYERS, KD, P, 12, 512).transpose(0, 3, 2, 1, 4).reshape(LAYERS, 12, P, 4096),
        "b_ada": v["b_ada"].reshape(LAYERS, 12, 1, 512),
        "w_mla": cat([slabs(v["w_mla_uq"][0]), slabs(v["w_mla_uk"][0]), slabs(v["w_mla_uv"][0])], 1),
        "w_band": cat([pool_bands(), v["w_pool"][0].transpose(1, 0, 2).reshape(P, 512)], 1),
        "w_out0": np.stack([slabs(v["w_out_even"][0][:, 512 * n:512 * n + 512]) for n in range(2)]),
        "w_out1": np.stack([slabs(v["w_out_odd"][0][:, 512 * n:512 * n + 512]) for n in range(2)]),
        "peer_wq": v["peer_wq"].reshape(LAYERS, KD, P, 4, 512).transpose(0, 3, 2, 1, 4).reshape(LAYERS, 4, P, 4096),
        "subkeys": v["peer_subkeys"].reshape(LAYERS, 16, NEXP, P).transpose(0, 3, 1, 2).reshape(LAYERS, P, 2048),
        "peer_u": v["peer_u"].reshape(LAYERS, NEXP, NG, GROUP, KD, P).transpose(0, 2, 5, 3, 4, 1)
                             .reshape(LAYERS, NG, P, GROUP * D),
        "peer_v": v["peer_v"].reshape(LAYERS, NEXP, NG, GROUP * D).transpose(0, 2, 1, 3),
    }
    for n, (at, w) in enumerate(EVEN_CHUNKS):
        ins[f"w_in0_{n}"] = slabs(w_even[:, at:at + w])
    for n, (at, w) in enumerate(ODD_CHUNKS):
        ins[f"w_in1_{n}"] = slabs(v["w_in_odd"][0][:, at:at + w])
    ins = {k: np.ascontiguousarray(x) for k, x in ins.items()}
    outs = {"y_prompt": (P, D), "y_sample": (512, D), "state": (2, 4, 64, P), "ckv": (P, 256), "kr": (P, 64),
            "win": (2, P, P)}
    nc = bacc.Bacc("TRN2", target_bir_lowering=False, num_devices=1)
    aps = {k: nc.dram_tensor(f"in_{k}", x.shape, F32, kind="ExternalInput").ap() for k, x in ins.items()}
    aps |= {k: nc.dram_tensor(f"out_{k}", s, F32, kind="ExternalOutput").ap() for k, s in outs.items()}
    build_program(nc, aps)
    r = run_bass_kernel_spmd(nc, [{f"in_{k}": x for k, x in ins.items()}], core_ids=[0]).results[0]
    return (r["out_y_prompt"].reshape(1, P, D), r["out_y_sample"].reshape(1, 512, D),
            r["out_state"].reshape(1, 1, 2, 4, 64, P), r["out_ckv"].reshape(1, 1, P, 256),
            r["out_kr"].reshape(1, 1, P, 64), r["out_win"].reshape(1, 1, 2, P, 2, 64))
```
